# Optimizing a Trainium2 kernel written in Bass

```python
import jax, jax.numpy as jnp
from jax import lax
import numpy as np

D_MODEL = 1024
BATCH = 1
SEQ = 256
DEPTH = 2

HEAD_DIM = 64
MIX_WIDTH = D_MODEL
MOBA_HEADS = 6
MLSTM_HEADS = 4
SWA_Q_HEADS = 6
SWA_KV_HEADS = 2
MOBA_WIDTH = MOBA_HEADS * HEAD_DIM
MLSTM_WIDTH = MLSTM_HEADS * HEAD_DIM
SWA_Q_WIDTH = SWA_Q_HEADS * HEAD_DIM
SWA_KV_WIDTH = SWA_KV_HEADS * HEAD_DIM
MOBA_BLOCK = 256
MOBA_TOPK = 3
MOBA_Q_CHUNK = 64
MLSTM_CHUNK = 64
CONV_WIDTH = 4
SWA_WINDOW = 128
ROPE_THETA = 10000.0
D_FF = 4 * D_MODEL
NORM_EPS = 1e-6
IN_SPLITS = (MOBA_WIDTH, MOBA_WIDTH, MOBA_WIDTH, SWA_Q_WIDTH, SWA_KV_WIDTH, SWA_KV_WIDTH, 2 * MLSTM_WIDTH, MLSTM_WIDTH, MLSTM_WIDTH, MLSTM_HEADS, MLSTM_HEADS)
IN_WIDTH = sum(IN_SPLITS)


def rms_norm(x, g):
    xf = x.astype(jnp.float32)
    y = xf * lax.rsqrt(jnp.mean(xf * xf, axis=-1, keepdims=True) + NORM_EPS)
    return (y * g.astype(jnp.float32)).astype(x.dtype)

def rope_tables(seq):
    inv = ROPE_THETA ** (-jnp.arange(0, HEAD_DIM, 2, dtype=jnp.float32) / HEAD_DIM)
    ang = jnp.arange(seq, dtype=jnp.float32)[:, None] * inv[None, :]
    return jnp.cos(ang), jnp.sin(ang)

def apply_rope(x, cos, sin):
    c = cos[:, None, :].astype(x.dtype)
    s = sin[:, None, :].astype(x.dtype)
    x1, x2 = jnp.split(x, 2, axis=-1)
    return jnp.concatenate([x1 * c - x2 * s, x2 * c + x1 * s], axis=-1)

def causal_depthwise_conv(x, w, b):
    C = x.shape[-1]
    y = lax.conv_general_dilated(x, w[:, None, :].astype(x.dtype), (1,), [(w.shape[0] - 1, 0)],
                                 dimension_numbers=('NWC', 'WIO', 'NWC'), feature_group_count=C)
    return y + b.astype(x.dtype)

def moba_attention(q, k, v):
    B, H, S, D = q.shape
    L = MOBA_BLOCK
    n_blocks = -(-S // L)
    s_pad = n_blocks * L
    if s_pad != S:
        padw = ((0, 0), (0, 0), (0, s_pad - S), (0, 0))
        q, k, v = jnp.pad(q, padw), jnp.pad(k, padw), jnp.pad(v, padw)
    k_blk = k.reshape(B, H, n_blocks, L, D)
    v_blk = v.reshape(B, H, n_blocks, L, D)
    k_mean = jnp.mean(k_blk.astype(jnp.float32), axis=3)
    top = min(MOBA_TOPK, n_blocks)
    scale = D ** -0.5
    Qc = MOBA_Q_CHUNK
    b_idx = jnp.arange(B)[:, None, None, None]
    h_idx = jnp.arange(H)[None, :, None, None]

    def one_chunk(c):
        start = c * Qc
        blk = start // L
        qc = lax.dynamic_slice_in_dim(q, start, Qc, axis=2)
        gate = jnp.einsum('bhqd,bhnd->bhqn', qc.astype(jnp.float32), k_mean)
        gate = jnp.where(jnp.arange(n_blocks) < blk, gate, -jnp.inf)
        _, sel = lax.top_k(gate, top)
        sel_ok = jnp.arange(top) < blk
        k_sel = k_blk[b_idx, h_idx, sel]
        v_sel = v_blk[b_idx, h_idx, sel]
        s_sel = jnp.einsum('bhqd,bhqrld->bhqrl', qc, k_sel).astype(jnp.float32) * scale
        s_sel = jnp.where(sel_ok[:, None], s_sel, -jnp.inf).reshape(B, H, Qc, top * L)
        k_own = lax.dynamic_slice_in_dim(k, blk * L, L, axis=2)
        v_own = lax.dynamic_slice_in_dim(v, blk * L, L, axis=2)
        s_own = jnp.einsum('bhqd,bhld->bhql', qc, k_own).astype(jnp.float32) * scale
        q_pos = start + jnp.arange(Qc)
        k_pos = blk * L + jnp.arange(L)
        s_own = jnp.where(k_pos[None, :] <= q_pos[:, None], s_own, -jnp.inf)
        p = jax.nn.softmax(jnp.concatenate([s_sel, s_own], axis=-1), axis=-1).astype(v.dtype)
        p_sel = p[..., :top * L].reshape(B, H, Qc, top, L)
        p_own = p[..., top * L:]
        return (jnp.einsum('bhqrl,bhqrld->bhqd', p_sel, v_sel)
                + jnp.einsum('bhql,bhld->bhqd', p_own, v_own))

    outs = lax.map(one_chunk, jnp.arange(s_pad // Qc))
    out = jnp.moveaxis(outs, 0, 2).reshape(B, H, s_pad, D)
    return out[:, :, :S]

def mlstm_chunkwise(q, k, v, i_pre, f_pre):
    B, H, S, D = q.shape
    L = MLSTM_CHUNK
    nc = S // L
    k = k * (D ** -0.5)
    log_f = jax.nn.log_sigmoid(f_pre)

    def chunks(a):
        return jnp.moveaxis(a.reshape(B, H, nc, L, *a.shape[3:]), 2, 0)

    causal = jnp.tril(jnp.ones((L, L), dtype=bool))

    def step(carry, inp):
        C, n, m = carry
        qc, kc, vc, ic, lfc = inp
        b = jnp.cumsum(lfc, axis=-1)
        a = b[..., -1]
        d = b[..., :, None] - b[..., None, :] + ic[..., None, :]
        d = jnp.where(causal, d, -jnp.inf)
        inter = b + m[..., None]
        m_t = jnp.maximum(inter, jnp.max(d, axis=-1))
        w_intra = jnp.exp(d - m_t[..., None])
        w_inter = jnp.exp(inter - m_t)
        qk = jnp.einsum('bhtd,bhsd->bhts', qc, kc) * w_intra
        num = (w_inter[..., None] * jnp.einsum('bhtd,bhde->bhte', qc, C)
               + jnp.einsum('bhts,bhse->bhte', qk, vc))
        den = w_inter * jnp.einsum('bhtd,bhd->bht', qc, n) + jnp.sum(qk, axis=-1)
        h = num / jnp.maximum(jnp.abs(den), jnp.exp(-m_t))[..., None]
        g = a[..., None] - b + ic
        m_new = jnp.maximum(a + m, jnp.max(g, axis=-1))
        w_s = jnp.exp(g - m_new[..., None])
        decay = jnp.exp(a + m - m_new)
        C_new = decay[..., None, None] * C + jnp.einsum('bhsd,bhse->bhde', kc * w_s[..., None], vc)
        n_new = decay[..., None] * n + jnp.einsum('bhs,bhsd->bhd', w_s, kc)
        return (C_new, n_new, m_new), h

    init = (jnp.zeros((B, H, D, D), jnp.float32), jnp.zeros((B, H, D), jnp.float32),
            jnp.zeros((B, H), jnp.float32))
    _, h = lax.scan(step, init, (chunks(q), chunks(k), chunks(v), chunks(i_pre), chunks(log_f)))
    return jnp.moveaxis(h, 0, 2).reshape(B, H, S, D)

def swa_attention(q, k, v, sinks):
    B, S, Hq, D = q.shape
    Hkv = k.shape[2]
    G = Hq // Hkv
    W = SWA_WINDOW
    nb = S // W
    qb = q.reshape(B, nb, W, Hkv, G, D)

    def band(a):
        ab = a.reshape(B, nb, W, Hkv, D)
        prev = jnp.pad(ab, ((0, 0), (1, 0), (0, 0), (0, 0), (0, 0)))[:, :-1]
        return jnp.concatenate([prev, ab], axis=2)

    kb, vb = band(k), band(v)
    s = jnp.einsum('bnqkgd,bnjkd->bnkgqj', qb, kb).astype(jnp.float32) * (D ** -0.5)
    qi = jnp.arange(W)[:, None] + W
    kj = jnp.arange(2 * W)[None, :]
    in_window = (qi - kj >= 0) & (qi - kj < W)
    exists = (jnp.arange(nb)[:, None, None] > 0) | (kj[None] >= W)
    mask = in_window[None] & exists
    s = jnp.where(mask[None, :, None, None], s, -jnp.inf)
    sink = jnp.broadcast_to(sinks.astype(jnp.float32).reshape(1, 1, Hkv, G, 1, 1), s.shape[:-1] + (1,))
    p = jax.nn.softmax(jnp.concatenate([s, sink], axis=-1), axis=-1)[..., :-1].astype(v.dtype)
    o = jnp.einsum('bnkgqj,bnjkd->bnqkgd', p, vb)
    return o.reshape(B, S, Hq, D)

def hybrid_layer(x, cos, sin, ln1, w_in, conv_w, conv_b, igate_b, fgate_b, mlstm_norm,
                 moba_q_norm, moba_k_norm, swa_q_norm, swa_k_norm, swa_sinks, w_out,
                 ln2, w_up, w_down):
    B, S, _ = x.shape
    hn = rms_norm(x, ln1)
    proj = hn @ w_in
    idx = np.cumsum(IN_SPLITS)[:-1].tolist()
    mq, mk, mv, sq, sk, sv, xqk, xv, xo, xi, xf = jnp.split(proj, idx, axis=-1)

    def heads(a):
        return a.reshape(B, S, -1, HEAD_DIM)

    def bhsd(a):
        return a.transpose(0, 2, 1, 3)

    mq = apply_rope(rms_norm(heads(mq), moba_q_norm), cos, sin)
    mk = apply_rope(rms_norm(heads(mk), moba_k_norm), cos, sin)
    y_moba = bhsd(moba_attention(bhsd(mq), bhsd(mk), bhsd(heads(mv)))).reshape(B, S, MOBA_WIDTH)

    qk = jax.nn.silu(causal_depthwise_conv(xqk, conv_w, conv_b))
    lq, lk = jnp.split(qk, 2, axis=-1)
    i_pre = (xi + igate_b).astype(jnp.float32).transpose(0, 2, 1)
    f_pre = (xf + fgate_b).astype(jnp.float32).transpose(0, 2, 1)
    h = mlstm_chunkwise(bhsd(heads(lq)).astype(jnp.float32), bhsd(heads(lk)).astype(jnp.float32),
                        bhsd(heads(xv)).astype(jnp.float32), i_pre, f_pre)
    h = bhsd(h).astype(x.dtype) * heads(jax.nn.sigmoid(xo))
    y_mlstm = rms_norm(h, mlstm_norm).reshape(B, S, MLSTM_WIDTH)

    sq = apply_rope(rms_norm(heads(sq), swa_q_norm), cos, sin)
    sk = apply_rope(rms_norm(heads(sk), swa_k_norm), cos, sin)
    y_swa = swa_attention(sq, sk, heads(sv), swa_sinks).reshape(B, S, SWA_Q_WIDTH)

    x = x + jnp.concatenate([y_moba, y_mlstm, y_swa], axis=-1) @ w_out
    u = rms_norm(x, ln2) @ w_up
    return x + jnp.square(jax.nn.relu(u)) @ w_down

def first_inputs(seed: int = 0) -> dict:
    key = jax.random.key(seed)
    ks = jax.random.split(key, 17)
    f32 = jnp.float32

    def nrm(k, shape, scale):
        return jax.random.normal(k, shape, f32) * scale

    return {
        'x': nrm(ks[0], (BATCH, SEQ, D_MODEL), 1.0),
        'ln1': 1.0 + nrm(ks[1], (DEPTH, D_MODEL), 0.02),
        'w_in': nrm(ks[2], (DEPTH, D_MODEL, IN_WIDTH), D_MODEL ** -0.5),
        'conv_w': nrm(ks[3], (DEPTH, CONV_WIDTH, 2 * MLSTM_WIDTH), CONV_WIDTH ** -0.5),
        'conv_b': nrm(ks[4], (DEPTH, 2 * MLSTM_WIDTH), 0.02),
        'igate_b': nrm(ks[5], (DEPTH, MLSTM_HEADS), 0.1),
        'fgate_b': jnp.linspace(3.0, 6.0, MLSTM_HEADS, dtype=f32)[None] + nrm(ks[6], (DEPTH, MLSTM_HEADS), 0.1),
        'mlstm_norm': 1.0 + nrm(ks[7], (DEPTH, MLSTM_HEADS, HEAD_DIM), 0.02),
        'moba_q_norm': 1.0 + nrm(ks[8], (DEPTH, HEAD_DIM), 0.02),
        'moba_k_norm': 1.0 + nrm(ks[9], (DEPTH, HEAD_DIM), 0.02),
        'swa_q_norm': 1.0 + nrm(ks[10], (DEPTH, HEAD_DIM), 0.02),
        'swa_k_norm': 1.0 + nrm(ks[11], (DEPTH, HEAD_DIM), 0.02),
        'swa_sinks': nrm(ks[12], (DEPTH, SWA_Q_HEADS), 1.0),
        'w_out': nrm(ks[13], (DEPTH, MIX_WIDTH, D_MODEL), MIX_WIDTH ** -0.5),
        'ln2': 1.0 + nrm(ks[14], (DEPTH, D_MODEL), 0.02),
        'w_up': nrm(ks[15], (DEPTH, D_MODEL, D_FF), D_MODEL ** -0.5),
        'w_down': nrm(ks[16], (DEPTH, D_FF, D_MODEL), D_FF ** -0.5),
    }

def first_block(x, ln1, w_in, conv_w, conv_b, igate_b, fgate_b, mlstm_norm, moba_q_norm,
              moba_k_norm, swa_q_norm, swa_k_norm, swa_sinks, w_out, ln2, w_up, w_down):
    cos, sin = rope_tables(x.shape[1])
    for l in range(DEPTH):
        x = hybrid_layer(x, cos, sin, ln1[l], w_in[l], conv_w[l], conv_b[l], igate_b[l], fgate_b[l],
                         mlstm_norm[l], moba_q_norm[l], moba_k_norm[l], swa_q_norm[l], swa_k_norm[l],
                         swa_sinks[l], w_out[l], ln2[l], w_up[l], w_down[l])
    return x


GRID_W = 64
CTX_LEN = 256
N_Q_HEADS = 8
N_KV_HEADS = 2
GQA_GROUP = N_Q_HEADS // N_KV_HEADS
ATTN_WIDTH = N_Q_HEADS * HEAD_DIM
KV_WIDTH = N_KV_HEADS * HEAD_DIM
CONV_GROUPS = 4
CONV_WIDTH_2 = CONV_GROUPS * 64
CONV_K = 3
FOURIER_GROUPS = 4
FOURIER_GROUP_DIM = 64
FOURIER_WIDTH = FOURIER_GROUPS * FOURIER_GROUP_DIM
N_BRANCHES = 3
D_FF_2 = 4 * D_MODEL
Q_BLOCK = 128
ROPE_HALF = HEAD_DIM // 2
EPS = 1e-6
N_MOD = 6

OFF_B = 0
OFF_C = OFF_B + CONV_WIDTH_2
OFF_X = OFF_C + CONV_WIDTH_2
OFF_F = OFF_X + CONV_WIDTH_2
OFF_Q = OFF_F + FOURIER_WIDTH
OFF_K = OFF_Q + ATTN_WIDTH
OFF_V = OFF_K + KV_WIDTH
OFF_G = OFF_V + KV_WIDTH
IN_WIDTH_2 = OFF_G + N_BRANCHES * D_MODEL


def rms_norm_2(x, g):
    xf = x.astype(jnp.float32)
    y = xf * lax.rsqrt(jnp.mean(xf * xf, axis=-1, keepdims=True) + EPS)
    return (y * g.astype(jnp.float32)).astype(x.dtype)

def modulate(x, g, shift, scale):
    return rms_norm_2(x, g) * (1 + scale) + shift

def axial_rope_tables(rows):
    n_freq = ROPE_HALF // 2
    inv = ROPE_THETA ** (-jnp.arange(n_freq, dtype=jnp.float32) / n_freq)
    row_ang = jnp.repeat(jnp.arange(rows, dtype=jnp.float32)[:, None] * inv, GRID_W, axis=0)
    col_ang = jnp.tile(jnp.arange(GRID_W, dtype=jnp.float32)[:, None] * inv, (rows, 1))
    ang = jnp.concatenate([row_ang, col_ang], axis=-1)
    return jnp.cos(ang), jnp.sin(ang)

def apply_rope_2(x, cos, sin):
    xf = x.astype(jnp.float32)
    x1, x2 = xf[..., :ROPE_HALF], xf[..., ROPE_HALF:]
    c = cos[None, :, None, :]
    s = sin[None, :, None, :]
    return jnp.concatenate([x1 * c - x2 * s, x1 * s + x2 * c], axis=-1).astype(x.dtype)

def short_conv(u, w):
    L = u.shape[1]
    pad = CONV_K // 2
    up = jnp.pad(u, ((0, 0), (pad, pad), (0, 0)))
    return sum(up[:, j:j + L] * w[j] for j in range(CONV_K))

def fourier_mix(u):
    b, L, _ = u.shape
    ug = u.astype(jnp.float32).reshape(b, L, FOURIER_GROUPS, FOURIER_GROUP_DIM)
    y = jnp.fft.fft2(ug, axes=(1, 3), norm="ortho").real
    return y.reshape(b, L, FOURIER_WIDTH).astype(u.dtype)

def local_branches(z, w_conv):
    y_conv = z[..., OFF_B:OFF_C] * short_conv(z[..., OFF_C:OFF_X] * z[..., OFF_X:OFF_F], w_conv)
    y_four = fourier_mix(z[..., OFF_F:OFF_Q])
    return y_conv, y_four

def qkv_heads(z, g_q, g_k):
    b, L, _ = z.shape
    q = rms_norm_2(z[..., OFF_Q:OFF_K].reshape(b, L, N_Q_HEADS, HEAD_DIM), g_q)
    k = rms_norm_2(z[..., OFF_K:OFF_V].reshape(b, L, N_KV_HEADS, HEAD_DIM), g_k)
    v = z[..., OFF_V:OFF_G].reshape(b, L, N_KV_HEADS, HEAD_DIM)
    return q, k, v

def gqa(q, k, v):
    b, lq = q.shape[:2]
    qg = q.reshape(b, lq, N_KV_HEADS, GQA_GROUP, HEAD_DIM)
    s = jnp.einsum('bqgrd,bkgd->bgrqk', qg, k).astype(jnp.float32) * (HEAD_DIM ** -0.5)
    p = jax.nn.softmax(s, axis=-1).astype(v.dtype)
    o = jnp.einsum('bgrqk,bkgd->bqgrd', p, v)
    return o.reshape(b, lq, ATTN_WIDTH)

def blocked_gqa(q, k, v):
    b, lq = q.shape[:2]
    nb = lq // Q_BLOCK
    qb = q.reshape(b, nb, Q_BLOCK, N_Q_HEADS, HEAD_DIM).transpose(1, 0, 2, 3, 4)
    ob = lax.map(lambda qi: gqa(qi, k, v), qb)
    return ob.transpose(1, 0, 2, 3).reshape(b, lq, ATTN_WIDTH)

def merge_branches(z, y_conv, y_four, y_attn, w_conv_out, w_four_out, w_attn_out, w_o):
    gates = jax.nn.sigmoid(z[..., OFF_G:].astype(jnp.float32)).astype(z.dtype)
    g_conv, g_four, g_attn = jnp.split(gates, N_BRANCHES, axis=-1)
    m = g_conv * (y_conv @ w_conv_out) + g_four * (y_four @ w_four_out) + g_attn * (y_attn @ w_attn_out)
    return m @ w_o

def sq_relu_mlp(h, w1, w2):
    return jnp.square(jax.nn.relu(h @ w1)) @ w2

def second_inputs(seed: int = 0) -> dict:
    key = jax.random.key(seed)
    ks = jax.random.split(key, 20)
    f32 = jnp.float32
    nrm = lambda k, shape, s: jax.random.normal(k, shape, f32) * s
    return {
        "x": nrm(ks[0], (BATCH, SEQ, D_MODEL), 1.0),
        "c": nrm(ks[1], (BATCH, D_MODEL), 1.0),
        "ctx": nrm(ks[2], (BATCH, CTX_LEN, D_MODEL), 1.0),
        "c_ctx": nrm(ks[3], (D_MODEL,), 1.0),
        "w_mod": nrm(ks[4], (DEPTH, D_MODEL, N_MOD * D_MODEL), 0.5 * D_MODEL ** -0.5),
        "b_mod": nrm(ks[5], (DEPTH, N_MOD * D_MODEL), 0.01),
        "g_norm1": 1.0 + nrm(ks[6], (DEPTH, D_MODEL), 0.05),
        "g_norm2": 1.0 + nrm(ks[7], (DEPTH, D_MODEL), 0.05),
        "w_in": nrm(ks[8], (DEPTH, D_MODEL, IN_WIDTH_2), D_MODEL ** -0.5),
        "w_conv": nrm(ks[9], (DEPTH, CONV_K, CONV_WIDTH_2), CONV_K ** -0.5),
        "g_q": 1.0 + nrm(ks[10], (DEPTH, HEAD_DIM), 0.05),
        "g_k": 1.0 + nrm(ks[11], (DEPTH, HEAD_DIM), 0.05),
        "w_conv_out": nrm(ks[12], (DEPTH, CONV_WIDTH_2, D_MODEL), CONV_WIDTH_2 ** -0.5),
        "w_four_out": nrm(ks[13], (DEPTH, FOURIER_WIDTH, D_MODEL), FOURIER_WIDTH ** -0.5),
        "w_attn_out": nrm(ks[14], (DEPTH, ATTN_WIDTH, D_MODEL), ATTN_WIDTH ** -0.5),
        "w_o": nrm(ks[15], (DEPTH, D_MODEL, D_MODEL), D_MODEL ** -0.5),
        "w_ff1": nrm(ks[16], (DEPTH, D_MODEL, D_FF_2), D_MODEL ** -0.5),
        "w_ff2": nrm(ks[17], (DEPTH, D_FF_2, D_MODEL), D_FF_2 ** -0.5),
    }

def second_block(x, c, ctx, c_ctx, w_mod, b_mod, g_norm1, g_norm2, w_in, w_conv, g_q, g_k,
              w_conv_out, w_four_out, w_attn_out, w_o, w_ff1, w_ff2):
    S = x.shape[1]
    ROWS = S // GRID_W
    cos, sin = axial_rope_tables(ROWS)
    ctx_s = ctx
    for l in range(DEPTH):
        mod = (jax.nn.silu(c) @ w_mod[l] + b_mod[l])[:, None, :]
        mod_c = (jax.nn.silu(c_ctx)[None] @ w_mod[l] + b_mod[l])[:, None, :]
        sh1, sc1, gt1, sh2, sc2, gt2 = jnp.split(mod, N_MOD, axis=-1)
        csh1, csc1, cgt1, csh2, csc2, cgt2 = jnp.split(mod_c, N_MOD, axis=-1)

        hc = modulate(ctx_s, g_norm1[l], csh1, csc1)
        zc = hc @ w_in[l]
        qc, kc, vc = qkv_heads(zc, g_q[l], g_k[l])

        h = modulate(x, g_norm1[l], sh1, sc1)
        z = h @ w_in[l]
        q, k, v = qkv_heads(z, g_q[l], g_k[l])
        q = apply_rope_2(q, cos, sin)
        k = apply_rope_2(k, cos, sin)
        k_all = jnp.concatenate([k, kc], axis=1)
        v_all = jnp.concatenate([v, vc], axis=1)
        y_attn = blocked_gqa(q, k_all, v_all)
        y_conv, y_four = local_branches(z, w_conv[l])
        x = x + gt1 * merge_branches(z, y_conv, y_four, y_attn,
                                     w_conv_out[l], w_four_out[l], w_attn_out[l], w_o[l])
        x = x + gt2 * sq_relu_mlp(modulate(x, g_norm2[l], sh2, sc2), w_ff1[l], w_ff2[l])

        if l < DEPTH - 1:
            yc_attn = gqa(qc, kc, vc)
            yc_conv, yc_four = local_branches(zc, w_conv[l])
            ctx_s = ctx_s + cgt1 * merge_branches(zc, yc_conv, yc_four, yc_attn,
                                                  w_conv_out[l], w_four_out[l], w_attn_out[l], w_o[l])
            ctx_s = ctx_s + cgt2 * sq_relu_mlp(modulate(ctx_s, g_norm2[l], csh2, csc2),
                                               w_ff1[l], w_ff2[l])
    return x


def setup_inputs(seed=0):
    out = dict(first_inputs(seed))
    for name, value in second_inputs(seed + 1).items():
        if name != "x":
            out[name + "_2"] = value
    return out


def reference(
    x, ln1, w_in, conv_w, conv_b, igate_b, fgate_b, mlstm_norm, moba_q_norm, moba_k_norm,
    swa_q_norm, swa_k_norm, swa_sinks, w_out, ln2, w_up, w_down, c_2, ctx_2, c_ctx_2, w_mod_2,
    b_mod_2, g_norm1_2, g_norm2_2, w_in_2, w_conv_2, g_q_2, g_k_2, w_conv_out_2, w_four_out_2,
    w_attn_out_2, w_o_2, w_ff1_2, w_ff2_2,
):
    x = first_block(
        x, ln1, w_in, conv_w, conv_b, igate_b, fgate_b, mlstm_norm, moba_q_norm, moba_k_norm,
        swa_q_norm, swa_k_norm, swa_sinks, w_out, ln2, w_up, w_down,
    )
    return second_block(
        x, c_2, ctx_2, c_ctx_2, w_mod_2, b_mod_2, g_norm1_2, g_norm2_2, w_in_2, w_conv_2, g_q_2,
        g_k_2, w_conv_out_2, w_four_out_2, w_attn_out_2, w_o_2, w_ff1_2, w_ff2_2,
    )


_drawn_inputs = setup_inputs


def setup_inputs(seed=0):
    import zlib

    import numpy as np

    out = dict(_drawn_inputs(seed))
    spreads = {}
    factors = {'conv_b': 4.109,
     'igate_b': 41.654,
     'mlstm_norm': 4.577,
     'moba_q_norm': 8.0,
     'moba_k_norm': 8.0,
     'swa_q_norm': 8.0,
     'swa_k_norm': 8.0,
     'swa_sinks': 3.645,
     'ctx_2': 8.0,
     'c_ctx_2': 3.045,
     'b_mod_2': 4.688,
     'g_norm1_2': 4.441,
     'g_norm2_2': 3.526,
     'g_q_2': 8.0,
     'g_k_2': 8.0}
    for name, (base, spread) in spreads.items():
        noise = np.random.default_rng([zlib.crc32(name.encode()), seed]).standard_normal(out[name].shape)
        drawn = base * np.exp(spread * noise) if base else spread * noise
        out[name] = __import__('jax').numpy.asarray(drawn.astype(out[name].dtype))
    for name, factor in factors.items():
        out[name] = (out[name] * factor).astype(out[name].dtype)
    return out
```

```python
from contextlib import ExitStack

import numpy as np

import concourse.bass as bass
from concourse import mybir

F32 = mybir.dt.float32
F32R = mybir.dt.float32r
ALU = mybir.AluOpType
ACT = mybir.ActivationFunctionType
AX_X = mybir.AxisListType.X

P = 128
D = 1024
KT = D // P
S = 256
NT = S // P
DEPTH = 2
DH = 64
FF = 4 * D
EPS = 1e-6
ISC = DH ** -0.5

MOBA_H, ML_H, SWA_H, SWA_KV = 6, 4, 6, 2
C_MQ, C_MV, C_SQ, C_SV = 0, 2 * MOBA_H * DH, 3 * MOBA_H * DH, 3 * MOBA_H * DH + (SWA_H + SWA_KV) * DH
C_LQK = C_SV + SWA_KV * DH
C_LV = C_LQK + 2 * ML_H * DH
C_GATE = C_LV + 2 * ML_H * DH
N_IN1 = C_GATE + 2 * ML_H
Z_LV = C_LQK
Z_LO = Z_LV + ML_H * DH
Z_GATE = Z_LO + ML_H * DH
ZW = Z_GATE + 2 * ML_H
NQK = 2 * MOBA_H + SWA_H + SWA_KV
NSL = NQK + SWA_KV

B_X3, B_F, B_Q, B_K, B_G = 0, 768, 1024, 1536, 1792
N_IN2 = B_G + 3 * D
QH, KVH = 8, 2

RAW_N, HL_N = 2, 4
CW = 2048
SPLIT_LEAD = 3
MODC = 4
CH1 = 60
GR1 = 10
UC1 = 18
LAST1 = MODC + 11
CH2 = 59
GR2 = 19
UC2 = 19

N_F, N_Q, N_K, N_V = 0, 256, 768, 896
M_SH, M_SC, M_GT = (0, 24), (8, 32), (16, 40)


class Pass:

    def __init__(self, p):
        self.p, self.layer, self.stream = p, (0, 0, 1)[p], (1, 0, 0)[p]
        mini = p == 2
        self.mini = mini
        self.c = CH1 * DEPTH + (CH2 + 3 * MODC) * p + mini
        self.mod = 0 if mini else MODC
        self.mg = 12 + 6 * p
        m = self.mod
        self.c_in, self.c_br, self.c_o, self.c_mlp = (self.c + m, self.c + m + 19, self.c + 2 * m + 23,
                                                      self.c + 3 * m + 27)
        self.g = GR1 * DEPTH + GR2 * p + mini
        self.u = UC1 * DEPTH + UC2 * p
        self.t = 12 * DEPTH + 14 * p + 4 * mini
        self.src = 3 * DEPTH + 4 * p + mini
        self.norm = 2 * DEPTH + 2 * p + mini
        self.pow = 4 * DEPTH + 3 * p + 2 * mini
        self.mlp = DEPTH + p
        self.qk = p + mini
        self.att = 16 * p


PASSES = [Pass(p) for p in range(3)]

K_ID, K_ONE, K_TRI = 0, 128, 256
K_M = 384
K_R1 = K_M + 512
K_R2 = K_R1 + 128
K_CL = K_R2 + 128
K_BD = K_CL + 4 * S
K_W = K_BD + 256


def shape_constants():
    t = np.zeros((P, K_W), np.float32)
    i = np.arange(P)
    t[:, K_ID:K_ID + P] = np.eye(P)
    t[:, K_ONE:K_ONE + P] = 1.0
    t[:, K_TRI:K_TRI + P] = i[:, None] <= i[None, :]
    low = np.float32(-1e30)
    causal = np.where(i[None, :] > i[:, None], low, 0)
    window = np.where(i[None, :] <= i[:, None], low, 0)
    t[:, K_M + 128:K_M + 256] = causal
    t[:, K_M + 256:K_M + 384] = window
    t[:, K_M + 384:K_M + 512] = causal
    inv = (np.float32(10000.0) ** (-np.arange(0, DH, 2, dtype=np.float32) / np.float32(DH))).astype(np.float32)
    ang = np.arange(S, dtype=np.float32)[:, None] * inv[None, :]
    inv2 = (np.float32(10000.0) ** (-np.arange(16, dtype=np.float32) / np.float32(16))).astype(np.float32)
    rows = np.repeat(np.arange(S // 64, dtype=np.float32)[:, None] * inv2, 64, axis=0)
    cols = np.tile(np.arange(64, dtype=np.float32)[:, None] * inv2, (S // 64, 1))
    ang2 = np.concatenate([rows, cols], axis=1)
    for at, a in ((K_R1, ang), (K_R2, ang2)):
        for f, fn in enumerate((np.cos, np.sin)):
            v = fn(a.astype(np.float32)).astype(np.float32).reshape(NT, P, 32)
            for n in range(NT):
                t[:, at + f * 64 + n * 32:at + f * 64 + n * 32 + 32] = v[n]
    k = np.arange(S)
    w = 2 * np.pi * ((k[:, None] * k[None, :]) % S) / S
    for f, fn in enumerate((np.cos, np.sin)):
        v = (fn(w) / 16.0).astype(np.float32).reshape(NT, P, S)
        for n in range(NT):
            t[:, K_CL + f * 2 * S + n * S:K_CL + f * 2 * S + (n + 1) * S] = v[n]
    k = np.arange(64)
    w = 2 * np.pi * ((k[:, None] * k[None, :]) % 64) / 64
    for f, v in enumerate((np.cos(w) / 8.0, -np.sin(w) / 8.0)):
        for b in range(2):
            t[b * 64:b * 64 + 64, K_BD + f * 128 + b * 64:K_BD + f * 128 + b * 64 + 64] = v
    return t


def build(nc, a, out):
    with ExitStack() as ctx:
        at = [16512]

        def sb(name, shape, dt=F32, where=None):
            size = 4 * int(np.prod(shape[1:]))
            offset = at[0] if where is None else where
            if where is None:
                at[0] += (size + 31) // 32 * 32
            return nc.alloc_sbuf_tensor_at(name, shape, dt, offset=offset)

        def sem(name):
            return ctx.enter_context(nc.semaphore(name))

        RAW = sb("RAW", [P, RAW_N, CW])
        HI = sb("HI", [P, HL_N, CW], F32R)
        LO = sb("LO", [P, HL_N, CW], F32R)
        X = sb("X", [P, NT, D])
        AH = sb("AH", [P, KT, S], F32R)
        AL = sb("AL", [P, KT, S], F32R)
        at_yn = at[0]
        YN = sb("YN", [P, NT, D])
        at_z = at[0]
        Z = sb("Z", [P, NT, ZW])
        QKT = sb("QKT", [P, NSL // 2, S])
        at[0] = at_z + 32768
        at_pm = at[0]
        PM = sb("PM", [P, 2, 512])
        at_pt = at[0]
        PTS = sb("PTS", [P, 2, 512])
        CT = sb("CT", [P, K_W])
        PAR = sb("PAR", [P, 256])
        MOD = sb("MOD", [P, DEPTH, 48, 2])
        GN = sb("GN", [P, DEPTH, 4, DH])
        MN = sb("MN", [P, DEPTH, ML_H * DH])
        IFB = sb("IFB", [P, DEPTH, 2 * ML_H])
        SK = sb("SK", [P, DEPTH, SWA_H])
        NSK = sb("NSK", [P, DEPTH, SWA_H])
        GQ2 = sb("GQ2", [P, DEPTH, 2, DH])
        CS = sb("CS", [P, 2, KT])
        C4 = sb("C4", [P, KT, 4], F32R)
        ROWS = sb("ROWS", [P, 512])
        SEL = sb("SEL", [4, 2])
        SGC = sb("SGC", [P, 16])
        SSQ = sb("SSQ", [P, 2])
        MS = sb("MS", [P, 64])
        RS = sb("RS", [P, 64])
        NHALF = sb("NHALF", [P, 64])
        MX = sb("MX", [P, 2, 2])
        NB = sb("NB", [P, MOBA_H + SWA_H, 2])
        SUM = sb("SUM", [P, MOBA_H + SWA_H, 2])
        SKE = sb("SKE", [P, SWA_H, 2])
        RIN = sb("RIN", [P, MOBA_H + SWA_H, 2])
        G8 = sb("G8", [P, NT, 8])
        GT1 = sb("GT1", [P, NT, 4])
        GT2 = sb("GT2", [P, NT, 4])
        ES = sb("ES", [P, NT, 4])
        BS = sb("BS", [P, NT, 4])
        RMX = sb("RMX", [P, 3, 4])
        RR = sb("RR", [P, NT, 4])
        DEN = sb("DEN", [P, NT, 4])
        SCL = sb("SCL", [P, DEPTH, 2, KT, 2])
        NM2 = sb("NM2", [P, QH, 2])
        SM2 = sb("SM2", [P, QH, 2])
        RN2 = sb("RN2", [P, QH, 2])
        at_scratch = at[0]
        QK = sb("QK", [P, NT, NSL, DH])
        XP = sb("XP", [P, 4, S + 3])
        CV = sb("CV", [P, 4, S])
        ME = sb("ME", [P, 3, ML_H, P])
        at_ptm = at[0]
        PTM = sb("PTM", [P, 3, ML_H, P])
        V65 = sb("V65", [P, NT, ML_H, DH + 1])
        HM = sb("HM", [P, NT, ML_H * DH])
        PR0 = sb("PR0", [P, P], F32, at_yn)
        PR1 = sb("PR1", [P, P], F32, at_yn + 512)
        TMP = sb("TMP", [P, 2, 512], F32, at_pm)
        U2 = sb("U2", [P, 2, 512], F32, at_pm)
        RL = sb("RL", [P, 2, 512], F32, at_pt)
        DG = sb("DG", [P, NT, ML_H, P], F32, at_ptm)
        SG = sb("SG", [P, 4, S], F32, at_ptm)
        SO = sb("SO", [P, NT, ML_H * DH], F32, at_ptm)
        HIDH = sb("HIDH", [P, 2, 4, S], F32R, at_z)
        HIDL = sb("HIDL", [P, 2, 4, S], F32R, at_z + 8192)
        GA = sb("GA", [P, NT, 3 * D], F32, at_z)
        ZN = sb("ZN", [P, NT, 1024], F32, at_z + 24576)
        M2 = sb("M2", [P, NT, D], F32, at_z + 24576)
        A12 = sb("A12", [P, 2, 2, S], F32, at_yn)
        YA = sb("YA", [P, NT, 512], F32, at_yn + 4096)
        UB = sb("UB", [P, 3, 2, S], F32, at_pm)
        TM = sb("TM", [P, 2, 512], F32, at_pt)
        DGB = sb("DGB", [P, 8, P], F32, at_pt)
        at_end = at[0]
        at[0] = at_scratch
        CTX = sb("CTX", [P, NT, D])
        QK2 = sb("QK2", [P, NT, 12, DH])
        QT2 = sb("QT2", [P, 4, S])
        KTB = sb("KTB", [P, 2, 2 * S])
        VB = sb("VB", [P, 2 * NT, P])
        GTB = sb("GTB", [P, D])
        CXP = sb("CXP", [P, 2, S + 2])
        YC = sb("YC", [P, 2, S])
        YF = sb("YF", [P, 2, S])
        at[0] = max(at_end, at[0])
        assert at[0] <= nc.sbuf_usable_end, at[0]
        IDM = CT[:, K_ID:K_ID + P]
        ONES = CT[:, K_ONE:K_ONE + P]
        TRI = CT[:, K_TRI:K_TRI + P]

        PS = ctx.enter_context(nc.psum_tensor("PS", [P, 8, 512], F32))

        s_cst = sem("constants_loaded")
        s_xin = sem("x_loaded")
        s_raw = [sem(f"raw_loaded_{i}") for i in range(RAW_N)]
        s_hi = sem("chunk_high_done")
        s_lo = sem("chunk_split_done")
        s_used = sem("chunk_used")
        s_gfree = sem("group_evacuated")
        s_ufree = sem("ubank_evacuated")
        s_mrow = sem("mod_rows_copied")
        s_mcol = sem("mod_columns")
        s_modc = sem("mod_copied")
        s_c4 = sem("silu_c_split")
        s_sel = sem("selector_loaded")
        s_init = sem("pool_constants")
        s_par = sem("params_transposed")
        s_parc = sem("params_copied")
        s_cs = sem("silu_c")
        s_av = sem("act_chain")
        s_dv = sem("dve_chain")
        s_ss = sem("sum_squares")
        s_ms = sem("mean_squares")
        s_rs = sem("rstd_done")
        s_src = sem("transpose_source")
        s_tp = sem("transposed")
        s_thi = sem("activation_high")
        s_tlo = sem("activation_low")
        s_sq = sem("qk_squares")
        s_qk = sem("qk_rotated")
        s_qsw = sem("qk_swapped_copied")
        s_qt = sem("qk_transposed")
        s_qtc = sem("qk_transposed_copied")
        s_s = sem("scores")
        s_sm = sem("scores_masked")
        s_nb = sem("row_max")
        s_e = sem("exp_done")
        s_pt = sem("probs_transposed")
        s_pe = sem("probs_copied")
        s_o = sem("head_output")
        s_oe = sem("head_output_copied")
        s_ske = sem("sink_in")
        s_sko = sem("sink_exp")
        s_cv = sem("conv_done")
        s_sg = sem("conv_sigmoid")
        s_lqk = sem("mlstm_qk")
        s_ga = sem("gate_abs")
        s_gl = sem("gate_log")
        s_lf = sem("log_forget")
        s_b = sem("cum_forget")
        s_dg = sem("diag_e")
        s_eb = sem("e_rows")
        s_me = sem("mlstm_exponent")
        s_mex = sem("mlstm_weights")
        s_mem = sem("mlstm_stabilizer")
        s_exm = sem("mlstm_floor")
        s_ms3 = sem("mlstm_scores")
        s_mp = sem("mlstm_probs")
        s_mt = sem("mlstm_transposed")
        s_mtc = sem("mlstm_transposed_copied")
        s_mo = sem("mlstm_output")
        s_h = sem("mlstm_h")
        s_hsq = sem("mlstm_h_squares")
        s_v65 = sem("mlstm_values")
        s_so = sem("output_gate")
        s_rl = sem("hidden_relu")
        s_u2 = sem("hidden_square")
        s_hh = sem("hidden_high")
        s_hl = sem("hidden_low")
        s_out = sem("result_written")
        s_ctx = sem("ctx_loaded")
        s_scl = sem("norm_scales")
        s_pad = sem("conv_pads")
        s_sq2 = sem("qk2_squares")
        s_qk2 = sem("qk2_normed")
        s_qw2 = sem("qk2_swapped_copied")
        s_qt2 = sem("qk2_transposed")
        s_qc2 = sem("qk2_transposed_copied")
        s_fa = sem("dft_tokens")
        s_fac = sem("dft_tokens_copied")
        s_fy = sem("dft_channels")
        s_fyc = sem("fourier_branch")
        s_yc = sem("conv_branch")
        s_yh = sem("branches_high")
        s_yl = sem("branches_low")
        s_s2 = sem("scores2")
        s_n2 = sem("row_max2")
        s_e2 = sem("exp2_done")
        s_t2 = sem("probs2_transposed")
        s_p2 = sem("probs2_copied")
        s_o2 = sem("head2_output")
        s_oe2 = sem("head2_output_copied")
        s_bg = sem("branch_half_done")
        s_dgb = sem("gate_diagonals")
        s_gt = sem("gate_rows")
        s_gtc = sem("gate_rows_copied")

        def tiled(w, l, r, kt, c, n):
            return w[l, r:r + kt * P, c:c + n].rearrange("(a p) n -> p a n", p=P)

        def mlp_chunks(up, down, l):
            for i in range(4):
                for j in (2 * i, 2 * i + 1):
                    for h in range(2):
                        yield tiled(up, l, 0, KT, 512 * j + 256 * h, 256), KT, 256
                for j in (2 * i, 2 * i + 1):
                    for h in range(2):
                        yield tiled(down, l, 512 * j, 4, 512 * h, 512), 4, 512

        def halves(w, l, c):
            for h in range(2):
                yield tiled(w, l, 512 * h, 4, c, 512), 4, 512

        def mod_chunks(l, g):
            for j in (g, g + 1):
                yield from halves(a["w_mod_2"], l, 512 * j)

        def chunks1(l):
            w = a["w_in"]
            yield from mod_chunks(0, 6 * l)
            for c in (0, 512, 1024):
                yield from halves(w, l, c)
            yield tiled(w, l, 0, KT, 1536, 256), KT, 256
            for c in (C_LQK, C_LQK + 256):
                yield tiled(w, l, 0, KT, c, 256), KT, 256
            yield from halves(w, l, C_LV)
            yield tiled(w, l, 0, KT, C_GATE, 8), KT, 8
            yield from mod_chunks(0, 6 * l + 2)
            for c in (0, 512):
                yield from halves(a["w_out"], l, c)
            yield from mod_chunks(0, 6 * l + 4)
            yield from mlp_chunks(a["w_up"], a["w_down"], l)

        def chunk_words(k):
            return KT * 8 if k < CH1 * DEPTH and k % CH1 == LAST1 else CW

        def chunks2(q):
            w, l = a["w_in_2"], q.layer
            if q.mini:
                yield tiled(w, l, 0, KT, B_K, 256), KT, 256
            if q.mod:
                yield from mod_chunks(1, 6 * q.p)
            for c in (0, 256, 512, B_F):
                yield tiled(w, l, 0, KT, c, 256), KT, 256
            yield from halves(w, l, B_Q)
            yield tiled(w, l, 0, KT, B_K, 256), KT, 256
            for j in range(6):
                yield from halves(w, l, B_G + 512 * j)
            for name in ("w_conv_out_2", "w_four_out_2"):
                yield tiled(a[name], l, 0, 2, 0, D), 2, D
            for j in range(2):
                yield tiled(a["w_attn_out_2"], l, 0, 4, 512 * j, 512), 4, 512
            if q.mod:
                yield from mod_chunks(1, 6 * q.p + 2)
            for j in range(2):
                yield from halves(a["w_o_2"], l, 512 * j)
            if q.mod:
                yield from mod_chunks(1, 6 * q.p + 4)
            yield from mlp_chunks(a["w_ff1_2"], a["w_ff2_2"], l)

        LP = PASSES[-1]
        NCH = LP.c + CH2

        def units(k):
            return range(2 * (k - 10), 2 * (k - 10) + (4 if k == 18 else 2)) if k >= 10 else ()

        block = ctx.enter_context(nc.Block())

        @block.sync
        def _(sp):
            sp.dma_start(X[:, :, :], a["x"][0].rearrange("(t p) d -> p t d", p=P)).then_inc(s_xin, 16)

            def load(c, k, src, kt, n):
                sp.wait_ge(s_lo, c + 1)
                dst = RAW[:, k % RAW_N, 0:kt * n].rearrange("p (a n) -> p a n", a=kt)
                sp.dma_start(dst, src).then_inc(s_raw[k % RAW_N], 16)

            for l in range(DEPTH):
                for k, (src, kt, n) in enumerate(chunks1(l)):
                    load(CH1 * l + k, k, src, kt, n)
                    if l == DEPTH - 1 and k == 24:
                        sp.wait_ge(s_src, 3 * l + 2)
                        sp.dma_start(CTX[:, :, :], a["ctx_2"][0].rearrange("(t p) d -> p t d", p=P)).then_inc(s_ctx, 16)
            for q in PASSES:
                for k, (src, kt, n) in enumerate(chunks2(q)):
                    c = q.c - q.mini + k
                    load(c, c, src, kt, n)
            sp.wait_ge(s_out, 16)

        @block.gpsimd
        def _(pool):
            nc.gpsimd.memset(NHALF[:, :], -0.5)
            nc.gpsimd.memset(XP[:, :, 0:3], 0.0)
            nc.gpsimd.memset(V65[:, :, :, DH:DH + 1], 1.0).then_inc(s_init, 1)
            pool.wait_ge(s_init, 1)

            def rsqrt(n, width):
                pool.wait_ge(s_ms, n + 1)
                nc.gpsimd.tensor_tensor(RS[:, 0:width], MS[:, 0:width], NHALF[:, 0:width], ALU.pow).then_inc(s_rs, 1)

            for l in range(DEPTH):
                for j, width in enumerate((2, 2 * NQK, 8, 2)):
                    rsqrt(4 * l + j, width)
            pool.wait_ge(s_src, 3 * DEPTH - 1)
            nc.gpsimd.memset(CXP[:, :, 0:1], 0.0)
            nc.gpsimd.memset(CXP[:, :, S + 1:S + 2], 0.0).then_inc(s_pad, 1)
            for q in PASSES:
                if q.mini:
                    rsqrt(q.pow - 2, 2)
                    rsqrt(q.pow - 1, 2 * KVH)
                for j, width in enumerate((2, 2 * (QH + KVH), 2)):
                    rsqrt(q.pow + j, width)

        @block.scalar
        def _(act):
            def cast(dst, src):
                return nc.scalar.copy(dst, src)

            chain = [0]

            def link(ins):
                chain[0] += 1
                ins.then_inc(s_av, 1)
                act.wait_ge(s_av, chain[0])

            n_cst = [0]

            def const(dst, src):
                act.dma_start(dst, src).then_inc(s_cst, 16)
                n_cst[0] += 1

            const(CT[:, :], a["constants"])
            const(SEL[:, :], a["selector"])
            for name, row, n in (("ln1", 0, 16), ("ln2", 16, 16), ("g_norm1_2", 32, 16), ("g_norm2_2", 48, 16)):
                const(PR0[row:row + n, :], a[name].rearrange("l (k p) -> (l k) p", p=P))
            const(PR0[64:72, :], a["c_2"].rearrange("l (k p) -> (l k) p", p=P))
            const(PR0[72:80, :], a["c_ctx_2"].rearrange("(k p) -> k p", p=P))
            const(PR0[80:112, :], a["conv_w"].rearrange("l j (k p) -> (l j k) p", p=P))
            const(PR0[112:120, :], a["conv_b"].rearrange("l (k p) -> (l k) p", p=P))
            const(PR1[0:96, :], a["b_mod_2"].rearrange("l (k p) -> (l k) p", p=P))
            const(PR1[96:108, :], a["w_conv_2"].rearrange("l j (k p) -> (l j k) p", p=P))

            def rows(dst, src):
                const(dst, src.partition_broadcast(P))

            for i, name in enumerate(("moba_q_norm", "moba_k_norm", "swa_q_norm", "swa_k_norm")):
                rows(GN[:, :, i, :], a[name])
            rows(MN[:, :, :], a["mlstm_norm"].rearrange("l h d -> l (h d)"))
            rows(IFB[:, :, 0:4], a["igate_b"])
            rows(IFB[:, :, 4:8], a["fgate_b"])
            rows(SK[:, :, :], a["swa_sinks"])
            for i, name in enumerate(("g_q_2", "g_k_2")):
                rows(GQ2[:, :, i, :], a[name])
            assert n_cst[0] == N_CONST

            act.wait_ge(s_par, 1)
            cast(PAR[:, 0:120], PS[:, 6, 0:120])
            cast(PAR[:, 128:236], PS[:, 7, 0:108]).then_inc(s_parc, 1)
            act.wait_ge(s_parc, 1)
            nc.scalar.activation(SGC[:, :], PAR[:, 64:80], ACT.Sigmoid).then_inc(s_cs, 1)
            act.wait_ge(s_cs, 2)
            cast(C4[:, :, 0:2], CS[:, :, :].rearrange("p s k -> p k s")).then_inc(s_c4, 1)

            def split(c, k):
                act.wait_ge(s_raw[k % RAW_N], 16 * (c // RAW_N + 1))
                act.wait_ge(s_used, c + 1)
                n = chunk_words(k)
                cast(HI[:, k % HL_N, 0:n], RAW[:, k % RAW_N, 0:n]).then_inc(s_hi, 1)

            def ahead(c):
                if c + SPLIT_LEAD < NCH:
                    split(c + SPLIT_LEAD, c + SPLIT_LEAD)

            def sum_squares(src):
                for t in range(NT):
                    last = nc.scalar.activation(YN[:, t, :], src[:, t, :], ACT.Square, accum_out=SSQ[:, t:t + 1])
                last.then_inc(s_ss, 1)

            def high(n, scale=None, shift=None, steps=range(4)):
                for s in steps:
                    act.wait_ge(s_tp, n + s - steps[0] + 1)
                    dst = AH[:, 2 * s:2 * s + 2, :].rearrange("p a n -> p (a n)")
                    if scale is None:
                        cast(dst, PS[:, 6 + s % 2, :]).then_inc(s_thi, 1)
                        continue
                    for j in range(2):
                        last = nc.scalar.activation(TMP[:, s % 2, 256 * j:256 * j + 256],
                                                    PS[:, 6 + s % 2, 256 * j:256 * j + 256], ACT.Identity,
                                                    scale=scale(2 * s + j),
                                                    bias=0.0 if shift is None else shift(2 * s + j))
                    link(last)
                    cast(dst, TMP[:, s % 2, :]).then_inc(s_thi, 1)

            def copy_group(pair, c, dst, n):
                act.wait_ge(s_used, c + 1 + HL_N)
                for t in range(NT):
                    last = cast(dst[:, t, :], PS[:, 2 * pair + t, 0:n])
                last.then_inc(s_gfree, 1)

            def modulation(g, c):
                for j in range(MODC):
                    ahead(c + j)
                    if j % 2:
                        act.wait_ge(s_used, c + j + 1 + HL_N)
                        if g + j // 2 > 0:
                            act.wait_ge(s_mcol, g + j // 2)
                        cast(ROWS[0:4, :], PS[0:4, 4 + j // 2, :]).then_inc(s_mrow, 1)

            def mlp(q, c, u):
                for i in range(4):
                    for j in range(8):
                        ahead(c + 8 * i + j)
                        if j < 4:
                            act.wait_ge(s_used, c + 8 * i + j + 1 + HL_N)
                            nc.scalar.activation(RL[:, j % 2, :], PS[:, 4 + (u + j) % 2, :], ACT.Relu).then_inc(s_rl, 1)
                            act.wait_ge(s_rl, 16 * q + 4 * i + j + 1)
                            nc.scalar.activation(HIDH[:, j // 2, 2 * (j % 2):2 * (j % 2) + 2, :].rearrange("p a n -> p (a n)"),
                                                 RL[:, j % 2, :], ACT.Square).then_inc(s_hh, 1)

            for c in range(SPLIT_LEAD):
                split(c, c)

            for l in range(DEPTH):
                c0, g0, u0, t0, h0 = CH1 * l + MODC, GR1 * l, UC1 * l, 3 * l, 12 * l
                if l == 0:
                    act.wait_ge(s_xin, 16)
                else:
                    act.wait_ge(s_gfree, g0 + 2)
                sum_squares(X)
                high(4 * t0, lambda k: PAR[:, 8 * l + k:8 * l + k + 1])
                modulation(6 * l, c0 - MODC)
                for k in range(12):
                    ahead(c0 + k)
                    if k in (1, 3, 5):
                        copy_group(k // 2 % 2, c0 + k, Z[:, :, 512 * (k // 2):512 * (k // 2) + 512], 512)
                    if k == 3:
                        act.wait_ge(s_gfree, g0 + 4)
                        nc.scalar.activation(QK[:, :, 0:12, :].rearrange("p t h d -> p t (h d)"),
                                             Z[:, :, 0:768], ACT.Square)
                    if k == 6:
                        copy_group(1, c0 + k, Z[:, :, 1536:1792], 256)
                        act.wait_ge(s_gfree, g0 + 6)
                        nc.scalar.activation(QK[:, :, 12:NQK, :].rearrange("p t h d -> p t (h d)"),
                                             Z[:, :, C_SQ:C_SV], ACT.Square).then_inc(s_sq, 1)
                    if k in (7, 8):
                        act.wait_ge(s_used, c0 + k + 1 + HL_N)
                        j = k - 7
                        cast(XP[:, 2 * j:2 * j + 2, 3:3 + S],
                             PS[:, 4 + j, :].rearrange("p (a n) -> p a n", a=2)).then_inc(s_ufree, 1)
                    if k == 10:
                        copy_group(0, c0 + k, Z[:, :, Z_LV:Z_GATE], 512)
                        act.wait_ge(s_gfree, g0 + 7)
                        cast(V65[:, :, :, 0:DH],
                             Z[:, :, Z_LV:Z_LO].rearrange("p t (h d) -> p t h d", h=ML_H)).then_inc(s_v65, 1)
                    if k == 11:
                        copy_group(1, c0 + k, Z[:, :, Z_GATE:ZW], 8)
                act.wait_ge(s_qk, l + 1)
                cast(QK[:, :, NQK, :], QK[:, :, NQK - 1, :])
                cast(QK[:, :, NQK + 1, :], QK[:, :, NQK - 2, :]).then_inc(s_qsw, 1)
                for j in range(6):
                    w = 512 if j < 5 else 256
                    act.wait_ge(s_qt, 6 * l + j + 1)
                    cast(QKT[:, 2 * j:2 * j + w // 256, :].rearrange("p a n -> p (a n)"),
                         PS[:, 6 + j % 2, 0:w]).then_inc(s_qtc, 1)

                def exps(h):
                    act.wait_ge(s_nb, h0 + h + 1)
                    nc.scalar.activation(PM[:, h % 2, 0:128], PM[:, h % 2, 0:128], ACT.Exp, scale=ISC,
                                         bias=NB[:, h, 0:1], accum_out=SUM[:, h, 0:1])
                    nc.scalar.activation(PM[:, h % 2, 128:384], PM[:, h % 2, 128:384], ACT.Exp, scale=ISC,
                                         bias=NB[:, h, 1:2], accum_out=SUM[:, h, 1:2]).then_inc(s_e, 1)

                def head_out(h):
                    act.wait_ge(s_o, h0 + h + 1 + 2)
                    col = DH * h if h < MOBA_H else DH * (h + ML_H)
                    cast(YN[:, :, col:col + DH],
                         PS[:, 4 + h % 2, 0:128].rearrange("p (t d) -> p t d", t=2)).then_inc(s_oe, 1)

                for h in range(14):
                    if h < 12:
                        exps(h)
                    if h >= 2:
                        head_out(h - 2)
                act.wait_ge(s_ske, l + 1)
                nc.scalar.activation(SKE[:, :, :], SKE[:, :, :], ACT.Exp).then_inc(s_sko, 1)

                act.wait_ge(s_ga, l + 1)
                link(nc.scalar.activation(GT1[:, :, :], GT1[:, :, :], ACT.Exp))
                nc.scalar.activation(GT1[:, :, :], GT1[:, :, :], ACT.Ln, bias=1.0).then_inc(s_gl, 1)
                act.wait_ge(s_me, l + 1)
                nc.scalar.activation(ME[:, :, :, :], ME[:, :, :, :], ACT.Exp).then_inc(s_mex, 1)
                act.wait_ge(s_mem, l + 1)
                nc.scalar.activation(GT2[:, :, :], GT2[:, :, :], ACT.Exp, scale=-1.0).then_inc(s_exm, 1)
                act.wait_ge(s_cv, l + 1)
                nc.scalar.activation(SG[:, :, :], CV[:, :, :], ACT.Sigmoid).then_inc(s_sg, 1)
                act.wait_ge(s_mt, l + 1)
                for j in range(3):
                    last = cast(PTM[:, j, :, :].rearrange("p a n -> p (a n)"), PS[:, 3 + j, :])
                last.then_inc(s_mtc, 1)
                nc.scalar.activation(Z[:, :, Z_LO:Z_GATE], Z[:, :, Z_LO:Z_GATE], ACT.Sigmoid).then_inc(s_so, 1)
                act.wait_ge(s_h, l + 1)
                nc.scalar.activation(CV[:, 0:2, :], HM[:, :, :], ACT.Square).then_inc(s_hsq, 1)

                high(4 * t0 + 4)
                modulation(6 * l + 2, c0 + 12)
                for k in range(12, 16):
                    ahead(c0 + MODC + k)
                act.wait_ge(s_gfree, g0 + 8 + 2)
                sum_squares(X)
                high(4 * t0 + 8, lambda k: PAR[:, 16 + 8 * l + k:17 + 8 * l + k])
                modulation(6 * l + 4, c0 + MODC + 16)
                mlp(l, c0 + 2 * MODC + 16, u0 + 2)

            act.wait_ge(s_ctx, 16)

            def norm_scale(q, n, stream):
                return (lambda k: SCL[:, q.layer, n, k, stream:stream + 1],
                        lambda k: MOD[:, q.layer, M_SH[n] + k, stream:stream + 1])

            def keys_out(qk, j, ctx):
                act.wait_ge(s_qt2, j + 1)
                cast(KTB[:, :, S * ctx:S * ctx + S],
                     PS[:, 6, :].rearrange("p (a n) -> p a n", a=2)).then_inc(s_qc2, 1)

            def gate_rows(n):
                act.wait_ge(s_gt, n + 1)
                cast(GTB[:, 0:512], PS[:, 6, :])
                cast(GTB[:, 512:1024], PS[:, 7, :]).then_inc(s_gtc, 1)

            for q in PASSES:
                c0, g0, R = q.c_in, q.g, CTX if q.stream else X
                act.wait_ge(s_scl, q.layer + 1)
                if q.mini:
                    act.wait_ge(s_gfree, q.g - 1 + 2)
                    sum_squares(CTX)
                    high(q.t - 4, *norm_scale(q, 0, 1))
                    ahead(c0 - 1)
                    copy_group(1, c0 - 1, ZN[:, :, N_K:1024], 256)
                    act.wait_ge(s_gfree, q.g + 2)
                    cast(VB[:, 2:4, :], ZN[:, :, N_V:1024])
                    nc.scalar.activation(QK2[:, :, 8:10, :].rearrange("p t h d -> p t (h d)"), ZN[:, :, N_K:N_V],
                                         ACT.Square).then_inc(s_sq2, 1)
                    act.wait_ge(s_qk2, q.qk)
                    cast(QK2[:, :, 10, :], QK2[:, :, 9, :])
                    cast(QK2[:, :, 11, :], QK2[:, :, 8, :]).then_inc(s_qw2, 1)
                    keys_out(q.qk - 1, 3 * (q.qk - 1), 1)
                else:
                    act.wait_ge(s_gfree, q.g + 2)
                sum_squares(R)
                high(q.t, *norm_scale(q, 0, q.stream))
                if q.mod:
                    modulation(q.mg, q.c)
                qt0 = 3 * q.p + (1 if q.mini else 0)
                for k in range(19):
                    ahead(c0 + k)
                    if k < 3:
                        act.wait_ge(s_used, c0 + k + 1 + HL_N)
                        cast(UB[:, k, :, :].rearrange("p a n -> p (a n)"), PS[:, 4 + (q.u + k) % 2, :]).then_inc(s_ufree, 1)
                    if k == 3:
                        copy_group(0, c0 + k, ZN[:, :, N_F:N_Q], 256)
                    if k == 5:
                        copy_group(1, c0 + k, ZN[:, :, N_Q:N_K], 512)
                    if k == 6:
                        copy_group(0, c0 + k, ZN[:, :, N_K:1024], 256)
                        act.wait_ge(s_gfree, g0 + 3 + 2)
                        nc.scalar.activation(QK2[:, :, 0:10, :].rearrange("p t h d -> p t (h d)"), ZN[:, :, N_Q:N_V],
                                             ACT.Square).then_inc(s_sq2, 1)
                        cast(VB[:, 2 * q.stream:2 * q.stream + 2, :], ZN[:, :, N_V:1024])
                        act.wait_ge(s_fa, q.p + 1)
                        for j in range(2):
                            last = cast(A12[:, j, :, :].rearrange("p a n -> p (a n)"), PS[:, 6 + j, :])
                        last.then_inc(s_fac, 1)
                    if k == 7:
                        act.wait_ge(s_fy, q.p + 1)
                        cast(YF[:, :, :].rearrange("p a n -> p (a n)"), PS[:, 6, :]).then_inc(s_fyc, 1)
                    if k >= 8 and k % 2 == 0:
                        j = k // 2 - 4
                        act.wait_ge(s_used, c0 + k + 1 + HL_N)
                        for t in range(NT):
                            last = nc.scalar.activation(GA[:, t, 512 * j:512 * j + 512], PS[:, t, :], ACT.Tanh, scale=0.5)
                        last.then_inc(s_gfree, 1)
                    if k == 9:
                        act.wait_ge(s_qk2, q.qk + 1)
                        cast(QK2[:, :, 10, :], QK2[:, :, 9, :])
                        cast(QK2[:, :, 11, :], QK2[:, :, 8, :]).then_inc(s_qw2, 1)
                        for j in range(2):
                            act.wait_ge(s_qt2, qt0 + j + 1)
                            cast(QT2[:, 2 * j:2 * j + 2, :].rearrange("p a n -> p (a n)"),
                                 PS[:, 6 + j, :]).then_inc(s_qc2, 1)
                        keys_out(q.qk, qt0 + 2, q.stream)
                    for v in units(k):
                        if v < 16:
                            h, t = divmod(v, 2)
                            n = 256 if q.stream else 512
                            act.wait_ge(s_n2, q.att + v + 1)
                            act.wait_ge(s_t2, q.att + v + 1)
                            nc.scalar.activation(PM[:, v % 2, 0:n], PS[:, 4 + v % 2, 0:n], ACT.Exp,
                                                 bias=NM2[:, h, t:t + 1], accum_out=SM2[:, h, t:t + 1]).then_inc(s_e2, 1)
                        if v >= 4:
                            h, t = divmod(v - 4, 2)
                            act.wait_ge(s_o2, q.att + v - 4 + 1 + 2)
                            cast(YA[:, t, DH * h:DH * h + DH], PS[:, 2 + v % 2, 0:DH]).then_inc(s_oe2, 1)
                act.wait_ge(s_yc, q.p + 1)
                act.wait_ge(s_fyc, q.p + 1)
                act.wait_ge(s_used, c0 + 19 + HL_N)
                cast(AH[:, 0:2, :], YC[:, :, :])
                cast(AH[:, 2:4, :], YF[:, :, :]).then_inc(s_yh, 1)
                high(q.t + 4, steps=(2, 3))
                for k in range(19, 23):
                    ahead(c0 + k)
                high(q.t + 6)
                if q.mod:
                    modulation(q.mg + 2, q.c_br + 4)
                gate_rows(2 * q.p)
                for k in range(4):
                    ahead(q.c_o + k)
                act.wait_ge(s_gfree, g0 + 17 + 2)
                sum_squares(R)
                high(q.t + 10, *norm_scale(q, 1, q.stream))
                if q.mod:
                    modulation(q.mg + 4, q.c_o + 4)
                gate_rows(2 * q.p + 1)
                mlp(q.mlp, q.c_mlp, q.u + 3)

            act.wait_ge(s_gfree, LP.g + GR2 + 2)
            act.dma_start(out[0].rearrange("(t p) d -> p t d", p=P), X[:, :, :]).then_inc(s_out, 16)
            act.wait_ge(s_out, 16)

        @block.vector
        def _(dve):
            chain = [0]

            def link(ins):
                chain[0] += 1
                ins.then_inc(s_dv, 1)
                dve.wait_ge(s_dv, chain[0])

            tt, ts, stt = nc.vector.tensor_tensor, nc.vector.tensor_scalar, nc.vector.scalar_tensor_tensor
            for s, n in ((s_lo, RAW_N), (s_used, HL_N), (s_gfree, 2), (s_ufree, 2), (s_tlo, 2), (s_qtc, 2), (s_sm, 2), (s_pt, 2), (s_pe, 2), (s_o, 2), (s_oe, 2),
                         (s_qc2, 2), (s_e2, 2), (s_t2, 2), (s_p2, 2), (s_o2, 2), (s_oe2, 2)):
                dve.sem_inc(s, n)

            dve.wait_ge(s_cst, 16 * N_CONST)
            link(ts(NSK[:, :, :], SK[:, :, :], -1.0, None, ALU.mult))
            dve.wait_ge(s_cs, 1)
            tt(CS[:, :, :].rearrange("p s k -> p (s k)"), PAR[:, 64:80], SGC[:, :], ALU.mult).then_inc(s_cs, 1)
            dve.wait_ge(s_c4, 1)
            tt(C4[:, :, 2:4], CS[:, :, :].rearrange("p s k -> p k s"), C4[:, :, 0:2].bitcast(F32),
               ALU.subtract).then_inc(s_c4, 1)

            def split(c, k):
                dve.wait_ge(s_hi, c + 1)
                n = chunk_words(k)
                tt(LO[:, k % HL_N, 0:n], RAW[:, k % RAW_N, 0:n], HI[:, k % HL_N, 0:n].bitcast(F32),
                   ALU.subtract).then_inc(s_lo, 1)

            def ahead(c):
                if c + SPLIT_LEAD < NCH:
                    split(c + SPLIT_LEAD, c + SPLIT_LEAD)

            def norm(n, m, src):
                dve.wait_ge(s_ss, n + 1)
                ts(MS[:, 0:2], SSQ[:, :], 1.0 / D, EPS, ALU.mult, ALU.add).then_inc(s_ms, 1)
                dve.wait_ge(s_rs, m + 1)
                for t in range(NT):
                    last = ts(YN[:, t, :], src[:, t, :], RS[:, t:t + 1], None, ALU.mult)
                last.then_inc(s_src, 1)

            def low(n, scaled, steps=range(4)):
                for s in steps:
                    dve.wait_ge(s_thi, n + s - steps[0] + 1)
                    full = TMP[:, s % 2, :] if scaled else PS[:, 6 + s % 2, :]
                    tt(AL[:, 2 * s:2 * s + 2, :].rearrange("p a n -> p (a n)"), full,
                       AH[:, 2 * s:2 * s + 2, :].rearrange("p a n -> p (a n)").bitcast(F32),
                       ALU.subtract).then_inc(s_tlo, 1)

            def add_group(c, half, res=X, gate=None, g=None):
                dve.wait_ge(s_used, c + 1 + HL_N)
                cols = slice(512 * half, 512 * half + 512)
                src = [PS[:, 2 * half + t, :] for t in range(NT)]
                if gate is not None:
                    dve.wait_ge(s_gfree, g + 2)
                    for t in range(NT):
                        last = tt(TM[:, t, :], src[t], gate[:, cols], ALU.mult)
                    link(last)
                    src = [TM[:, t, :] for t in range(NT)]
                for t in range(NT):
                    last = tt(res[:, t, cols], src[t], res[:, t, cols], ALU.add)
                last.then_inc(s_gfree, 1)

            def modulation(l, g, c):
                for j in range(MODC):
                    ahead(c + j)
                for j in (g, g + 1):
                    dve.wait_ge(s_mcol, j + 1)
                    k = 4 * (j % 12)
                    tt(MOD[:, l, k:k + 4, :], PS[:, 4 + j % 2, 0:8].rearrange("p (c s) -> p c s", s=2),
                       PAR[:, 128 + 48 * l + k:132 + 48 * l + k].unsqueeze(2).to_broadcast((P, 4, 2)),
                       ALU.add).then_inc(s_modc, 1)

            def mlp(q, c, u):
                for i in range(4):
                    for j in range(8):
                        ahead(c + 8 * i + j)
                        if j < 4:
                            cols = 2 * (j % 2)
                            hid = HIDH[:, j // 2, cols:cols + 2, :].rearrange("p a n -> p (a n)")
                            dve.wait_ge(s_rl, 16 * q + 4 * i + j + 1)
                            stt(U2[:, j % 2, :], PS[:, 4 + (u + j) % 2, :], 0.0, RL[:, j % 2, :], ALU.max,
                                ALU.mult).then_inc(s_ufree, 1)
                            dve.wait_ge(s_ufree, u + 4 * i + j + 1 + 2)
                            dve.wait_ge(s_hh, 16 * q + 4 * i + j + 1)
                            tt(HIDL[:, j // 2, cols:cols + 2, :].rearrange("p a n -> p (a n)"),
                               U2[:, j % 2, :], hid.bitcast(F32), ALU.subtract).then_inc(s_hl, 1)

            for c in range(SPLIT_LEAD):
                split(c, c)

            for l in range(DEPTH):
                c0, g0, u0, t0, h0 = CH1 * l + MODC, GR1 * l, UC1 * l, 3 * l, 12 * l
                norm(2 * l, 4 * l, X)
                low(4 * t0, True)
                modulation(0, 6 * l, c0 - MODC)
                runs = ((QK[:, :, 0:12, :], Z[:, :, 0:768]), (QK[:, :, 12:NQK, :], Z[:, :, C_SQ:C_SV]))
                runs = [(q, z.rearrange("p t (h d) -> p t h d", d=DH)) for q, z in runs]
                for k in range(12):
                    ahead(c0 + k)
                    if k == 7:
                        dve.wait_ge(s_sq, l + 1)
                        link(nc.vector.tensor_reduce(MS[:, 0:2 * NQK].rearrange("p (t h) -> p t h", t=NT),
                                                     QK[:, :, 0:NQK, :], AX_X, ALU.add))
                        ts(MS[:, 0:2 * NQK], MS[:, 0:2 * NQK], 1.0 / DH, EPS, ALU.mult, ALU.add).then_inc(s_ms, 1)
                    if k == 8:
                        dve.wait_ge(s_rs, 4 * l + 2)
                        rs = RS[:, 0:2 * NQK].rearrange("p (t h) -> p t h", t=NT).unsqueeze(3)
                        for (q, z), (h1, h2) in zip(runs, ((0, 12), (12, NQK))):
                            last = tt(q, z, rs[:, :, h1:h2, :].to_broadcast((P, NT, h2 - h1, DH)), ALU.mult)
                        link(last)
                        for i, (h1, h2) in enumerate(((0, 6), (6, 12), (12, 18), (18, 20))):
                            q = QK[:, :, h1:h2, :]
                            g = GN[:, l:l + 1, i:i + 1, :].to_broadcast((P, NT, h2 - h1, DH))
                            last = tt(q, q, g, ALU.mult)
                        link(last)
                    if k == 9:
                        sin = CT[:, K_R1 + 64:K_R1 + 128].rearrange("p (t h d) -> p t h d", t=NT, h=1)
                        for q, z in runs:
                            b = sin.to_broadcast((P, NT, q.shape[2], 32))
                            tt(z[:, :, :, 0:32], q[:, :, :, 32:64], b, ALU.mult)
                            last = tt(z[:, :, :, 32:64], q[:, :, :, 0:32], b, ALU.mult)
                        link(last)
                    if k == 10:
                        cos = CT[:, K_R1:K_R1 + 64].rearrange("p (t h d) -> p t h d", t=NT, h=1)
                        q = QK[:, :, 0:NQK, :].rearrange("p t h (a d) -> p t (h a) d", a=2)
                        link(tt(q, q, cos.to_broadcast((P, NT, 2 * NQK, 32)), ALU.mult))
                        for q, z in runs:
                            tt(q[:, :, :, 0:32], q[:, :, :, 0:32], z[:, :, :, 0:32], ALU.subtract)
                            last = tt(q[:, :, :, 32:64], q[:, :, :, 32:64], z[:, :, :, 32:64], ALU.add)
                        last.then_inc(s_qk, 1)

                zero_m, caus = CT[:, K_M:K_M + 128], CT[:, K_M + 128:K_M + 256]
                for h in range(13):
                    if h < 12:
                        dve.wait_ge(s_s, h0 + h + 1)
                        dve.wait_ge(s_pt, h0 + h + 1)
                        old = CT[:, K_M:K_M + 256] if h < MOBA_H else CT[:, K_M + 256:K_M + 512]
                        nc.vector.tensor_tensor_reduce(PM[:, h % 2, 0:128], PS[:, h % 2, 0:128], caus, 1.0, -3e38,
                                                       ALU.add, ALU.max, MX[:, h % 2, 0:1])
                        nc.vector.tensor_tensor_reduce(PM[:, h % 2, 128:384], PS[:, h % 2, 128:384], old, 1.0, -3e38,
                                                       ALU.add, ALU.max, MX[:, h % 2, 1:2]).then_inc(s_sm, 1)
                        dve.wait_ge(s_sm, h0 + h + 1 + 2)
                        if h < MOBA_H:
                            ts(NB[:, h, :], MX[:, h % 2, :], -ISC, None, ALU.mult).then_inc(s_nb, 1)
                        else:
                            ts(NB[:, h, :], MX[:, h % 2, :], -ISC, NSK[:, l, h - 6:h - 5], ALU.mult,
                               ALU.min).then_inc(s_nb, 1)
                    if h >= 1:
                        dve.wait_ge(s_pt, h0 + h + 2)
                        dve.wait_ge(s_o, h0 + h)
                        nc.vector.tensor_copy(PTS[:, (h - 1) % 2, 0:384],
                                              PS[:, 2 + (h - 1) % 2, 0:384]).then_inc(s_pe, 1)
                tt(SKE[:, :, :], NB[:, 6:12, :], SK[:, l, :].unsqueeze(2).to_broadcast((P, 6, 2)),
                   ALU.add).then_inc(s_ske, 1)
                dve.wait_ge(s_e, h0 + 12)
                dve.wait_ge(s_sko, l + 1)
                link(tt(SUM[:, 6:12, :], SUM[:, 6:12, :], SKE[:, :, :], ALU.add))
                link(nc.vector.reciprocal(RIN[:, :, :], SUM[:, :, :]))
                dve.wait_ge(s_oe, h0 + 12 + 2)
                for col, h1 in ((0, 0), (DH * (MOBA_H + ML_H), 6)):
                    y = YN[:, :, col:col + 6 * DH].rearrange("p t (h d) -> p t h d", h=6)
                    tt(y, y, RIN[:, h1:h1 + 6, :].rearrange("p h t -> p t h").unsqueeze(3).to_broadcast((P, NT, 6, DH)),
                       ALU.mult)

                dve.wait_ge(s_gfree, g0 + 6 + 2)
                link(tt(G8[:, :, :], Z[:, :, Z_GATE:ZW], IFB[:, l:l + 1, :].to_broadcast((P, NT, 8)), ALU.add))
                f = G8[:, :, 4:8]
                stt(GT1[:, :, :], f, -1.0, f, ALU.mult, ALU.min).then_inc(s_ga, 1)
                dve.wait_ge(s_gl, l + 1)
                stt(GT2[:, :, :], f, 0.0, GT1[:, :, :], ALU.min, ALU.subtract).then_inc(s_lf, 1)
                dve.wait_ge(s_b, l + 1)
                link(nc.vector.tensor_copy(BS[:, :, :], PS[:, 6, 0:8].rearrange("p (t h) -> p t h", t=NT)))
                link(tt(ES[:, :, :], G8[:, :, 0:4], BS[:, :, :], ALU.subtract))
                for t in range(NT):
                    last = tt(DG[:, t, :, :], IDM.unsqueeze(1).to_broadcast((P, ML_H, P)),
                              ES[:, t, :].unsqueeze(2).to_broadcast((P, ML_H, P)), ALU.mult)
                last.then_inc(s_dg, 1)
                dve.wait_ge(s_eb, l + 1)
                for j in range(3):
                    m = (zero_m if j == 1 else caus).unsqueeze(1).to_broadcast((P, ML_H, P))
                    last = tt(ME[:, j, :, :], PS[:, 6 + j // 2, :].rearrange("p (h n) -> p h n", h=ML_H), m, ALU.add)
                link(last)
                link(nc.vector.tensor_reduce(RMX[:, :, :], ME[:, :, :, :], AX_X, ALU.max))
                link(tt(RMX[:, 1, :], RMX[:, 1, :], RMX[:, 2, :], ALU.max))
                link(ts(RR[:, :, :], RMX[:, 0:2, :], 0.0, None, ALU.max))
                for j in range(3):
                    last = tt(ME[:, j, :, :], ME[:, j, :, :],
                              RR[:, (j + 1) // 2, :].unsqueeze(2).to_broadcast((P, ML_H, P)), ALU.subtract)
                last.then_inc(s_me, 1)
                tt(GT2[:, :, :], BS[:, :, :], RR[:, :, :], ALU.add).then_inc(s_mem, 1)
                dve.wait_ge(s_ufree, u0 + 2 + 2)
                wc = lambda j, q: PAR[:, 80 + 16 * l + 4 * j + q:81 + 16 * l + 4 * j + q]
                for q in range(4):
                    ts(CV[:, q, :], XP[:, q, 0:S], wc(0, q), PAR[:, 112 + 4 * l + q:113 + 4 * l + q],
                       ALU.mult, ALU.add)
                for j in range(1, 4):
                    link(nc.vector.engine_nop())
                    for q in range(4):
                        last = stt(CV[:, q, :], XP[:, q, j:j + S], wc(j, q), CV[:, q, :], ALU.mult, ALU.add)
                last.then_inc(s_cv, 1)
                dve.wait_ge(s_sg, l + 1)
                tt(CV[:, :, :], CV[:, :, :], SG[:, :, :], ALU.mult).then_inc(s_lqk, 1)
                dve.wait_ge(s_mex, l + 1)
                dve.wait_ge(s_ms3, l + 1)
                for j in range(3):
                    for b in range(2):
                        m = ME[:, j, b:ML_H:2, :]
                        last = stt(m, PS[:, 2 * j + b, 0:256].rearrange("p (h n) -> p h n", h=2), ISC, m,
                                   ALU.mult, ALU.mult)
                last.then_inc(s_mp, 1)
                dve.wait_ge(s_exm, l + 1)
                dve.wait_ge(s_mo, l + 1)
                o = PS[:, 6:8, 0:260].rearrange("p t (h d) -> p t h d", h=ML_H)
                link(nc.vector.tensor_copy(DEN[:, :, :], o[:, :, :, DH]))
                link(stt(GT1[:, :, :], DEN[:, :, :], -1.0, DEN[:, :, :], ALU.mult, ALU.max))
                link(tt(DEN[:, :, :], GT1[:, :, :], GT2[:, :, :], ALU.max))
                link(nc.vector.reciprocal(DEN[:, :, :], DEN[:, :, :]))
                hm = HM[:, :, :].rearrange("p t (h d) -> p t h d", h=ML_H)
                link(tt(hm, o[:, :, :, 0:DH], DEN[:, :, :].unsqueeze(3).to_broadcast((P, NT, ML_H, DH)), ALU.mult))
                dve.wait_ge(s_so, l + 1)
                tt(HM[:, :, :], HM[:, :, :], Z[:, :, Z_LO:Z_GATE], ALU.mult).then_inc(s_h, 1)
                dve.wait_ge(s_hsq, l + 1)
                link(nc.vector.tensor_reduce(MS[:, 0:8].rearrange("p (t h) -> p t h", t=NT),
                                             CV[:, 0:2, :].rearrange("p t (h d) -> p t h d", h=ML_H), AX_X, ALU.add))
                ts(MS[:, 0:8], MS[:, 0:8], 1.0 / DH, EPS, ALU.mult, ALU.add).then_inc(s_ms, 1)
                dve.wait_ge(s_rs, 4 * l + 3)
                link(tt(hm, hm, RS[:, 0:8].rearrange("p (t h) -> p t h", t=NT).unsqueeze(3)
                        .to_broadcast((P, NT, ML_H, DH)), ALU.mult))
                tt(YN[:, :, MOBA_H * DH:(MOBA_H + ML_H) * DH], HM[:, :, :],
                   MN[:, l:l + 1, :].to_broadcast((P, NT, ML_H * DH)), ALU.mult).then_inc(s_src, 1)

                low(4 * t0 + 4, False)
                modulation(0, 6 * l + 2, c0 + 12)
                for k in range(12, 16):
                    ahead(c0 + MODC + k)
                    if k % 2:
                        add_group(c0 + MODC + k, (k - 12) // 2)
                norm(2 * l + 1, 4 * l + 3, X)
                low(4 * t0 + 8, True)
                modulation(0, 6 * l + 4, c0 + MODC + 16)
                mlp(l, c0 + 2 * MODC + 16, u0 + 2)
                for half in range(2):
                    add_group(c0 + 2 * MODC + 46 + half, half)

            def norm_scales(l):
                dve.wait_ge(s_modc, 12 * l + 12)
                for n in range(2):
                    g = PAR[:, 32 + 16 * n + 8 * l:40 + 16 * n + 8 * l].unsqueeze(2).to_broadcast((P, KT, 2))
                    stt(SCL[:, l, n, :, :], MOD[:, l, M_SC[n]:M_SC[n] + 8, :], 1.0, g, ALU.add, ALU.mult)
                ts(GQ2[:, l, 0, :], GQ2[:, l, 0, :], ISC, None, ALU.mult).then_inc(s_scl, 1)
                dve.wait_ge(s_scl, l + 1)

            norm_scales(0)
            dve.wait_ge(s_pad, 1)

            def head_squares(q, n, h1):
                dve.wait_ge(s_sq2, n + 1)
                w = NT * (10 - h1)
                link(nc.vector.tensor_reduce(MS[:, 0:w].rearrange("p (t h) -> p t h", t=NT), QK2[:, :, h1:10, :],
                                             AX_X, ALU.add))
                ts(MS[:, 0:w], MS[:, 0:w], 1.0 / DH, EPS, ALU.mult, ALU.add).then_inc(s_ms, 1)

            def head_norm(q, m, h1, signal):
                dve.wait_ge(s_rs, m + 1)
                w = NT * (10 - h1)
                z = ZN[:, :, N_Q + DH * h1:N_V].rearrange("p t (h d) -> p t h d", d=DH)
                rs = RS[:, 0:w].rearrange("p (t h) -> p t h", t=NT).unsqueeze(3)
                link(tt(QK2[:, :, h1:10, :], z, rs.to_broadcast((P, NT, 10 - h1, DH)), ALU.mult))
                for i, (a1, a2) in enumerate(((h1, 8), (8, 10))):
                    if a1 < a2:
                        h = QK2[:, :, a1:a2, :]
                        last = tt(h, h, GQ2[:, q.layer:q.layer + 1, i:i + 1, :].to_broadcast((P, NT, a2 - a1, DH)),
                                  ALU.mult)
                last.then_inc(s_qk2, 1) if signal else link(last)

            def gate_diagonals(q, n, factor):
                gt = MOD[:, q.layer, M_GT[n]:M_GT[n] + 8, q.stream]
                last = stt(DGB[:, :, :], gt.unsqueeze(2).to_broadcast((P, 8, P)), factor,
                           IDM.unsqueeze(1).to_broadcast((P, 8, P)), ALU.mult, ALU.mult)
                last.then_inc(s_dgb, 1)

            for q in PASSES:
                c0, g0, R = q.c_in, q.g, CTX if q.stream else X
                if q.mini:
                    norm_scales(1)
                    norm(q.norm - 1, q.pow - 2, CTX)
                    low(q.t - 4, True)
                    ahead(c0 - 1)
                    head_squares(q, q.qk - 1, 8)
                    head_norm(q, q.pow - 1, 8, True)
                norm(q.norm, q.pow, R)
                low(q.t, True)
                if q.mod:
                    modulation(1, q.mg, q.c)
                for k in range(19):
                    ahead(c0 + k)
                    if k == 3:
                        dve.wait_ge(s_ufree, q.u + 3 + 2)
                        link(tt(CXP[:, :, 1:1 + S], UB[:, 1, :, :], UB[:, 2, :, :], ALU.mult))
                        wc = lambda j, b: PAR[:, 224 + 6 * q.layer + 2 * j + b:225 + 6 * q.layer + 2 * j + b]
                        for b in range(2):
                            last = ts(YC[:, b, :], CXP[:, b, 0:S], wc(0, b), None, ALU.mult)
                        link(last)
                    if k in (4, 5):
                        for b in range(2):
                            last = stt(YC[:, b, :], CXP[:, b, k - 3:k - 3 + S], wc(k - 3, b), YC[:, b, :], ALU.mult,
                                       ALU.add)
                        link(last)
                        if k == 5:
                            tt(YC[:, :, :], YC[:, :, :], UB[:, 0, :, :], ALU.mult).then_inc(s_yc, 1)
                    if k == 7:
                        head_squares(q, q.qk, 0)
                        head_norm(q, q.pow + 1, 0, q.stream == 1)
                    if k == 8 and q.stream == 0:
                        qk = QK2[:, :, 0:10, :]
                        z = ZN[:, :, N_Q:N_V].rearrange("p t (h d) -> p t h d", d=DH)
                        sin = CT[:, K_R2 + 64:K_R2 + 128].rearrange("p (t h d) -> p t h d", t=NT, h=1)
                        cos = CT[:, K_R2:K_R2 + 64].rearrange("p (t h d) -> p t h d", t=NT, h=1)
                        b = sin.to_broadcast((P, NT, 10, 32))
                        tt(z[:, :, :, 0:32], qk[:, :, :, 32:64], b, ALU.mult)
                        link(tt(z[:, :, :, 32:64], qk[:, :, :, 0:32], b, ALU.mult))
                        q2 = qk.rearrange("p t h (a d) -> p t (h a) d", a=2)
                        link(tt(q2, q2, cos.to_broadcast((P, NT, 20, 32)), ALU.mult))
                        tt(qk[:, :, :, 0:32], qk[:, :, :, 0:32], z[:, :, :, 0:32], ALU.subtract)
                        tt(qk[:, :, :, 32:64], qk[:, :, :, 32:64], z[:, :, :, 32:64], ALU.add).then_inc(s_qk2, 1)
                    for v in units(k):
                        n = 256 if q.stream else 512
                        if v < 16:
                            h, t = divmod(v, 2)
                            dve.wait_ge(s_s2, q.att + v + 1)
                            nc.vector.tensor_reduce(NM2[:, h, t:t + 1], PS[:, 4 + v % 2, 0:n], AX_X, ALU.max,
                                                    negate=True).then_inc(s_n2, 1)
                        if 2 <= v < 18:
                            dve.wait_ge(s_t2, q.att + v - 2 + 1 + 2)
                            dve.wait_ge(s_o2, q.att + v - 2 + 1)
                            nc.vector.tensor_copy(PTS[:, v % 2, 0:n], PS[:, 6 + v % 2, 0:n]).then_inc(s_p2, 1)
                dve.wait_ge(s_yh, q.p + 1)
                tt(AL[:, 0:2, :], YC[:, :, :], AH[:, 0:2, :].bitcast(F32), ALU.subtract)
                tt(AL[:, 2:4, :], YF[:, :, :], AH[:, 2:4, :].bitcast(F32), ALU.subtract).then_inc(s_yl, 1)
                dve.wait_ge(s_oe2, q.att + 16 + 2)
                link(nc.vector.reciprocal(RN2[:, :, :], SM2[:, :, :]))
                for t in range(NT):
                    y = YA[:, t, :].rearrange("p (h d) -> p h d", h=QH)
                    last = tt(y, y, RN2[:, :, t].unsqueeze(2).to_broadcast((P, QH, DH)), ALU.mult)
                last.then_inc(s_src, 1)
                low(q.t + 4, False, (2, 3))
                for k in range(19, 23):
                    b, halfs = ((0, (0, 1)), (1, (0, 1)), (2, (0,)), (2, (1,)))[k - 19]
                    ahead(c0 + k)
                    for half in halfs:
                        if b < 2 and half == 0:
                            dve.wait_ge(s_bg, 2 * q.p + b + 1)
                        else:
                            dve.wait_ge(s_used, c0 + k + 1 + HL_N)
                        cols = slice(512 * half, 512 * half + 512)
                        for t in range(NT):
                            ga = GA[:, t, D * b + 512 * half:D * b + 512 * half + 512]
                            dst = M2[:, t, cols] if b == 0 else TM[:, t, :]
                            last = stt(dst, ga, 1.0, PS[:, 2 * half + t, :], ALU.add, ALU.mult)
                        last.then_inc(s_gfree, 1)
                        if b > 0:
                            dve.wait_ge(s_gfree, g0 + 9 + 2 * b + half + 1 + 2)
                            for t in range(NT):
                                last = tt(M2[:, t, cols], M2[:, t, cols], TM[:, t, :], ALU.add)
                            if b == 2 and half == 1:
                                last.then_inc(s_src, 1)
                            else:
                                link(last)
                dve.wait_ge(s_src, q.src + 3)
                gate_diagonals(q, 0, 0.5)
                low(q.t + 6, False)
                if q.mod:
                    modulation(1, q.mg + 2, q.c_br + 4)
                dve.wait_ge(s_gtc, 2 * q.p + 1)
                for k in range(4):
                    ahead(q.c_o + k)
                    if k % 2:
                        add_group(q.c_o + k, k // 2, R, GTB, g0 + 15 + k // 2)
                norm(q.norm + 1, q.pow + 2, R)
                dve.wait_ge(s_gfree, g0 + 17 + 2)
                gate_diagonals(q, 1, 1.0)
                low(q.t + 10, True)
                if q.mod:
                    modulation(1, q.mg + 4, q.c_o + 4)
                mlp(q.mlp, q.c_mlp, q.u + 3)
                dve.wait_ge(s_gtc, 2 * q.p + 2)
                for half in range(2):
                    add_group(q.c_mlp + 30 + half, half, R, GTB, g0 + 17 + half)

        @block.tensor
        def _(pe):
            mm = nc.tensor.matmul
            pe.wait_ge(s_cst, 16 * N_CONST)
            nc.tensor.transpose(PS[:, 6, 0:120], PR0[0:120, :], IDM[0:120, 0:120])
            nc.tensor.transpose(PS[:, 7, 0:108], PR1[0:108, :], IDM[0:108, 0:108]).then_inc(s_par, 1)
            pe.wait_ge(s_c4, 2)

            def transposes(source, n, src, steps=range(4)):
                pe.wait_ge(s_src, source + 1)
                for s in range(len(steps)):
                    pe.wait_ge(s_tlo, n + s + 1)
                    for k in range(2):
                        for t in range(NT):
                            last = nc.tensor.transpose(PS[:, 6 + s % 2, 256 * k + 128 * t:256 * k + 128 * t + 128],
                                                       src[:, t, 128 * (2 * s + k):128 * (2 * s + k) + 128], IDM)
                    last.then_inc(s_tp, 1)
                return n + len(steps)

            def split_done(steps):
                pe.wait_ge(s_tlo, steps + 2)

            def arrived(c):
                pe.wait_ge(s_lo, c + 1 + RAW_N)

            def slot(k, kt, n):
                hi = HI[:, k % HL_N, 0:kt * n].rearrange("p (a n) -> p a n", a=kt)
                lo = LO[:, k % HL_N, 0:kt * n].rearrange("p (a n) -> p a n", a=kt)
                return hi, lo

            def tokens_out(c, k, bank, kt, n, ah, al, first, last):
                arrived(c)
                hi, lo = slot(k, kt, n)
                for t in range(NT):
                    o = PS[:, bank + t, 0:n]
                    for j in range(kt):
                        th, tl = ah[:, j, 128 * t:128 * t + 128], al[:, j, 128 * t:128 * t + 128]
                        mm(o, th, hi[:, j, :], start=first and j == 0, stop=False)
                        mm(o, th, lo[:, j, :], start=False, stop=False)
                        ins = mm(o, tl, hi[:, j, :], start=False, stop=last and j == kt - 1)
                ins.then_inc(s_used, 1)

            def features_out(c, k, bank, ah, al):
                arrived(c)
                hi, lo = slot(k, KT, 256)
                for q in range(2):
                    o = PS[:, bank, 256 * q:256 * q + 256]
                    for j in range(KT):
                        wh, wl = hi[:, j, 128 * q:128 * q + 128], lo[:, j, 128 * q:128 * q + 128]
                        mm(o, wh, ah[:, j, :], start=j == 0, stop=False)
                        mm(o, wh, al[:, j, :], start=False, stop=False)
                        ins = mm(o, wl, ah[:, j, :], start=False, stop=j == KT - 1)
                ins.then_inc(s_used, 1)

            def group(g, c, k, n=512):
                pe.wait_ge(s_gfree, g + 1)
                for h in range(2):
                    half_group(c + h, k + h, g % 2, h, n)

            def half_group(c, k, pair, h, n=512):
                tokens_out(c, k, 2 * pair, 4, n, AH[:, 4 * h:4 * h + 4, :], AL[:, 4 * h:4 * h + 4, :], h == 0, h == 1)

            def modulation(g, c, u, ts):
                pe.wait_ge(s_ufree, u + 2)
                for j in range(MODC):
                    arrived(c + j)
                    hi, lo = slot(c + j, 4, 512)
                    for k in range(4):
                        w, o = C4[:, 4 * (j % 2) + k, :], PS[0:4, 4 + j // 2, :]
                        mm(o, w, hi[:, k, :], start=j % 2 == 0 and k == 0, stop=False)
                        last = mm(o, w, lo[:, k, :], start=False, stop=j % 2 == 1 and k == 3)
                    last.then_inc(s_used, 1)
                for j in range(2):
                    pe.wait_ge(s_mrow, g + j + 1)
                    for k in range(4):
                        last = mm(PS[:, 4 + j, 2 * k:2 * k + 2], ROWS[0:4, 128 * k:128 * k + 128], SEL[:, :],
                                  start=True, stop=True)
                    last.then_inc(s_mcol, 1)
                split_done(ts)
                pe.wait_ge(s_modc, g + 2)

            def mlp(q, c, u):
                for i in range(4):
                    for j in range(4):
                        pe.wait_ge(s_ufree, u + 4 * i + j + 1)
                        features_out(c + 8 * i + j, c + 8 * i + j, 4 + (u + j) % 2, AH, AL)
                    for j in range(4):
                        b = j // 2
                        pe.wait_ge(s_hl, 16 * q + 4 * i + 2 * b + 2)
                        tokens_out(c + 8 * i + 4 + j, c + 8 * i + 4 + j, 2 * (j % 2), 4, 512, HIDH[:, b, :, :],
                                   HIDL[:, b, :, :], i == 0 and b == 0, i == 3 and b == 1)

            for l in range(DEPTH):
                c0, g0, u0, t0, h0 = CH1 * l + MODC, GR1 * l, UC1 * l, 3 * l, 12 * l
                ts = transposes(t0, 4 * t0, YN)
                modulation(6 * l, c0 - MODC, u0, ts)
                for j in range(3):
                    group(g0 + j, c0 + 2 * j, 2 * j)
                pe.wait_ge(s_gfree, g0 + 4)
                tokens_out(c0 + 6, 6, 2, KT, 256, AH, AL, True, True)
                for j in range(2):
                    pe.wait_ge(s_ufree, u0 + j + 1)
                    features_out(c0 + 7 + j, 7 + j, 4 + j, AH, AL)
                group(g0 + 4, c0 + 9, 9)
                pe.wait_ge(s_gfree, g0 + 6)
                tokens_out(c0 + 11, 11, 2, KT, 8, AH, AL, True, True)

                pe.wait_ge(s_qsw, l + 1)
                for j in range(6):
                    pe.wait_ge(s_qtc, 6 * l + j + 1)
                    for k in range(2 if j < 5 else 1):
                        for t in range(NT):
                            h = 2 * (2 * j + k)
                            last = nc.tensor.transpose(
                                PS[:, 6 + j % 2, 256 * k + 128 * t:256 * k + 128 * t + 128],
                                QK[:, t, h:h + 2, :].rearrange("p h d -> p (h d)"), IDM)
                    last.then_inc(s_qt, 1)
                pe.wait_ge(s_qtc, 6 * l + 6 + 2)
                pe.wait_ge(s_gfree, g0 + 6 + 2)
                pe.wait_ge(s_ufree, u0 + 2 + 2)

                def scores(h):
                    r = 64 * (h % 2)
                    if h < MOBA_H:
                        q, k = QKT[r:r + 64, h // 2, :], QKT[r:r + 64, 3 + h // 2, :]
                    else:
                        kv = (h - 6) // 3
                        q = QKT[r:r + 64, 6 + (h - 6) // 2, :]
                        k = QKT[r:r + 64, 9 if kv == h % 2 else 10, :]
                    pe.wait_ge(s_sm, h0 + h + 1)
                    mm(PS[:, h % 2, 0:128], q[:, 0:128], k[:, 0:128], start=True, stop=True)
                    mm(PS[:, h % 2, 128:384], q[:, 128:256], k, start=True, stop=True).then_inc(s_s, 1)

                def turn(h):
                    pe.wait_ge(s_e, h0 + h + 1)
                    pe.wait_ge(s_pe, h0 + h + 1)
                    for j in range(3):
                        last = nc.tensor.transpose(PS[:, 2 + h % 2, 128 * j:128 * j + 128],
                                                   PM[:, h % 2, 128 * j:128 * j + 128], IDM)
                    last.then_inc(s_pt, 1)

                def values(h):
                    col = C_MV + DH * h if h < MOBA_H else C_SV + DH * ((h - 6) // 3)
                    v = Z[:, :, col:col + DH]
                    pe.wait_ge(s_pe, h0 + h + 1 + 2)
                    pe.wait_ge(s_oe, h0 + h + 1)
                    p, o = PTS[:, h % 2, :], PS[:, 4 + h % 2, :]
                    mm(o[:, 0:64], p[:, 0:128], v[:, 0, :], start=True, stop=True)
                    mm(o[:, 64:128], p[:, 128:256], v[:, 0, :], start=True, stop=False)
                    mm(o[:, 64:128], p[:, 256:384], v[:, 1, :], start=False, stop=True).then_inc(s_o, 1)

                for h in range(14):
                    if h < 12:
                        scores(h)
                    if 1 <= h <= 12:
                        turn(h - 1)
                    if h >= 2:
                        values(h - 2)

                pe.wait_ge(s_lf, l + 1)
                mm(PS[:, 6, 0:4], TRI, GT2[:, 0, :], start=True, stop=True)
                mm(PS[:, 6, 4:8], ONES, GT2[:, 0, :], start=True, stop=False)
                mm(PS[:, 6, 4:8], TRI, GT2[:, 1, :], start=False, stop=True).then_inc(s_b, 1)
                pe.wait_ge(s_dg, l + 1)
                for t in range(NT):
                    last = mm(PS[:, 6 + t, :], ONES, DG[:, t, :, :].rearrange("p h n -> p (h n)"), start=True, stop=True)
                last.then_inc(s_eb, 1)
                pe.wait_ge(s_lqk, l + 1)
                pe.wait_ge(s_oe, h0 + 12 + 2)
                for j, (t, s) in enumerate(((0, 0), (1, 0), (1, 1))):
                    for h in range(ML_H):
                        r = 64 * (h % 2)
                        o = PS[:, 2 * j + h % 2, 128 * (h // 2):128 * (h // 2) + 128]
                        last = mm(o, CV[r:r + 64, h // 2, 128 * t:128 * t + 128],
                                  CV[r:r + 64, 2 + h // 2, 128 * s:128 * s + 128], start=True, stop=True)
                last.then_inc(s_ms3, 1)
                pe.wait_ge(s_mp, l + 1)
                for j in range(3):
                    for h in range(ML_H):
                        last = nc.tensor.transpose(PS[:, 3 + j, 128 * h:128 * h + 128], ME[:, j, h, :], IDM)
                last.then_inc(s_mt, 1)
                pe.wait_ge(s_mtc, l + 1)
                pe.wait_ge(s_v65, l + 1)
                for h in range(ML_H):
                    o0, o1 = PS[:, 6, 65 * h:65 * h + 65], PS[:, 7, 65 * h:65 * h + 65]
                    mm(o0, PTM[:, 0, h, :], V65[:, 0, h, :], start=True, stop=True)
                    mm(o1, PTM[:, 1, h, :], V65[:, 0, h, :], start=True, stop=False)
                    last = mm(o1, PTM[:, 2, h, :], V65[:, 1, h, :], start=False, stop=True)
                last.then_inc(s_mo, 1)

                ts = transposes(t0 + 1, 4 * t0 + 4, YN)
                modulation(6 * l + 2, c0 + 12, u0 + 2, ts)
                for j in range(2):
                    group(g0 + 6 + j, c0 + MODC + 12 + 2 * j, 12 + 2 * j)
                ts = transposes(t0 + 2, 4 * t0 + 8, YN)
                modulation(6 * l + 4, c0 + MODC + 16, u0 + 2, ts)
                pe.wait_ge(s_gfree, g0 + 8 + 2)

                mlp(l, c0 + 2 * MODC + 16, u0 + 2)

            def turn_heads(n, steps):
                for j, (h, bank) in enumerate(steps):
                    pe.wait_ge(s_qc2, n + j + (2 if len(steps) == 1 or j == 2 else 1))
                    for k in range(2):
                        for t in range(NT):
                            last = nc.tensor.transpose(PS[:, bank, 256 * k + 128 * t:256 * k + 128 * t + 128],
                                                       QK2[:, t, h + 2 * k:h + 2 * k + 2, :].rearrange("p h d -> p (h d)"),
                                                       IDM)
                    last.then_inc(s_qt2, 1)

            def gate_rows(n):
                pe.wait_ge(s_dgb, n + 1)
                for j in range(2):
                    last = mm(PS[:, 6 + j, :], ONES, DGB[:, 4 * j:4 * j + 4, :].rearrange("p k n -> p (k n)"),
                              start=True, stop=True)
                last.then_inc(s_gt, 1)

            for q in PASSES:
                c0, g0 = q.c_in, q.g
                qt0 = 3 * q.p + (1 if q.mini else 0)
                if q.mini:
                    split_done(transposes(q.src - 1, q.t - 4, YN))
                    pe.wait_ge(s_gfree, g0 - 1 + 2)
                    tokens_out(c0 - 1, c0 - 1, 2, KT, 256, AH, AL, True, True)
                    pe.wait_ge(s_qw2, q.qk)
                    turn_heads(qt0 - 1, ((8, 6),))
                ts = transposes(q.src, q.t, YN)
                if q.mod:
                    modulation(q.mg, q.c, q.u, ts)
                split_done(ts)
                for k in range(3):
                    pe.wait_ge(s_ufree, q.u + k + 1)
                    features_out(c0 + k, c0 + k, 4 + (q.u + k) % 2, AH, AL)
                pe.wait_ge(s_gfree, g0 + 1)
                tokens_out(c0 + 3, c0 + 3, 0, KT, 256, AH, AL, True, True)
                pe.wait_ge(s_gfree, g0 + 2)
                for h in range(2):
                    half_group(c0 + 4 + h, c0 + 4 + h, 1, h)
                pe.wait_ge(s_gfree, g0 + 3)
                tokens_out(c0 + 6, c0 + 6, 0, KT, 256, AH, AL, True, True)
                for f in range(2):
                    for b in range(2):
                        for t in range(NT):
                            tab = CT[:, K_CL + 2 * S * f + S * t:K_CL + 2 * S * f + S * t + S]
                            last = mm(PS[:, 6 + f, 256 * b:256 * b + 256], ZN[:, t, N_F + 128 * b:N_F + 128 * b + 128],
                                      tab, start=t == 0, stop=t == NT - 1)
                last.then_inc(s_fa, 1)
                for k in range(7, 19):
                    if k % 2:
                        pe.wait_ge(s_gfree, g0 + 3 + (k - 7) // 2 + 2)
                    half_group(c0 + k, c0 + k, 0, (k - 7) % 2)
                    if k == 7:
                        pe.wait_ge(s_fac, q.p + 1)
                        for b in range(2):
                            for f in range(2):
                                last = mm(PS[:, 6, 256 * b:256 * b + 256], CT[:, K_BD + 128 * f:K_BD + 128 * f + 128],
                                          A12[:, f, b, :], start=f == 0, stop=f == 1)
                        last.then_inc(s_fy, 1)
                    if k == 9:
                        pe.wait_ge(s_qw2, q.qk + 1)
                        pe.wait_ge(s_fyc, q.p + 1)
                        turn_heads(qt0, ((0, 6), (4, 7), (8, 6)))
                        pe.wait_ge(s_qc2, qt0 + 3 + 2)
                    n = 256 if q.stream else 512
                    for v in units(k):
                        if v < 16:
                            h, t = divmod(v, 2)
                            r = 64 * (h % 2)
                            pe.wait_ge(s_e2, q.att + v + 1)
                            mm(PS[:, 4 + v % 2, 0:n], QT2[r:r + 64, h // 2, 128 * t:128 * t + 128],
                               KTB[r:r + 64, 0 if h // 4 == h % 2 else 1, 2 * S - n if q.stream else 0:2 * S],
                               start=True, stop=True).then_inc(s_s2, 1)
                        if 2 <= v < 18:
                            pe.wait_ge(s_e2, q.att + v - 2 + 1 + 2)
                            pe.wait_ge(s_p2, q.att + v - 2 + 1)
                            for j in range(n // 128):
                                last = nc.tensor.transpose(PS[:, 6 + v % 2, 128 * j:128 * j + 128],
                                                           PM[:, v % 2, 128 * j:128 * j + 128], IDM)
                            last.then_inc(s_t2, 1)
                        if v >= 4:
                            h, t = divmod(v - 4, 2)
                            pe.wait_ge(s_p2, q.att + v - 4 + 1 + 2)
                            pe.wait_ge(s_oe2, q.att + v - 4 + 1)
                            for j in range(n // 128):
                                last = mm(PS[:, 2 + v % 2, 0:DH], PTS[:, v % 2, 128 * j:128 * j + 128],
                                          VB[:, j + 2 * q.stream, DH * (h // 4):DH * (h // 4) + DH],
                                          start=j == 0, stop=j == n // 128 - 1)
                            last.then_inc(s_o2, 1)
                split_done(transposes(q.src + 1, q.t + 4, YA, (2, 3)))
                pe.wait_ge(s_yl, q.p + 1)
                for b in range(2):
                    c = c0 + 19 + b
                    arrived(c)
                    hi, lo = slot(c, 2, D)
                    for half in range(2):
                        pe.wait_ge(s_gfree, g0 + 9 + 2 * b + half + (2 if b == 0 and half == 0 else 1))
                        for t in range(NT):
                            for j in range(2):
                                o, cols = PS[:, 2 * half + t, :], slice(512 * half, 512 * half + 512)
                                th, tl = (w[:, 2 * b + j, 128 * t:128 * t + 128] for w in (AH, AL))
                                mm(o, th, hi[:, j, cols], start=j == 0, stop=False)
                                mm(o, th, lo[:, j, cols], start=False, stop=False)
                                last = mm(o, tl, hi[:, j, cols], start=False, stop=j == 1)
                        last.then_inc(s_used if half else s_bg, 1)
                for half in range(2):
                    pe.wait_ge(s_gfree, g0 + 13 + half + 1)
                    c = c0 + 21 + half
                    tokens_out(c, c, 2 * half, 4, 512, AH[:, 4:8, :], AL[:, 4:8, :], True, True)
                ts = transposes(q.src + 2, q.t + 6, M2)
                if q.mod:
                    modulation(q.mg + 2, q.c_br + 4, q.u + 3, ts)
                split_done(ts)
                gate_rows(2 * q.p)
                for half in range(2):
                    pe.wait_ge(s_gfree, g0 + 15 + half + 1)
                    for h in range(2):
                        half_group(q.c_o + 2 * half + h, q.c_o + 2 * half + h, half, h)
                ts = transposes(q.src + 3, q.t + 10, YN)
                if q.mod:
                    modulation(q.mg + 4, q.c_o + 4, q.u + 3, ts)
                split_done(ts)
                gate_rows(2 * q.p + 1)
                pe.wait_ge(s_gfree, g0 + 17 + 2)
                mlp(q.mlp, q.c_mlp, q.u + 3)


N_CONST = 22
INPUTS = ["x", "ln1", "w_in", "conv_w", "conv_b", "igate_b", "fgate_b", "mlstm_norm", "moba_q_norm", "moba_k_norm",
          "swa_q_norm", "swa_k_norm", "swa_sinks", "w_out", "ln2", "w_up", "w_down", "c_2", "ctx_2", "c_ctx_2",
          "w_mod_2", "b_mod_2", "g_norm1_2", "g_norm2_2", "w_in_2", "w_conv_2", "g_q_2", "g_k_2", "w_conv_out_2",
          "w_four_out_2", "w_attn_out_2", "w_o_2", "w_ff1_2", "w_ff2_2"]


def kernel(**inputs):
    import concourse.bacc as bacc
    from concourse.bass_utils import run_bass_kernel_spmd

    nc = bacc.Bacc("TRN2", target_bir_lowering=False, num_devices=1)
    arrays, args = {}, {}
    for name in INPUTS:
        v = np.ascontiguousarray(inputs[name])
        arrays[f"in_{name}"] = v
        args[name] = nc.dram_tensor(f"in_{name}", v.shape, mybir.dt.from_np(v.dtype), kind="ExternalInput").ap()
    table = shape_constants()
    arrays["constants"] = table
    args["constants"] = nc.dram_tensor("constants", table.shape, F32, kind="ExternalInput").ap()
    pairs = np.tile(np.eye(2, dtype=np.float32), (2, 1))
    arrays["selector"] = pairs
    args["selector"] = nc.dram_tensor("selector", pairs.shape, F32, kind="ExternalInput").ap()
    out = nc.dram_tensor("out", (1, S, D), F32, kind="ExternalOutput").ap()
    build(nc, args, out)
    return run_bass_kernel_spmd(nc, [arrays], core_ids=[0]).results[0]["out"]
```

```python
from contextlib import ExitStack

import numpy as np

import concourse.bass as bass
from concourse import mybir

F32 = mybir.dt.float32
F32R = mybir.dt.float32r
ALU = mybir.AluOpType
ACT = mybir.ActivationFunctionType
AX_X = mybir.AxisListType.X

P = 128
D = 1024
KT = D // P
S = 256
NT = S // P
DEPTH = 2
DH = 64
FF = 4 * D
EPS = 1e-6
ISC = DH ** -0.5

MOBA_H, ML_H, SWA_H, SWA_KV = 6, 4, 6, 2
C_MQ, C_MV, C_SQ, C_SV = 0, 2 * MOBA_H * DH, 3 * MOBA_H * DH, 3 * MOBA_H * DH + (SWA_H + SWA_KV) * DH
C_LQK = C_SV + SWA_KV * DH
C_LV = C_LQK + 2 * ML_H * DH
C_GATE = C_LV + 2 * ML_H * DH
N_IN1 = C_GATE + 2 * ML_H
Z_LV = C_LQK
Z_LO = Z_LV + ML_H * DH
Z_GATE = Z_LO + ML_H * DH
ZW = Z_GATE + 2 * ML_H
NQK = 2 * MOBA_H + SWA_H + SWA_KV
NSL = NQK + SWA_KV

B_X3, B_F, B_Q, B_K, B_G = 0, 768, 1024, 1536, 1792
N_IN2 = B_G + 3 * D
QH, KVH = 8, 2

RAW_N, HL_N = 2, 4
CW = 2048
SPLIT_LEAD = 3
MODC = 4
N1 = 12 + 4 + 32
GR1 = 10
UC1 = 18
CH2 = 59
GR2 = 19
UC2 = 19

N_F, N_Q, N_K, N_V = 0, 256, 768, 896
M_SH, M_SC, M_GT = (0, 24), (8, 32), (16, 40)


class Slot:
    made = 0

    def __init__(self, c, here):
        self.c, self.here, self.n = c, here, MODC if here else 0
        self.g = 2 * Slot.made
        Slot.made += here
        self.next = c + self.n


class Layer:

    def __init__(self, l):
        c = LAYERS[-1].end if l else 0
        self.m_in = Slot(c, l > 0)
        self.c_in = self.m_in.next
        self.m_o = Slot(self.c_in + 12, True)
        self.c_o = self.m_o.next
        self.m_mlp = Slot(self.c_o + 4, True)
        self.c_mlp = self.m_mlp.next
        self.end = self.c_mlp + 32


LAYERS = []
for _l in range(DEPTH):
    LAYERS.append(Layer(_l))


class Pass:

    def __init__(self, p):
        self.p, self.layer, self.stream = p, (0, 0, 1)[p], (1, 0, 0)[p]
        mini = p == 2
        self.mini = mini
        self.c = (PASSES[-1].end if p else LAYERS[-1].end) + mini
        self.m_in = Slot(self.c, True)
        self.c_in = self.m_in.next
        self.m_o = Slot(self.c_in + 23, not mini)
        self.c_o = self.m_o.next
        self.m_mlp = Slot(self.c_o + 4, not mini)
        self.c_mlp = self.m_mlp.next
        self.end = self.c_mlp + 32
        self.g = GR1 * DEPTH + GR2 * p + mini
        self.u = UC1 * DEPTH + UC2 * p
        self.t = 12 * DEPTH + 14 * p + 4 * mini
        self.src = 3 * DEPTH + 4 * p + mini
        self.norm = 2 * DEPTH + 2 * p + mini
        self.pow = 4 * DEPTH + 3 * p + 2 * mini
        self.mlp = DEPTH + p
        self.qk = p + mini
        self.att = 16 * p


PASSES = []
for _p in range(3):
    PASSES.append(Pass(_p))
assert Slot.made == DEPTH * 6
NO_SLOT = Slot(0, False)
NARROW = [k.c_in + 11 for k in LAYERS]

K_ID, K_ONE, K_TRI = 0, 128, 256
K_M = 384
K_R1 = K_M + 512
K_R2 = K_R1 + 128
K_CL = K_R2 + 128
K_BD = K_CL + 4 * S
K_W = K_BD + 256


def shape_constants():
    t = np.zeros((P, K_W), np.float32)
    i = np.arange(P)
    t[:, K_ID:K_ID + P] = np.eye(P)
    t[:, K_ONE:K_ONE + P] = 1.0
    t[:, K_TRI:K_TRI + P] = i[:, None] <= i[None, :]
    low = np.float32(-1e30)
    causal = np.where(i[None, :] > i[:, None], low, 0)
    window = np.where(i[None, :] <= i[:, None], low, 0)
    t[:, K_M + 128:K_M + 256] = causal
    t[:, K_M + 256:K_M + 384] = window
    t[:, K_M + 384:K_M + 512] = causal
    inv = (np.float32(10000.0) ** (-np.arange(0, DH, 2, dtype=np.float32) / np.float32(DH))).astype(np.float32)
    ang = np.arange(S, dtype=np.float32)[:, None] * inv[None, :]
    inv2 = (np.float32(10000.0) ** (-np.arange(16, dtype=np.float32) / np.float32(16))).astype(np.float32)
    rows = np.repeat(np.arange(S // 64, dtype=np.float32)[:, None] * inv2, 64, axis=0)
    cols = np.tile(np.arange(64, dtype=np.float32)[:, None] * inv2, (S // 64, 1))
    ang2 = np.concatenate([rows, cols], axis=1)
    for at, a in ((K_R1, ang), (K_R2, ang2)):
        for f, fn in enumerate((np.cos, np.sin)):
            v = fn(a.astype(np.float32)).astype(np.float32).reshape(NT, P, 32)
            for n in range(NT):
                t[:, at + f * 64 + n * 32:at + f * 64 + n * 32 + 32] = v[n]
    k = np.arange(S)
    w = 2 * np.pi * ((k[:, None] * k[None, :]) % S) / S
    for f, fn in enumerate((np.cos, np.sin)):
        v = (fn(w) / 16.0).astype(np.float32).reshape(NT, P, S)
        for n in range(NT):
            t[:, K_CL + f * 2 * S + n * S:K_CL + f * 2 * S + (n + 1) * S] = v[n]
    k = np.arange(64)
    w = 2 * np.pi * ((k[:, None] * k[None, :]) % 64) / 64
    for f, v in enumerate((np.cos(w) / 8.0, -np.sin(w) / 8.0)):
        for b in range(2):
            t[b * 64:b * 64 + 64, K_BD + f * 128 + b * 64:K_BD + f * 128 + b * 64 + 64] = v
    return t


def build(nc, a, out):
    with ExitStack() as ctx:
        at = [16512]

        def sb(name, shape, dt=F32, where=None):
            size = 4 * int(np.prod(shape[1:]))
            offset = at[0] if where is None else where
            if where is None:
                at[0] += (size + 31) // 32 * 32
            return nc.alloc_sbuf_tensor_at(name, shape, dt, offset=offset)

        def sem(name):
            return ctx.enter_context(nc.semaphore(name))

        RAW = sb("RAW", [P, RAW_N, CW])
        HI = sb("HI", [P, HL_N, CW], F32R)
        LO = sb("LO", [P, HL_N, CW], F32R)
        X = sb("X", [P, NT, D])
        AH = sb("AH", [P, KT, S], F32R)
        AL = sb("AL", [P, KT, S], F32R)
        at_yn = at[0]
        YN = sb("YN", [P, NT, D])
        at_z = at[0]
        Z = sb("Z", [P, NT, ZW])
        QKT = sb("QKT", [P, NSL // 2, S])
        at[0] = at_z + 32768
        at_pm = at[0]
        PM = sb("PM", [P, 2, 512])
        at_pt = at[0]
        PTS = sb("PTS", [P, 2, 512])
        CT = sb("CT", [P, K_W])
        PAR = sb("PAR", [P, 256])
        MOD = sb("MOD", [P, DEPTH, 48, 2])
        GN = sb("GN", [P, DEPTH, 4, DH])
        MN = sb("MN", [P, DEPTH, ML_H * DH])
        IFB = sb("IFB", [P, DEPTH, 2 * ML_H])
        SK = sb("SK", [P, DEPTH, SWA_H])
        NSK = sb("NSK", [P, DEPTH, SWA_H])
        GQ2 = sb("GQ2", [P, DEPTH, 2, DH])
        CS = sb("CS", [P, 2, KT])
        C4 = sb("C4", [P, KT, 4], F32R)
        SEL = sb("SEL", [4, 2])
        SGC = sb("SGC", [P, 16])
        SSQ = sb("SSQ", [P, 2])
        MS = sb("MS", [P, 64])
        RS = sb("RS", [P, 64])
        NHALF = sb("NHALF", [P, 64])
        MX = sb("MX", [P, 2, 2])
        NB = sb("NB", [P, MOBA_H + SWA_H, 2])
        SUM = sb("SUM", [P, MOBA_H + SWA_H, 2])
        SKE = sb("SKE", [P, SWA_H, 2])
        RIN = sb("RIN", [P, MOBA_H + SWA_H, 2])
        G8 = sb("G8", [P, NT, 8])
        GT1 = sb("GT1", [P, NT, 4])
        GT2 = sb("GT2", [P, NT, 4])
        ES = sb("ES", [P, NT, 4])
        BS = sb("BS", [P, NT, 4])
        RMX = sb("RMX", [P, 3, 4])
        RR = sb("RR", [P, NT, 4])
        DEN = sb("DEN", [P, NT, 4])
        SCL = sb("SCL", [P, DEPTH, 2, KT, 2])
        NM2 = sb("NM2", [P, QH, 2])
        SM2 = sb("SM2", [P, QH, 2])
        RN2 = sb("RN2", [P, QH, 2])
        at_scratch = at[0]
        QK = sb("QK", [P, NT, NSL, DH])
        XP = sb("XP", [P, 4, S + 3])
        CV = sb("CV", [P, 4, S])
        ME = sb("ME", [P, 3, ML_H, P])
        at_ptm = at[0]
        PTM = sb("PTM", [P, 3, ML_H, P])
        V65 = sb("V65", [P, NT, ML_H, DH + 1])
        HM = sb("HM", [P, NT, ML_H * DH])
        PR0 = sb("PR0", [P, P], F32, at_yn)
        PR1 = sb("PR1", [P, P], F32, at_yn + 512)
        ROWS = sb("ROWS", [P, 2, 512], F32, at_yn)
        TMP = sb("TMP", [P, 2, 512], F32, at_pm)
        U2 = sb("U2", [P, 2, 512], F32, at_pm)
        RL = sb("RL", [P, 2, 512], F32, at_pt)
        DG = sb("DG", [P, NT, ML_H, P], F32, at_ptm)
        SG = sb("SG", [P, 4, S], F32, at_ptm)
        SO = sb("SO", [P, NT, ML_H * DH], F32, at_ptm)
        HIDH = sb("HIDH", [P, 2, 4, S], F32R, at_z)
        HIDL = sb("HIDL", [P, 2, 4, S], F32R, at_z + 8192)
        GA = sb("GA", [P, NT, 3 * D], F32, at_z)
        ZN = sb("ZN", [P, NT, 1024], F32, at_z + 24576)
        M2 = sb("M2", [P, NT, D], F32, at_z + 24576)
        A12 = sb("A12", [P, 2, 2, S], F32, at_yn)
        YA = sb("YA", [P, NT, 512], F32, at_yn + 4096)
        UB = sb("UB", [P, 3, 2, S], F32, at_pm)
        TM = sb("TM", [P, 2, 512], F32, at_pt)
        DGB = sb("DGB", [P, 8, P], F32, at_pt)
        at_end = at[0]
        at[0] = at_scratch
        CTX = sb("CTX", [P, NT, D])
        QK2 = sb("QK2", [P, NT, 12, DH])
        QT2 = sb("QT2", [P, 4, S])
        KTB = sb("KTB", [P, 2, 2 * S])
        VB = sb("VB", [P, 2 * NT, P])
        GTB = sb("GTB", [P, D])
        CXP = sb("CXP", [P, 2, S + 2])
        YC = sb("YC", [P, 2, S])
        YF = sb("YF", [P, 2, S])
        at[0] = max(at_end, at[0])
        assert at[0] <= nc.sbuf_usable_end, at[0]
        IDM = CT[:, K_ID:K_ID + P]
        ONES = CT[:, K_ONE:K_ONE + P]
        TRI = CT[:, K_TRI:K_TRI + P]

        PS = ctx.enter_context(nc.psum_tensor("PS", [P, 8, 512], F32))

        s_cst = sem("constants_loaded")
        s_xin = sem("x_loaded")
        s_raw = [sem(f"raw_loaded_{i}") for i in range(RAW_N)]
        s_hi = sem("chunk_high_done")
        s_lo = sem("chunk_split_done")
        s_used = sem("chunk_used")
        s_gfree = sem("group_evacuated")
        s_ufree = sem("ubank_evacuated")
        s_mrow = sem("mod_rows_copied")
        s_mcol = sem("mod_columns")
        s_modc = sem("mod_copied")
        s_c4 = sem("silu_c_split")
        s_sel = sem("selector_loaded")
        s_init = sem("pool_constants")
        s_par = sem("params_transposed")
        s_parc = sem("params_copied")
        s_cs = sem("silu_c")
        s_av = sem("act_chain")
        s_dv = sem("dve_chain")
        s_ss = sem("sum_squares")
        s_ms = sem("mean_squares")
        s_rs = sem("rstd_done")
        s_src = sem("transpose_source")
        s_tp = sem("transposed")
        s_thi = sem("activation_high")
        s_tlo = sem("activation_low")
        s_sq = sem("qk_squares")
        s_qk = sem("qk_rotated")
        s_qsw = sem("qk_swapped_copied")
        s_qt = sem("qk_transposed")
        s_qtc = sem("qk_transposed_copied")
        s_s = sem("scores")
        s_sm = sem("scores_masked")
        s_nb = sem("row_max")
        s_e = sem("exp_done")
        s_pt = sem("probs_transposed")
        s_pe = sem("probs_copied")
        s_o = sem("head_output")
        s_oe = sem("head_output_copied")
        s_ske = sem("sink_in")
        s_sko = sem("sink_exp")
        s_cv = sem("conv_done")
        s_sg = sem("conv_sigmoid")
        s_lqk = sem("mlstm_qk")
        s_ga = sem("gate_abs")
        s_gl = sem("gate_log")
        s_lf = sem("log_forget")
        s_b = sem("cum_forget")
        s_dg = sem("diag_e")
        s_eb = sem("e_rows")
        s_me = sem("mlstm_exponent")
        s_mex = sem("mlstm_weights")
        s_mem = sem("mlstm_stabilizer")
        s_exm = sem("mlstm_floor")
        s_ms3 = sem("mlstm_scores")
        s_mp = sem("mlstm_probs")
        s_mt = sem("mlstm_transposed")
        s_mtc = sem("mlstm_transposed_copied")
        s_mo = sem("mlstm_output")
        s_h = sem("mlstm_h")
        s_hsq = sem("mlstm_h_squares")
        s_v65 = sem("mlstm_values")
        s_so = sem("output_gate")
        s_rl = sem("hidden_relu")
        s_u2 = sem("hidden_square")
        s_hh = sem("hidden_high")
        s_hl = sem("hidden_low")
        s_out = sem("result_written")
        s_ctx = sem("ctx_loaded")
        s_scl = sem("norm_scales")
        s_pad = sem("conv_pads")
        s_sq2 = sem("qk2_squares")
        s_qk2 = sem("qk2_normed")
        s_qw2 = sem("qk2_swapped_copied")
        s_qt2 = sem("qk2_transposed")
        s_qc2 = sem("qk2_transposed_copied")
        s_fa = sem("dft_tokens")
        s_fac = sem("dft_tokens_copied")
        s_fy = sem("dft_channels")
        s_fyc = sem("fourier_branch")
        s_yc = sem("conv_branch")
        s_yh = sem("branches_high")
        s_yl = sem("branches_low")
        s_s2 = sem("scores2")
        s_n2 = sem("row_max2")
        s_e2 = sem("exp2_done")
        s_t2 = sem("probs2_transposed")
        s_p2 = sem("probs2_copied")
        s_o2 = sem("head2_output")
        s_oe2 = sem("head2_output_copied")
        s_bg = sem("branch_half_done")
        s_dgb = sem("gate_diagonals")
        s_gt = sem("gate_rows")
        s_gtc = sem("gate_rows_copied")

        def tiled(w, l, r, kt, c, n):
            return w[l, r:r + kt * P, c:c + n].rearrange("(a p) n -> p a n", p=P)

        def mlp_chunks(up, down, l):
            for i in range(4):
                for j in (2 * i, 2 * i + 1):
                    for h in range(2):
                        yield tiled(up, l, 0, KT, 512 * j + 256 * h, 256), KT, 256
                for j in (2 * i, 2 * i + 1):
                    for h in range(2):
                        yield tiled(down, l, 512 * j, 4, 512 * h, 512), 4, 512

        def halves(w, l, c):
            for h in range(2):
                yield tiled(w, l, 512 * h, 4, c, 512), 4, 512

        def mod_chunks(m):
            if m.here:
                for j in (m.g, m.g + 1):
                    yield from halves(a["w_mod_2"], j // 12, 512 * (j % 12))

        def chunks1(l):
            w = a["w_in"]
            yield from mod_chunks(LAYERS[l].m_in)
            for c in (0, 512, 1024):
                yield from halves(w, l, c)
            yield tiled(w, l, 0, KT, 1536, 256), KT, 256
            for c in (C_LQK, C_LQK + 256):
                yield tiled(w, l, 0, KT, c, 256), KT, 256
            yield from halves(w, l, C_LV)
            yield tiled(w, l, 0, KT, C_GATE, 8), KT, 8
            yield from mod_chunks(LAYERS[l].m_o)
            for c in (0, 512):
                yield from halves(a["w_out"], l, c)
            yield from mod_chunks(LAYERS[l].m_mlp)
            yield from mlp_chunks(a["w_up"], a["w_down"], l)

        def chunk_words(c):
            return KT * 8 if c in NARROW else CW

        def chunks2(q):
            w, l = a["w_in_2"], q.layer
            if q.mini:
                yield tiled(w, l, 0, KT, B_K, 256), KT, 256
            yield from mod_chunks(q.m_in)
            for c in (0, 256, 512, B_F):
                yield tiled(w, l, 0, KT, c, 256), KT, 256
            yield from halves(w, l, B_Q)
            yield tiled(w, l, 0, KT, B_K, 256), KT, 256
            for j in range(6):
                yield from halves(w, l, B_G + 512 * j)
            for name in ("w_conv_out_2", "w_four_out_2"):
                yield tiled(a[name], l, 0, 2, 0, D), 2, D
            for j in range(2):
                yield tiled(a["w_attn_out_2"], l, 0, 4, 512 * j, 512), 4, 512
            yield from mod_chunks(q.m_o)
            for j in range(2):
                yield from halves(a["w_o_2"], l, 512 * j)
            yield from mod_chunks(q.m_mlp)
            yield from mlp_chunks(a["w_ff1_2"], a["w_ff2_2"], l)

        LP = PASSES[-1]
        NCH = LP.end

        def units(k):
            return range(2 * (k - 10), 2 * (k - 10) + (4 if k == 18 else 2)) if k >= 10 else ()

        block = ctx.enter_context(nc.Block())

        @block.sync
        def _(sp):
            sp.dma_start(X[:, :, :], a["x"][0].rearrange("(t p) d -> p t d", p=P)).then_inc(s_xin, 16)

            def load(c, src, kt, n):
                sp.wait_ge(s_lo, c + 1)
                dst = RAW[:, c % RAW_N, 0:kt * n].rearrange("p (a n) -> p a n", a=kt)
                sp.dma_start(dst, src).then_inc(s_raw[c % RAW_N], 16)

            for l in range(DEPTH):
                for k, (src, kt, n) in enumerate(chunks1(l)):
                    c = LAYERS[l].m_in.c + k
                    load(c, src, kt, n)
                    if c == LAYERS[-1].c_mlp:
                        sp.wait_ge(s_src, 3 * l + 2)
                        sp.dma_start(CTX[:, :, :], a["ctx_2"][0].rearrange("(t p) d -> p t d", p=P)).then_inc(s_ctx, 16)
            for q in PASSES:
                for k, (src, kt, n) in enumerate(chunks2(q)):
                    c = q.c - q.mini + k
                    load(c, src, kt, n)
            sp.wait_ge(s_out, 16)

        @block.gpsimd
        def _(pool):
            nc.gpsimd.memset(NHALF[:, :], -0.5)
            nc.gpsimd.memset(XP[:, :, 0:3], 0.0)
            nc.gpsimd.memset(V65[:, :, :, DH:DH + 1], 1.0).then_inc(s_init, 1)
            pool.wait_ge(s_init, 1)

            def rsqrt(n, width):
                pool.wait_ge(s_ms, n + 1)
                nc.gpsimd.tensor_tensor(RS[:, 0:width], MS[:, 0:width], NHALF[:, 0:width], ALU.pow).then_inc(s_rs, 1)

            for l in range(DEPTH):
                for j, width in enumerate((2, 2 * NQK, 8, 2)):
                    rsqrt(4 * l + j, width)
            pool.wait_ge(s_src, 3 * DEPTH - 1)
            nc.gpsimd.memset(CXP[:, :, 0:1], 0.0)
            nc.gpsimd.memset(CXP[:, :, S + 1:S + 2], 0.0).then_inc(s_pad, 1)
            for q in PASSES:
                if q.mini:
                    rsqrt(q.pow - 2, 2)
                    rsqrt(q.pow - 1, 2 * KVH)
                for j, width in enumerate((2, 2 * (QH + KVH), 2)):
                    rsqrt(q.pow + j, width)

        @block.scalar
        def _(act):
            def cast(dst, src):
                return nc.scalar.copy(dst, src)

            chain = [0]

            def link(ins):
                chain[0] += 1
                ins.then_inc(s_av, 1)
                act.wait_ge(s_av, chain[0])

            n_cst = [0]

            def const(dst, src):
                act.dma_start(dst, src).then_inc(s_cst, 16)
                n_cst[0] += 1

            const(CT[:, :], a["constants"])
            const(SEL[:, :], a["selector"])
            for name, row, n in (("ln1", 0, 16), ("ln2", 16, 16), ("g_norm1_2", 32, 16), ("g_norm2_2", 48, 16)):
                const(PR0[row:row + n, :], a[name].rearrange("l (k p) -> (l k) p", p=P))
            const(PR0[64:72, :], a["c_2"].rearrange("l (k p) -> (l k) p", p=P))
            const(PR0[72:80, :], a["c_ctx_2"].rearrange("(k p) -> k p", p=P))
            const(PR0[80:112, :], a["conv_w"].rearrange("l j (k p) -> (l j k) p", p=P))
            const(PR0[112:120, :], a["conv_b"].rearrange("l (k p) -> (l k) p", p=P))
            const(PR1[0:96, :], a["b_mod_2"].rearrange("l (k p) -> (l k) p", p=P))
            const(PR1[96:108, :], a["w_conv_2"].rearrange("l j (k p) -> (l j k) p", p=P))

            def rows(dst, src):
                const(dst, src.partition_broadcast(P))

            for i, name in enumerate(("moba_q_norm", "moba_k_norm", "swa_q_norm", "swa_k_norm")):
                rows(GN[:, :, i, :], a[name])
            rows(MN[:, :, :], a["mlstm_norm"].rearrange("l h d -> l (h d)"))
            rows(IFB[:, :, 0:4], a["igate_b"])
            rows(IFB[:, :, 4:8], a["fgate_b"])
            rows(SK[:, :, :], a["swa_sinks"])
            for i, name in enumerate(("g_q_2", "g_k_2")):
                rows(GQ2[:, :, i, :], a[name])
            assert n_cst[0] == N_CONST

            act.wait_ge(s_par, 1)
            cast(PAR[:, 0:120], PS[:, 6, 0:120])
            cast(PAR[:, 128:236], PS[:, 7, 0:108]).then_inc(s_parc, 1)
            act.wait_ge(s_parc, 1)
            nc.scalar.activation(SGC[:, :], PAR[:, 64:80], ACT.Sigmoid).then_inc(s_cs, 1)
            act.wait_ge(s_cs, 2)
            cast(C4[:, :, 0:2], CS[:, :, :].rearrange("p s k -> p k s")).then_inc(s_c4, 1)

            def split(c):
                act.wait_ge(s_raw[c % RAW_N], 16 * (c // RAW_N + 1))
                act.wait_ge(s_used, c + 1)
                n = chunk_words(c)
                cast(HI[:, c % HL_N, 0:n], RAW[:, c % RAW_N, 0:n]).then_inc(s_hi, 1)

            def ahead(c):
                if c + SPLIT_LEAD < NCH:
                    split(c + SPLIT_LEAD)

            def sum_squares(src):
                for t in range(NT):
                    last = nc.scalar.activation(YN[:, t, :], src[:, t, :], ACT.Square, accum_out=SSQ[:, t:t + 1])
                last.then_inc(s_ss, 1)

            def high(n, scale=None, shift=None, steps=range(4)):
                for s in steps:
                    act.wait_ge(s_tp, n + s - steps[0] + 1)
                    dst = AH[:, 2 * s:2 * s + 2, :].rearrange("p a n -> p (a n)")
                    if scale is None:
                        cast(dst, PS[:, 6 + s % 2, :]).then_inc(s_thi, 1)
                        continue
                    for j in range(2):
                        last = nc.scalar.activation(TMP[:, s % 2, 256 * j:256 * j + 256],
                                                    PS[:, 6 + s % 2, 256 * j:256 * j + 256], ACT.Identity,
                                                    scale=scale(2 * s + j),
                                                    bias=0.0 if shift is None else shift(2 * s + j))
                    link(last)
                    cast(dst, TMP[:, s % 2, :]).then_inc(s_thi, 1)

            def copy_group(pair, c, dst, n):
                act.wait_ge(s_used, c + 1 + HL_N)
                for t in range(NT):
                    last = cast(dst[:, t, :], PS[:, 2 * pair + t, 0:n])
                last.then_inc(s_gfree, 1)

            def spare(m, j):
                if m.here:
                    ahead(m.c + j)

            def rows_out(m, banks):
                if m.here:
                    for j in range(2):
                        act.wait_ge(s_used, m.c + 2 * j + 2 + HL_N)
                        cast(ROWS[0:4, j, :], PS[0:4, banks[j], :]).then_inc(s_mrow, 1)
                    ahead(m.c + 2)
                    ahead(m.c + 3)

            def mlp(q, c, u):
                for i in range(4):
                    for j in range(8):
                        ahead(c + 8 * i + j)
                        if j < 4:
                            act.wait_ge(s_used, c + 8 * i + j + 1 + HL_N)
                            nc.scalar.activation(RL[:, j % 2, :], PS[:, 4 + (u + j) % 2, :], ACT.Relu).then_inc(s_rl, 1)
                            act.wait_ge(s_rl, 16 * q + 4 * i + j + 1)
                            nc.scalar.activation(HIDH[:, j // 2, 2 * (j % 2):2 * (j % 2) + 2, :].rearrange("p a n -> p (a n)"),
                                                 RL[:, j % 2, :], ACT.Square).then_inc(s_hh, 1)

            for c in range(SPLIT_LEAD):
                split(c)

            for l in range(DEPTH):
                L = LAYERS[l]
                c0, g0, u0, t0, h0 = L.c_in, GR1 * l, UC1 * l, 3 * l, 12 * l
                spare(L.m_in, 0)
                if l == 0:
                    act.wait_ge(s_xin, 16)
                else:
                    act.wait_ge(s_gfree, g0 + 2)
                sum_squares(X)
                spare(L.m_in, 1)
                high(4 * t0, lambda k: PAR[:, 8 * l + k:8 * l + k + 1])
                rows_out(L.m_in, (4, 5))
                for k in range(12):
                    ahead(c0 + k)
                    if k in (1, 3, 5):
                        copy_group(k // 2 % 2, c0 + k, Z[:, :, 512 * (k // 2):512 * (k // 2) + 512], 512)
                    if k == 3:
                        act.wait_ge(s_gfree, g0 + 4)
                        nc.scalar.activation(QK[:, :, 0:12, :].rearrange("p t h d -> p t (h d)"),
                                             Z[:, :, 0:768], ACT.Square)
                    if k == 6:
                        copy_group(1, c0 + k, Z[:, :, 1536:1792], 256)
                        act.wait_ge(s_gfree, g0 + 6)
                        nc.scalar.activation(QK[:, :, 12:NQK, :].rearrange("p t h d -> p t (h d)"),
                                             Z[:, :, C_SQ:C_SV], ACT.Square).then_inc(s_sq, 1)
                    if k in (7, 8):
                        act.wait_ge(s_used, c0 + k + 1 + HL_N)
                        j = k - 7
                        cast(XP[:, 2 * j:2 * j + 2, 3:3 + S],
                             PS[:, 4 + j, :].rearrange("p (a n) -> p a n", a=2)).then_inc(s_ufree, 1)
                    if k == 10:
                        copy_group(0, c0 + k, Z[:, :, Z_LV:Z_GATE], 512)
                        act.wait_ge(s_gfree, g0 + 7)
                        cast(V65[:, :, :, 0:DH],
                             Z[:, :, Z_LV:Z_LO].rearrange("p t (h d) -> p t h d", h=ML_H)).then_inc(s_v65, 1)
                    if k == 11:
                        copy_group(1, c0 + k, Z[:, :, Z_GATE:ZW], 8)
                act.wait_ge(s_qk, l + 1)
                cast(QK[:, :, NQK, :], QK[:, :, NQK - 1, :])
                cast(QK[:, :, NQK + 1, :], QK[:, :, NQK - 2, :]).then_inc(s_qsw, 1)
                for j in range(6):
                    w = 512 if j < 5 else 256
                    act.wait_ge(s_qt, 6 * l + j + 1)
                    cast(QKT[:, 2 * j:2 * j + w // 256, :].rearrange("p a n -> p (a n)"),
                         PS[:, 6 + j % 2, 0:w]).then_inc(s_qtc, 1)

                def exps(h):
                    act.wait_ge(s_nb, h0 + h + 1)
                    nc.scalar.activation(PM[:, h % 2, 0:128], PM[:, h % 2, 0:128], ACT.Exp, scale=ISC,
                                         bias=NB[:, h, 0:1], accum_out=SUM[:, h, 0:1])
                    nc.scalar.activation(PM[:, h % 2, 128:384], PM[:, h % 2, 128:384], ACT.Exp, scale=ISC,
                                         bias=NB[:, h, 1:2], accum_out=SUM[:, h, 1:2]).then_inc(s_e, 1)

                def head_out(h):
                    act.wait_ge(s_o, h0 + h + 1 + 2)
                    col = DH * h if h < MOBA_H else DH * (h + ML_H)
                    cast(YN[:, :, col:col + DH],
                         PS[:, 4 + h % 2, 0:128].rearrange("p (t d) -> p t d", t=2)).then_inc(s_oe, 1)

                for h in range(14):
                    if h < 12:
                        exps(h)
                    if h >= 2:
                        head_out(h - 2)
                act.wait_ge(s_ske, l + 1)
                nc.scalar.activation(SKE[:, :, :], SKE[:, :, :], ACT.Exp).then_inc(s_sko, 1)

                act.wait_ge(s_ga, l + 1)
                link(nc.scalar.activation(GT1[:, :, :], GT1[:, :, :], ACT.Exp))
                nc.scalar.activation(GT1[:, :, :], GT1[:, :, :], ACT.Ln, bias=1.0).then_inc(s_gl, 1)
                act.wait_ge(s_me, l + 1)
                nc.scalar.activation(ME[:, :, :, :], ME[:, :, :, :], ACT.Exp).then_inc(s_mex, 1)
                act.wait_ge(s_mem, l + 1)
                nc.scalar.activation(GT2[:, :, :], GT2[:, :, :], ACT.Exp, scale=-1.0).then_inc(s_exm, 1)
                act.wait_ge(s_cv, l + 1)
                nc.scalar.activation(SG[:, :, :], CV[:, :, :], ACT.Sigmoid).then_inc(s_sg, 1)
                act.wait_ge(s_mt, l + 1)
                for j in range(3):
                    last = cast(PTM[:, j, :, :].rearrange("p a n -> p (a n)"), PS[:, 3 + j, :])
                last.then_inc(s_mtc, 1)
                nc.scalar.activation(Z[:, :, Z_LO:Z_GATE], Z[:, :, Z_LO:Z_GATE], ACT.Sigmoid).then_inc(s_so, 1)
                act.wait_ge(s_h, l + 1)
                nc.scalar.activation(CV[:, 0:2, :], HM[:, :, :], ACT.Square).then_inc(s_hsq, 1)

                spare(L.m_o, 0)
                spare(L.m_o, 1)
                high(4 * t0 + 4)
                rows_out(L.m_o, (4, 5))
                for k in range(4):
                    ahead(L.c_o + k)
                spare(L.m_mlp, 0)
                act.wait_ge(s_gfree, g0 + 8 + 2)
                sum_squares(X)
                spare(L.m_mlp, 1)
                high(4 * t0 + 8, lambda k: PAR[:, 16 + 8 * l + k:17 + 8 * l + k])
                rows_out(L.m_mlp, (0, 2))
                mlp(l, L.c_mlp, u0 + 2)

            act.wait_ge(s_ctx, 16)

            def norm_scale(q, n, stream):
                return (lambda k: SCL[:, q.layer, n, k, stream:stream + 1],
                        lambda k: MOD[:, q.layer, M_SH[n] + k, stream:stream + 1])

            def keys_out(qk, j, ctx):
                act.wait_ge(s_qt2, j + 1)
                cast(KTB[:, :, S * ctx:S * ctx + S],
                     PS[:, 6, :].rearrange("p (a n) -> p a n", a=2)).then_inc(s_qc2, 1)

            def gate_rows(n):
                act.wait_ge(s_gt, n + 1)
                cast(GTB[:, 0:512], PS[:, 6, :])
                cast(GTB[:, 512:1024], PS[:, 7, :]).then_inc(s_gtc, 1)

            for q in PASSES:
                c0, g0, R = q.c_in, q.g, CTX if q.stream else X
                act.wait_ge(s_scl, q.layer + 1)
                if q.mini:
                    act.wait_ge(s_gfree, q.g - 1 + 2)
                    sum_squares(CTX)
                    high(q.t - 4, *norm_scale(q, 0, 1))
                    ahead(q.c - 1)
                    copy_group(1, q.c - 1, ZN[:, :, N_K:1024], 256)
                    act.wait_ge(s_gfree, q.g + 2)
                    cast(VB[:, 2:4, :], ZN[:, :, N_V:1024])
                    nc.scalar.activation(QK2[:, :, 8:10, :].rearrange("p t h d -> p t (h d)"), ZN[:, :, N_K:N_V],
                                         ACT.Square).then_inc(s_sq2, 1)
                    act.wait_ge(s_qk2, q.qk)
                    cast(QK2[:, :, 10, :], QK2[:, :, 9, :])
                    cast(QK2[:, :, 11, :], QK2[:, :, 8, :]).then_inc(s_qw2, 1)
                    keys_out(q.qk - 1, 3 * (q.qk - 1), 1)
                    spare(q.m_in, 0)
                else:
                    spare(q.m_in, 0)
                    act.wait_ge(s_gfree, q.g + 2)
                sum_squares(R)
                spare(q.m_in, 1)
                high(q.t, *norm_scale(q, 0, q.stream))
                rows_out(q.m_in, (0, 2))
                qt0 = 3 * q.p + (1 if q.mini else 0)
                for k in range(19):
                    ahead(c0 + k)
                    if k < 3:
                        act.wait_ge(s_used, c0 + k + 1 + HL_N)
                        cast(UB[:, k, :, :].rearrange("p a n -> p (a n)"), PS[:, 4 + (q.u + k) % 2, :]).then_inc(s_ufree, 1)
                    if k == 3:
                        copy_group(0, c0 + k, ZN[:, :, N_F:N_Q], 256)
                    if k == 5:
                        copy_group(1, c0 + k, ZN[:, :, N_Q:N_K], 512)
                    if k == 6:
                        copy_group(0, c0 + k, ZN[:, :, N_K:1024], 256)
                        act.wait_ge(s_gfree, g0 + 3 + 2)
                        nc.scalar.activation(QK2[:, :, 0:10, :].rearrange("p t h d -> p t (h d)"), ZN[:, :, N_Q:N_V],
                                             ACT.Square).then_inc(s_sq2, 1)
                        cast(VB[:, 2 * q.stream:2 * q.stream + 2, :], ZN[:, :, N_V:1024])
                        act.wait_ge(s_fa, q.p + 1)
                        for j in range(2):
                            last = cast(A12[:, j, :, :].rearrange("p a n -> p (a n)"), PS[:, 6 + j, :])
                        last.then_inc(s_fac, 1)
                    if k == 7:
                        act.wait_ge(s_fy, q.p + 1)
                        cast(YF[:, :, :].rearrange("p a n -> p (a n)"), PS[:, 6, :]).then_inc(s_fyc, 1)
                    if k >= 8 and k % 2 == 0:
                        j = k // 2 - 4
                        act.wait_ge(s_used, c0 + k + 1 + HL_N)
                        for t in range(NT):
                            last = nc.scalar.activation(GA[:, t, 512 * j:512 * j + 512], PS[:, t, :], ACT.Tanh, scale=0.5)
                        last.then_inc(s_gfree, 1)
                    if k == 9:
                        act.wait_ge(s_qk2, q.qk + 1)
                        cast(QK2[:, :, 10, :], QK2[:, :, 9, :])
                        cast(QK2[:, :, 11, :], QK2[:, :, 8, :]).then_inc(s_qw2, 1)
                        for j in range(2):
                            act.wait_ge(s_qt2, qt0 + j + 1)
                            cast(QT2[:, 2 * j:2 * j + 2, :].rearrange("p a n -> p (a n)"),
                                 PS[:, 6 + j, :]).then_inc(s_qc2, 1)
                        keys_out(q.qk, qt0 + 2, q.stream)
                    for v in units(k):
                        if v < 16:
                            h, t = divmod(v, 2)
                            n = 256 if q.stream else 512
                            act.wait_ge(s_n2, q.att + v + 1)
                            act.wait_ge(s_t2, q.att + v + 1)
                            nc.scalar.activation(PM[:, v % 2, 0:n], PS[:, 4 + v % 2, 0:n], ACT.Exp,
                                                 bias=NM2[:, h, t:t + 1], accum_out=SM2[:, h, t:t + 1]).then_inc(s_e2, 1)
                        if v >= 4:
                            h, t = divmod(v - 4, 2)
                            act.wait_ge(s_o2, q.att + v - 4 + 1 + 2)
                            cast(YA[:, t, DH * h:DH * h + DH], PS[:, 2 + v % 2, 0:DH]).then_inc(s_oe2, 1)
                act.wait_ge(s_yc, q.p + 1)
                act.wait_ge(s_fyc, q.p + 1)
                act.wait_ge(s_used, c0 + 19 + HL_N)
                cast(AH[:, 0:2, :], YC[:, :, :])
                cast(AH[:, 2:4, :], YF[:, :, :]).then_inc(s_yh, 1)
                high(q.t + 4, steps=(2, 3))
                for k in range(19, 23):
                    ahead(c0 + k)
                spare(q.m_o, 0)
                spare(q.m_o, 1)
                high(q.t + 6)
                gate_rows(2 * q.p)
                rows_out(q.m_o, (4, 5))
                for k in range(4):
                    ahead(q.c_o + k)
                spare(q.m_mlp, 0)
                act.wait_ge(s_gfree, g0 + 17 + 2)
                sum_squares(R)
                spare(q.m_mlp, 1)
                high(q.t + 10, *norm_scale(q, 1, q.stream))
                gate_rows(2 * q.p + 1)
                rows_out(q.m_mlp, (0, 2))
                mlp(q.mlp, q.c_mlp, q.u + 3)

            act.wait_ge(s_gfree, LP.g + GR2 + 2)
            act.dma_start(out[0].rearrange("(t p) d -> p t d", p=P), X[:, :, :]).then_inc(s_out, 16)
            act.wait_ge(s_out, 16)

        @block.vector
        def _(dve):
            chain = [0]

            def link(ins):
                chain[0] += 1
                ins.then_inc(s_dv, 1)
                dve.wait_ge(s_dv, chain[0])

            tt, ts, stt = nc.vector.tensor_tensor, nc.vector.tensor_scalar, nc.vector.scalar_tensor_tensor
            for s, n in ((s_lo, RAW_N), (s_used, HL_N), (s_gfree, 2), (s_ufree, 2), (s_tlo, 2), (s_qtc, 2), (s_sm, 2), (s_pt, 2), (s_pe, 2), (s_o, 2), (s_oe, 2),
                         (s_qc2, 2), (s_e2, 2), (s_t2, 2), (s_p2, 2), (s_o2, 2), (s_oe2, 2)):
                dve.sem_inc(s, n)

            dve.wait_ge(s_cst, 16 * N_CONST)
            link(ts(NSK[:, :, :], SK[:, :, :], -1.0, None, ALU.mult))
            dve.wait_ge(s_cs, 1)
            tt(CS[:, :, :].rearrange("p s k -> p (s k)"), PAR[:, 64:80], SGC[:, :], ALU.mult).then_inc(s_cs, 1)
            dve.wait_ge(s_c4, 1)
            tt(C4[:, :, 2:4], CS[:, :, :].rearrange("p s k -> p k s"), C4[:, :, 0:2].bitcast(F32),
               ALU.subtract).then_inc(s_c4, 1)

            def split(c):
                dve.wait_ge(s_hi, c + 1)
                n = chunk_words(c)
                tt(LO[:, c % HL_N, 0:n], RAW[:, c % RAW_N, 0:n], HI[:, c % HL_N, 0:n].bitcast(F32),
                   ALU.subtract).then_inc(s_lo, 1)

            def ahead(c):
                if c + SPLIT_LEAD < NCH:
                    split(c + SPLIT_LEAD)

            def norm(n, m, src):
                dve.wait_ge(s_ss, n + 1)
                ts(MS[:, 0:2], SSQ[:, :], 1.0 / D, EPS, ALU.mult, ALU.add).then_inc(s_ms, 1)
                dve.wait_ge(s_rs, m + 1)
                for t in range(NT):
                    last = ts(YN[:, t, :], src[:, t, :], RS[:, t:t + 1], None, ALU.mult)
                last.then_inc(s_src, 1)

            def low(n, scaled, steps=range(4)):
                for s in steps:
                    dve.wait_ge(s_thi, n + s - steps[0] + 1)
                    full = TMP[:, s % 2, :] if scaled else PS[:, 6 + s % 2, :]
                    tt(AL[:, 2 * s:2 * s + 2, :].rearrange("p a n -> p (a n)"), full,
                       AH[:, 2 * s:2 * s + 2, :].rearrange("p a n -> p (a n)").bitcast(F32),
                       ALU.subtract).then_inc(s_tlo, 1)

            def add_group(c, half, res=X, gate=None, g=None):
                dve.wait_ge(s_used, c + 1 + HL_N)
                cols = slice(512 * half, 512 * half + 512)
                src = [PS[:, 2 * half + t, :] for t in range(NT)]
                if gate is not None:
                    dve.wait_ge(s_gfree, g + 2)
                    for t in range(NT):
                        last = tt(TM[:, t, :], src[t], gate[:, cols], ALU.mult)
                    link(last)
                    src = [TM[:, t, :] for t in range(NT)]
                for t in range(NT):
                    last = tt(res[:, t, cols], src[t], res[:, t, cols], ALU.add)
                last.then_inc(s_gfree, 1)

            def spare(m, *js):
                if m.here:
                    for j in js:
                        ahead(m.c + j)

            def mod_out(m, banks):
                if m.here:
                    for j in range(2):
                        g = m.g + j
                        l, k = g // 12, 4 * (g % 12)
                        dve.wait_ge(s_mcol, g + 1)
                        tt(MOD[:, l, k:k + 4, :], PS[:, banks[j], 0:8].rearrange("p (c s) -> p c s", s=2),
                           PAR[:, 128 + 48 * l + k:132 + 48 * l + k].unsqueeze(2).to_broadcast((P, 4, 2)),
                           ALU.add).then_inc(s_modc, 1)

            def mlp(q, c, u, m):
                for i in range(4):
                    for j in range(8):
                        ahead(c + 8 * i + j)
                        if j < 4:
                            cols = 2 * (j % 2)
                            hid = HIDH[:, j // 2, cols:cols + 2, :].rearrange("p a n -> p (a n)")
                            dve.wait_ge(s_rl, 16 * q + 4 * i + j + 1)
                            stt(U2[:, j % 2, :], PS[:, 4 + (u + j) % 2, :], 0.0, RL[:, j % 2, :], ALU.max,
                                ALU.mult).then_inc(s_ufree, 1)
                            dve.wait_ge(s_ufree, u + 4 * i + j + 1 + 2)
                            dve.wait_ge(s_hh, 16 * q + 4 * i + j + 1)
                            tt(HIDL[:, j // 2, cols:cols + 2, :].rearrange("p a n -> p (a n)"),
                               U2[:, j % 2, :], hid.bitcast(F32), ALU.subtract).then_inc(s_hl, 1)
                        if i == 0 and j == 0:
                            mod_out(m, (0, 2))

            for c in range(SPLIT_LEAD):
                split(c)

            for l in range(DEPTH):
                L = LAYERS[l]
                c0, g0, u0, t0, h0 = L.c_in, GR1 * l, UC1 * l, 3 * l, 12 * l
                spare(L.m_in, 0)
                norm(2 * l, 4 * l, X)
                spare(L.m_in, 1)
                low(4 * t0, True)
                spare(L.m_in, 2, 3)
                runs = ((QK[:, :, 0:12, :], Z[:, :, 0:768]), (QK[:, :, 12:NQK, :], Z[:, :, C_SQ:C_SV]))
                runs = [(q, z.rearrange("p t (h d) -> p t h d", d=DH)) for q, z in runs]
                for k in range(12):
                    ahead(c0 + k)
                    if k == 0:
                        mod_out(L.m_in, (4, 5))
                    if k == 7:
                        dve.wait_ge(s_sq, l + 1)
                        link(nc.vector.tensor_reduce(MS[:, 0:2 * NQK].rearrange("p (t h) -> p t h", t=NT),
                                                     QK[:, :, 0:NQK, :], AX_X, ALU.add))
                        ts(MS[:, 0:2 * NQK], MS[:, 0:2 * NQK], 1.0 / DH, EPS, ALU.mult, ALU.add).then_inc(s_ms, 1)
                    if k == 8:
                        dve.wait_ge(s_rs, 4 * l + 2)
                        rs = RS[:, 0:2 * NQK].rearrange("p (t h) -> p t h", t=NT).unsqueeze(3)
                        for (q, z), (h1, h2) in zip(runs, ((0, 12), (12, NQK))):
                            last = tt(q, z, rs[:, :, h1:h2, :].to_broadcast((P, NT, h2 - h1, DH)), ALU.mult)
                        link(last)
                        for i, (h1, h2) in enumerate(((0, 6), (6, 12), (12, 18), (18, 20))):
                            q = QK[:, :, h1:h2, :]
                            g = GN[:, l:l + 1, i:i + 1, :].to_broadcast((P, NT, h2 - h1, DH))
                            last = tt(q, q, g, ALU.mult)
                        link(last)
                    if k == 9:
                        sin = CT[:, K_R1 + 64:K_R1 + 128].rearrange("p (t h d) -> p t h d", t=NT, h=1)
                        for q, z in runs:
                            b = sin.to_broadcast((P, NT, q.shape[2], 32))
                            tt(z[:, :, :, 0:32], q[:, :, :, 32:64], b, ALU.mult)
                            last = tt(z[:, :, :, 32:64], q[:, :, :, 0:32], b, ALU.mult)
                        link(last)
                    if k == 10:
                        cos = CT[:, K_R1:K_R1 + 64].rearrange("p (t h d) -> p t h d", t=NT, h=1)
                        q = QK[:, :, 0:NQK, :].rearrange("p t h (a d) -> p t (h a) d", a=2)
                        link(tt(q, q, cos.to_broadcast((P, NT, 2 * NQK, 32)), ALU.mult))
                        for q, z in runs:
                            tt(q[:, :, :, 0:32], q[:, :, :, 0:32], z[:, :, :, 0:32], ALU.subtract)
                            last = tt(q[:, :, :, 32:64], q[:, :, :, 32:64], z[:, :, :, 32:64], ALU.add)
                        last.then_inc(s_qk, 1)

                zero_m, caus = CT[:, K_M:K_M + 128], CT[:, K_M + 128:K_M + 256]
                for h in range(13):
                    if h < 12:
                        dve.wait_ge(s_s, h0 + h + 1)
                        dve.wait_ge(s_pt, h0 + h + 1)
                        old = CT[:, K_M:K_M + 256] if h < MOBA_H else CT[:, K_M + 256:K_M + 512]
                        nc.vector.tensor_tensor_reduce(PM[:, h % 2, 0:128], PS[:, h % 2, 0:128], caus, 1.0, -3e38,
                                                       ALU.add, ALU.max, MX[:, h % 2, 0:1])
                        nc.vector.tensor_tensor_reduce(PM[:, h % 2, 128:384], PS[:, h % 2, 128:384], old, 1.0, -3e38,
                                                       ALU.add, ALU.max, MX[:, h % 2, 1:2]).then_inc(s_sm, 1)
                        dve.wait_ge(s_sm, h0 + h + 1 + 2)
                        if h < MOBA_H:
                            ts(NB[:, h, :], MX[:, h % 2, :], -ISC, None, ALU.mult).then_inc(s_nb, 1)
                        else:
                            ts(NB[:, h, :], MX[:, h % 2, :], -ISC, NSK[:, l, h - 6:h - 5], ALU.mult,
                               ALU.min).then_inc(s_nb, 1)
                    if h >= 1:
                        dve.wait_ge(s_pt, h0 + h + 2)
                        dve.wait_ge(s_o, h0 + h)
                        nc.vector.tensor_copy(PTS[:, (h - 1) % 2, 0:384],
                                              PS[:, 2 + (h - 1) % 2, 0:384]).then_inc(s_pe, 1)
                tt(SKE[:, :, :], NB[:, 6:12, :], SK[:, l, :].unsqueeze(2).to_broadcast((P, 6, 2)),
                   ALU.add).then_inc(s_ske, 1)
                dve.wait_ge(s_e, h0 + 12)
                dve.wait_ge(s_sko, l + 1)
                link(tt(SUM[:, 6:12, :], SUM[:, 6:12, :], SKE[:, :, :], ALU.add))
                link(nc.vector.reciprocal(RIN[:, :, :], SUM[:, :, :]))
                dve.wait_ge(s_oe, h0 + 12 + 2)
                for col, h1 in ((0, 0), (DH * (MOBA_H + ML_H), 6)):
                    y = YN[:, :, col:col + 6 * DH].rearrange("p t (h d) -> p t h d", h=6)
                    tt(y, y, RIN[:, h1:h1 + 6, :].rearrange("p h t -> p t h").unsqueeze(3).to_broadcast((P, NT, 6, DH)),
                       ALU.mult)

                dve.wait_ge(s_gfree, g0 + 6 + 2)
                link(tt(G8[:, :, :], Z[:, :, Z_GATE:ZW], IFB[:, l:l + 1, :].to_broadcast((P, NT, 8)), ALU.add))
                f = G8[:, :, 4:8]
                stt(GT1[:, :, :], f, -1.0, f, ALU.mult, ALU.min).then_inc(s_ga, 1)
                dve.wait_ge(s_gl, l + 1)
                stt(GT2[:, :, :], f, 0.0, GT1[:, :, :], ALU.min, ALU.subtract).then_inc(s_lf, 1)
                dve.wait_ge(s_b, l + 1)
                link(nc.vector.tensor_copy(BS[:, :, :], PS[:, 6, 0:8].rearrange("p (t h) -> p t h", t=NT)))
                link(tt(ES[:, :, :], G8[:, :, 0:4], BS[:, :, :], ALU.subtract))
                for t in range(NT):
                    last = tt(DG[:, t, :, :], IDM.unsqueeze(1).to_broadcast((P, ML_H, P)),
                              ES[:, t, :].unsqueeze(2).to_broadcast((P, ML_H, P)), ALU.mult)
                last.then_inc(s_dg, 1)
                dve.wait_ge(s_eb, l + 1)
                for j in range(3):
                    m = (zero_m if j == 1 else caus).unsqueeze(1).to_broadcast((P, ML_H, P))
                    last = tt(ME[:, j, :, :], PS[:, 6 + j // 2, :].rearrange("p (h n) -> p h n", h=ML_H), m, ALU.add)
                link(last)
                link(nc.vector.tensor_reduce(RMX[:, :, :], ME[:, :, :, :], AX_X, ALU.max))
                link(tt(RMX[:, 1, :], RMX[:, 1, :], RMX[:, 2, :], ALU.max))
                link(ts(RR[:, :, :], RMX[:, 0:2, :], 0.0, None, ALU.max))
                for j in range(3):
                    last = tt(ME[:, j, :, :], ME[:, j, :, :],
                              RR[:, (j + 1) // 2, :].unsqueeze(2).to_broadcast((P, ML_H, P)), ALU.subtract)
                last.then_inc(s_me, 1)
                tt(GT2[:, :, :], BS[:, :, :], RR[:, :, :], ALU.add).then_inc(s_mem, 1)
                dve.wait_ge(s_ufree, u0 + 2 + 2)
                wc = lambda j, q: PAR[:, 80 + 16 * l + 4 * j + q:81 + 16 * l + 4 * j + q]
                for q in range(4):
                    ts(CV[:, q, :], XP[:, q, 0:S], wc(0, q), PAR[:, 112 + 4 * l + q:113 + 4 * l + q],
                       ALU.mult, ALU.add)
                for j in range(1, 4):
                    link(nc.vector.engine_nop())
                    for q in range(4):
                        last = stt(CV[:, q, :], XP[:, q, j:j + S], wc(j, q), CV[:, q, :], ALU.mult, ALU.add)
                last.then_inc(s_cv, 1)
                dve.wait_ge(s_sg, l + 1)
                tt(CV[:, :, :], CV[:, :, :], SG[:, :, :], ALU.mult).then_inc(s_lqk, 1)
                dve.wait_ge(s_mex, l + 1)
                dve.wait_ge(s_ms3, l + 1)
                for j in range(3):
                    for b in range(2):
                        m = ME[:, j, b:ML_H:2, :]
                        last = stt(m, PS[:, 2 * j + b, 0:256].rearrange("p (h n) -> p h n", h=2), ISC, m,
                                   ALU.mult, ALU.mult)
                last.then_inc(s_mp, 1)
                dve.wait_ge(s_exm, l + 1)
                dve.wait_ge(s_mo, l + 1)
                o = PS[:, 6:8, 0:260].rearrange("p t (h d) -> p t h d", h=ML_H)
                link(nc.vector.tensor_copy(DEN[:, :, :], o[:, :, :, DH]))
                link(stt(GT1[:, :, :], DEN[:, :, :], -1.0, DEN[:, :, :], ALU.mult, ALU.max))
                link(tt(DEN[:, :, :], GT1[:, :, :], GT2[:, :, :], ALU.max))
                link(nc.vector.reciprocal(DEN[:, :, :], DEN[:, :, :]))
                hm = HM[:, :, :].rearrange("p t (h d) -> p t h d", h=ML_H)
                link(tt(hm, o[:, :, :, 0:DH], DEN[:, :, :].unsqueeze(3).to_broadcast((P, NT, ML_H, DH)), ALU.mult))
                dve.wait_ge(s_so, l + 1)
                tt(HM[:, :, :], HM[:, :, :], Z[:, :, Z_LO:Z_GATE], ALU.mult).then_inc(s_h, 1)
                dve.wait_ge(s_hsq, l + 1)
                link(nc.vector.tensor_reduce(MS[:, 0:8].rearrange("p (t h) -> p t h", t=NT),
                                             CV[:, 0:2, :].rearrange("p t (h d) -> p t h d", h=ML_H), AX_X, ALU.add))
                ts(MS[:, 0:8], MS[:, 0:8], 1.0 / DH, EPS, ALU.mult, ALU.add).then_inc(s_ms, 1)
                dve.wait_ge(s_rs, 4 * l + 3)
                link(tt(hm, hm, RS[:, 0:8].rearrange("p (t h) -> p t h", t=NT).unsqueeze(3)
                        .to_broadcast((P, NT, ML_H, DH)), ALU.mult))
                tt(YN[:, :, MOBA_H * DH:(MOBA_H + ML_H) * DH], HM[:, :, :],
                   MN[:, l:l + 1, :].to_broadcast((P, NT, ML_H * DH)), ALU.mult).then_inc(s_src, 1)

                spare(L.m_o, 0, 1)
                low(4 * t0 + 4, False)
                spare(L.m_o, 2, 3)
                for k in range(4):
                    ahead(L.c_o + k)
                    if k == 0:
                        mod_out(L.m_o, (4, 5))
                    if k % 2:
                        add_group(L.c_o + k, k // 2)
                spare(L.m_mlp, 0)
                norm(2 * l + 1, 4 * l + 3, X)
                spare(L.m_mlp, 1)
                low(4 * t0 + 8, True)
                spare(L.m_mlp, 2, 3)
                mlp(l, L.c_mlp, u0 + 2, L.m_mlp)
                for half in range(2):
                    add_group(L.c_mlp + 30 + half, half)

            def norm_scales(l):
                dve.wait_ge(s_modc, 12 * l + 10)
                for n in range(2):
                    g = PAR[:, 32 + 16 * n + 8 * l:40 + 16 * n + 8 * l].unsqueeze(2).to_broadcast((P, KT, 2))
                    stt(SCL[:, l, n, :, :], MOD[:, l, M_SC[n]:M_SC[n] + 8, :], 1.0, g, ALU.add, ALU.mult)
                ts(GQ2[:, l, 0, :], GQ2[:, l, 0, :], ISC, None, ALU.mult).then_inc(s_scl, 1)
                dve.wait_ge(s_scl, l + 1)

            norm_scales(0)
            dve.wait_ge(s_pad, 1)

            def head_squares(q, n, h1):
                dve.wait_ge(s_sq2, n + 1)
                w = NT * (10 - h1)
                link(nc.vector.tensor_reduce(MS[:, 0:w].rearrange("p (t h) -> p t h", t=NT), QK2[:, :, h1:10, :],
                                             AX_X, ALU.add))
                ts(MS[:, 0:w], MS[:, 0:w], 1.0 / DH, EPS, ALU.mult, ALU.add).then_inc(s_ms, 1)

            def head_norm(q, m, h1, signal):
                dve.wait_ge(s_rs, m + 1)
                w = NT * (10 - h1)
                z = ZN[:, :, N_Q + DH * h1:N_V].rearrange("p t (h d) -> p t h d", d=DH)
                rs = RS[:, 0:w].rearrange("p (t h) -> p t h", t=NT).unsqueeze(3)
                link(tt(QK2[:, :, h1:10, :], z, rs.to_broadcast((P, NT, 10 - h1, DH)), ALU.mult))
                for i, (a1, a2) in enumerate(((h1, 8), (8, 10))):
                    if a1 < a2:
                        h = QK2[:, :, a1:a2, :]
                        last = tt(h, h, GQ2[:, q.layer:q.layer + 1, i:i + 1, :].to_broadcast((P, NT, a2 - a1, DH)),
                                  ALU.mult)
                last.then_inc(s_qk2, 1) if signal else link(last)

            def gate_diagonals(q, n, factor):
                gt = MOD[:, q.layer, M_GT[n]:M_GT[n] + 8, q.stream]
                last = stt(DGB[:, :, :], gt.unsqueeze(2).to_broadcast((P, 8, P)), factor,
                           IDM.unsqueeze(1).to_broadcast((P, 8, P)), ALU.mult, ALU.mult)
                last.then_inc(s_dgb, 1)

            for q in PASSES:
                c0, g0, R = q.c_in, q.g, CTX if q.stream else X
                if q.mini:
                    norm_scales(1)
                    norm(q.norm - 1, q.pow - 2, CTX)
                    low(q.t - 4, True)
                    ahead(q.c - 1)
                    head_squares(q, q.qk - 1, 8)
                    head_norm(q, q.pow - 1, 8, True)
                spare(q.m_in, 0)
                norm(q.norm, q.pow, R)
                spare(q.m_in, 1)
                low(q.t, True)
                spare(q.m_in, 2, 3)
                for k in range(19):
                    ahead(c0 + k)
                    if k == 0:
                        mod_out(q.m_in, (0, 2))
                    if k == 3:
                        dve.wait_ge(s_ufree, q.u + 3 + 2)
                        link(tt(CXP[:, :, 1:1 + S], UB[:, 1, :, :], UB[:, 2, :, :], ALU.mult))
                        wc = lambda j, b: PAR[:, 224 + 6 * q.layer + 2 * j + b:225 + 6 * q.layer + 2 * j + b]
                        for b in range(2):
                            last = ts(YC[:, b, :], CXP[:, b, 0:S], wc(0, b), None, ALU.mult)
                        link(last)
                    if k in (4, 5):
                        for b in range(2):
                            last = stt(YC[:, b, :], CXP[:, b, k - 3:k - 3 + S], wc(k - 3, b), YC[:, b, :], ALU.mult,
                                       ALU.add)
                        link(last)
                        if k == 5:
                            tt(YC[:, :, :], YC[:, :, :], UB[:, 0, :, :], ALU.mult).then_inc(s_yc, 1)
                    if k == 7:
                        head_squares(q, q.qk, 0)
                        head_norm(q, q.pow + 1, 0, q.stream == 1)
                    if k == 8 and q.stream == 0:
                        qk = QK2[:, :, 0:10, :]
                        z = ZN[:, :, N_Q:N_V].rearrange("p t (h d) -> p t h d", d=DH)
                        sin = CT[:, K_R2 + 64:K_R2 + 128].rearrange("p (t h d) -> p t h d", t=NT, h=1)
                        cos = CT[:, K_R2:K_R2 + 64].rearrange("p (t h d) -> p t h d", t=NT, h=1)
                        b = sin.to_broadcast((P, NT, 10, 32))
                        tt(z[:, :, :, 0:32], qk[:, :, :, 32:64], b, ALU.mult)
                        link(tt(z[:, :, :, 32:64], qk[:, :, :, 0:32], b, ALU.mult))
                        q2 = qk.rearrange("p t h (a d) -> p t (h a) d", a=2)
                        link(tt(q2, q2, cos.to_broadcast((P, NT, 20, 32)), ALU.mult))
                        tt(qk[:, :, :, 0:32], qk[:, :, :, 0:32], z[:, :, :, 0:32], ALU.subtract)
                        tt(qk[:, :, :, 32:64], qk[:, :, :, 32:64], z[:, :, :, 32:64], ALU.add).then_inc(s_qk2, 1)
                    for v in units(k):
                        n = 256 if q.stream else 512
                        if v < 16:
                            h, t = divmod(v, 2)
                            dve.wait_ge(s_s2, q.att + v + 1)
                            nc.vector.tensor_reduce(NM2[:, h, t:t + 1], PS[:, 4 + v % 2, 0:n], AX_X, ALU.max,
                                                    negate=True).then_inc(s_n2, 1)
                        if 2 <= v < 18:
                            dve.wait_ge(s_t2, q.att + v - 2 + 1 + 2)
                            dve.wait_ge(s_o2, q.att + v - 2 + 1)
                            nc.vector.tensor_copy(PTS[:, v % 2, 0:n], PS[:, 6 + v % 2, 0:n]).then_inc(s_p2, 1)
                dve.wait_ge(s_yh, q.p + 1)
                tt(AL[:, 0:2, :], YC[:, :, :], AH[:, 0:2, :].bitcast(F32), ALU.subtract)
                tt(AL[:, 2:4, :], YF[:, :, :], AH[:, 2:4, :].bitcast(F32), ALU.subtract).then_inc(s_yl, 1)
                dve.wait_ge(s_oe2, q.att + 16 + 2)
                link(nc.vector.reciprocal(RN2[:, :, :], SM2[:, :, :]))
                for t in range(NT):
                    y = YA[:, t, :].rearrange("p (h d) -> p h d", h=QH)
                    last = tt(y, y, RN2[:, :, t].unsqueeze(2).to_broadcast((P, QH, DH)), ALU.mult)
                last.then_inc(s_src, 1)
                low(q.t + 4, False, (2, 3))
                for k in range(19, 23):
                    b, halfs = ((0, (0, 1)), (1, (0, 1)), (2, (0,)), (2, (1,)))[k - 19]
                    ahead(c0 + k)
                    for half in halfs:
                        if b < 2 and half == 0:
                            dve.wait_ge(s_bg, 2 * q.p + b + 1)
                        else:
                            dve.wait_ge(s_used, c0 + k + 1 + HL_N)
                        cols = slice(512 * half, 512 * half + 512)
                        for t in range(NT):
                            ga = GA[:, t, D * b + 512 * half:D * b + 512 * half + 512]
                            dst = M2[:, t, cols] if b == 0 else TM[:, t, :]
                            last = stt(dst, ga, 1.0, PS[:, 2 * half + t, :], ALU.add, ALU.mult)
                        last.then_inc(s_gfree, 1)
                        if b > 0:
                            dve.wait_ge(s_gfree, g0 + 9 + 2 * b + half + 1 + 2)
                            for t in range(NT):
                                last = tt(M2[:, t, cols], M2[:, t, cols], TM[:, t, :], ALU.add)
                            if b == 2 and half == 1:
                                last.then_inc(s_src, 1)
                            else:
                                link(last)
                dve.wait_ge(s_src, q.src + 3)
                gate_diagonals(q, 0, 0.5)
                spare(q.m_o, 0, 1)
                low(q.t + 6, False)
                spare(q.m_o, 2, 3)
                dve.wait_ge(s_gtc, 2 * q.p + 1)
                for k in range(4):
                    ahead(q.c_o + k)
                    if k == 0:
                        mod_out(q.m_o, (4, 5))
                    if k % 2:
                        add_group(q.c_o + k, k // 2, R, GTB, g0 + 15 + k // 2)
                spare(q.m_mlp, 0)
                norm(q.norm + 1, q.pow + 2, R)
                dve.wait_ge(s_gfree, g0 + 17 + 2)
                gate_diagonals(q, 1, 1.0)
                spare(q.m_mlp, 1)
                low(q.t + 10, True)
                spare(q.m_mlp, 2, 3)
                mlp(q.mlp, q.c_mlp, q.u + 3, q.m_mlp)
                dve.wait_ge(s_gtc, 2 * q.p + 2)
                for half in range(2):
                    add_group(q.c_mlp + 30 + half, half, R, GTB, g0 + 17 + half)

        @block.tensor
        def _(pe):
            mm = nc.tensor.matmul
            pe.wait_ge(s_cst, 16 * N_CONST)
            nc.tensor.transpose(PS[:, 6, 0:120], PR0[0:120, :], IDM[0:120, 0:120])
            nc.tensor.transpose(PS[:, 7, 0:108], PR1[0:108, :], IDM[0:108, 0:108]).then_inc(s_par, 1)
            pe.wait_ge(s_c4, 2)

            def transposes(source, n, src, steps=range(4), m=NO_SLOT, banks=(4, 5)):
                if m.here:
                    for j in range(3):
                        mod_chunk(m, j, banks)
                pe.wait_ge(s_src, source + 1)
                for s in range(len(steps)):
                    if m.here and s == 2:
                        mod_chunk(m, 3, banks)
                    pe.wait_ge(s_tlo, n + s + 1)
                    for k in range(2):
                        for t in range(NT):
                            last = nc.tensor.transpose(PS[:, 6 + s % 2, 256 * k + 128 * t:256 * k + 128 * t + 128],
                                                       src[:, t, 128 * (2 * s + k):128 * (2 * s + k) + 128], IDM)
                    last.then_inc(s_tp, 1)
                return n + len(steps)

            def split_done(steps):
                pe.wait_ge(s_tlo, steps + 2)

            def arrived(c):
                pe.wait_ge(s_lo, c + 1 + RAW_N)

            def slot(k, kt, n):
                hi = HI[:, k % HL_N, 0:kt * n].rearrange("p (a n) -> p a n", a=kt)
                lo = LO[:, k % HL_N, 0:kt * n].rearrange("p (a n) -> p a n", a=kt)
                return hi, lo

            def tokens_out(c, k, bank, kt, n, ah, al, first, last):
                arrived(c)
                hi, lo = slot(k, kt, n)
                for t in range(NT):
                    o = PS[:, bank + t, 0:n]
                    for j in range(kt):
                        th, tl = ah[:, j, 128 * t:128 * t + 128], al[:, j, 128 * t:128 * t + 128]
                        mm(o, th, hi[:, j, :], start=first and j == 0, stop=False)
                        mm(o, th, lo[:, j, :], start=False, stop=False)
                        ins = mm(o, tl, hi[:, j, :], start=False, stop=last and j == kt - 1)
                ins.then_inc(s_used, 1)

            def features_out(c, k, bank, ah, al):
                arrived(c)
                hi, lo = slot(k, KT, 256)
                for q in range(2):
                    o = PS[:, bank, 256 * q:256 * q + 256]
                    for j in range(KT):
                        wh, wl = hi[:, j, 128 * q:128 * q + 128], lo[:, j, 128 * q:128 * q + 128]
                        mm(o, wh, ah[:, j, :], start=j == 0, stop=False)
                        mm(o, wh, al[:, j, :], start=False, stop=False)
                        ins = mm(o, wl, ah[:, j, :], start=False, stop=j == KT - 1)
                ins.then_inc(s_used, 1)

            def group(g, c, k, n=512):
                pe.wait_ge(s_gfree, g + 1)
                for h in range(2):
                    half_group(c + h, k + h, g % 2, h, n)

            def half_group(c, k, pair, h, n=512):
                tokens_out(c, k, 2 * pair, 4, n, AH[:, 4 * h:4 * h + 4, :], AL[:, 4 * h:4 * h + 4, :], h == 0, h == 1)

            def mod_chunk(m, j, banks):
                arrived(m.c + j)
                hi, lo = slot(m.c + j, 4, 512)
                for k in range(4):
                    w, o = C4[:, 4 * (j % 2) + k, :], PS[0:4, banks[j // 2], :]
                    mm(o, w, hi[:, k, :], start=j % 2 == 0 and k == 0, stop=False)
                    last = mm(o, w, lo[:, k, :], start=False, stop=j % 2 == 1 and k == 3)
                last.then_inc(s_used, 1)

            def mod_columns(m, banks):
                if m.here:
                    for j in range(2):
                        pe.wait_ge(s_mrow, m.g + j + 1)
                        for k in range(4):
                            last = mm(PS[:, banks[j], 2 * k:2 * k + 2], ROWS[0:4, j, 128 * k:128 * k + 128], SEL[:, :],
                                      start=True, stop=True)
                        last.then_inc(s_mcol, 1)

            def mod_done(m):
                if m.here:
                    pe.wait_ge(s_modc, m.g + 2)

            def mlp(q, c, u, m):
                for i in range(4):
                    for j in range(4):
                        pe.wait_ge(s_ufree, u + 4 * i + j + 1)
                        features_out(c + 8 * i + j, c + 8 * i + j, 4 + (u + j) % 2, AH, AL)
                        if i == 0 and j == 0:
                            mod_columns(m, (0, 2))
                        if i == 0 and j == 1:
                            mod_done(m)
                    for j in range(4):
                        b = j // 2
                        pe.wait_ge(s_hl, 16 * q + 4 * i + 2 * b + 2)
                        tokens_out(c + 8 * i + 4 + j, c + 8 * i + 4 + j, 2 * (j % 2), 4, 512, HIDH[:, b, :, :],
                                   HIDL[:, b, :, :], i == 0 and b == 0, i == 3 and b == 1)

            for l in range(DEPTH):
                L = LAYERS[l]
                c0, g0, u0, t0, h0 = L.c_in, GR1 * l, UC1 * l, 3 * l, 12 * l
                pe.wait_ge(s_ufree, u0 + 2)
                split_done(transposes(t0, 4 * t0, YN, m=L.m_in))
                for j in range(3):
                    group(g0 + j, c0 + 2 * j, 2 * j)
                    if j == 0:
                        mod_columns(L.m_in, (4, 5))
                    if j == 1:
                        mod_done(L.m_in)
                pe.wait_ge(s_gfree, g0 + 4)
                tokens_out(c0 + 6, 6, 2, KT, 256, AH, AL, True, True)
                for j in range(2):
                    pe.wait_ge(s_ufree, u0 + j + 1)
                    features_out(c0 + 7 + j, 7 + j, 4 + j, AH, AL)
                group(g0 + 4, c0 + 9, 9)
                pe.wait_ge(s_gfree, g0 + 6)
                tokens_out(c0 + 11, 11, 2, KT, 8, AH, AL, True, True)

                pe.wait_ge(s_qsw, l + 1)
                for j in range(6):
                    pe.wait_ge(s_qtc, 6 * l + j + 1)
                    for k in range(2 if j < 5 else 1):
                        for t in range(NT):
                            h = 2 * (2 * j + k)
                            last = nc.tensor.transpose(
                                PS[:, 6 + j % 2, 256 * k + 128 * t:256 * k + 128 * t + 128],
                                QK[:, t, h:h + 2, :].rearrange("p h d -> p (h d)"), IDM)
                    last.then_inc(s_qt, 1)
                pe.wait_ge(s_qtc, 6 * l + 6 + 2)
                pe.wait_ge(s_gfree, g0 + 6 + 2)
                pe.wait_ge(s_ufree, u0 + 2 + 2)

                def scores(h):
                    r = 64 * (h % 2)
                    if h < MOBA_H:
                        q, k = QKT[r:r + 64, h // 2, :], QKT[r:r + 64, 3 + h // 2, :]
                    else:
                        kv = (h - 6) // 3
                        q = QKT[r:r + 64, 6 + (h - 6) // 2, :]
                        k = QKT[r:r + 64, 9 if kv == h % 2 else 10, :]
                    pe.wait_ge(s_sm, h0 + h + 1)
                    mm(PS[:, h % 2, 0:128], q[:, 0:128], k[:, 0:128], start=True, stop=True)
                    mm(PS[:, h % 2, 128:384], q[:, 128:256], k, start=True, stop=True).then_inc(s_s, 1)

                def turn(h):
                    pe.wait_ge(s_e, h0 + h + 1)
                    pe.wait_ge(s_pe, h0 + h + 1)
                    for j in range(3):
                        last = nc.tensor.transpose(PS[:, 2 + h % 2, 128 * j:128 * j + 128],
                                                   PM[:, h % 2, 128 * j:128 * j + 128], IDM)
                    last.then_inc(s_pt, 1)

                def values(h):
                    col = C_MV + DH * h if h < MOBA_H else C_SV + DH * ((h - 6) // 3)
                    v = Z[:, :, col:col + DH]
                    pe.wait_ge(s_pe, h0 + h + 1 + 2)
                    pe.wait_ge(s_oe, h0 + h + 1)
                    p, o = PTS[:, h % 2, :], PS[:, 4 + h % 2, :]
                    mm(o[:, 0:64], p[:, 0:128], v[:, 0, :], start=True, stop=True)
                    mm(o[:, 64:128], p[:, 128:256], v[:, 0, :], start=True, stop=False)
                    mm(o[:, 64:128], p[:, 256:384], v[:, 1, :], start=False, stop=True).then_inc(s_o, 1)

                for h in range(14):
                    if h < 12:
                        scores(h)
                    if 1 <= h <= 12:
                        turn(h - 1)
                    if h >= 2:
                        values(h - 2)

                pe.wait_ge(s_lf, l + 1)
                mm(PS[:, 6, 0:4], TRI, GT2[:, 0, :], start=True, stop=True)
                mm(PS[:, 6, 4:8], ONES, GT2[:, 0, :], start=True, stop=False)
                mm(PS[:, 6, 4:8], TRI, GT2[:, 1, :], start=False, stop=True).then_inc(s_b, 1)
                pe.wait_ge(s_dg, l + 1)
                for t in range(NT):
                    last = mm(PS[:, 6 + t, :], ONES, DG[:, t, :, :].rearrange("p h n -> p (h n)"), start=True, stop=True)
                last.then_inc(s_eb, 1)
                pe.wait_ge(s_lqk, l + 1)
                pe.wait_ge(s_oe, h0 + 12 + 2)
                for j, (t, s) in enumerate(((0, 0), (1, 0), (1, 1))):
                    for h in range(ML_H):
                        r = 64 * (h % 2)
                        o = PS[:, 2 * j + h % 2, 128 * (h // 2):128 * (h // 2) + 128]
                        last = mm(o, CV[r:r + 64, h // 2, 128 * t:128 * t + 128],
                                  CV[r:r + 64, 2 + h // 2, 128 * s:128 * s + 128], start=True, stop=True)
                last.then_inc(s_ms3, 1)
                pe.wait_ge(s_mp, l + 1)
                for j in range(3):
                    for h in range(ML_H):
                        last = nc.tensor.transpose(PS[:, 3 + j, 128 * h:128 * h + 128], ME[:, j, h, :], IDM)
                last.then_inc(s_mt, 1)
                pe.wait_ge(s_mtc, l + 1)
                pe.wait_ge(s_v65, l + 1)
                for h in range(ML_H):
                    o0, o1 = PS[:, 6, 65 * h:65 * h + 65], PS[:, 7, 65 * h:65 * h + 65]
                    mm(o0, PTM[:, 0, h, :], V65[:, 0, h, :], start=True, stop=True)
                    mm(o1, PTM[:, 1, h, :], V65[:, 0, h, :], start=True, stop=False)
                    last = mm(o1, PTM[:, 2, h, :], V65[:, 1, h, :], start=False, stop=True)
                last.then_inc(s_mo, 1)

                split_done(transposes(t0 + 1, 4 * t0 + 4, YN, m=L.m_o))
                pe.wait_ge(s_gfree, g0 + 6 + 1)
                half_group(L.c_o, L.c_o, 0, 0)
                mod_columns(L.m_o, (4, 5))
                half_group(L.c_o + 1, L.c_o + 1, 0, 1)
                mod_done(L.m_o)
                group(g0 + 7, L.c_o + 2, L.c_o + 2)
                pe.wait_ge(s_gfree, g0 + 8 + 2)
                split_done(transposes(t0 + 2, 4 * t0 + 8, YN, m=L.m_mlp, banks=(0, 2)))
                mlp(l, L.c_mlp, u0 + 2, L.m_mlp)

            def turn_heads(n, steps):
                for j, (h, bank) in enumerate(steps):
                    pe.wait_ge(s_qc2, n + j + (2 if len(steps) == 1 or j == 2 else 1))
                    for k in range(2):
                        for t in range(NT):
                            last = nc.tensor.transpose(PS[:, bank, 256 * k + 128 * t:256 * k + 128 * t + 128],
                                                       QK2[:, t, h + 2 * k:h + 2 * k + 2, :].rearrange("p h d -> p (h d)"),
                                                       IDM)
                    last.then_inc(s_qt2, 1)

            def gate_rows(n):
                pe.wait_ge(s_dgb, n + 1)
                for j in range(2):
                    last = mm(PS[:, 6 + j, :], ONES, DGB[:, 4 * j:4 * j + 4, :].rearrange("p k n -> p (k n)"),
                              start=True, stop=True)
                last.then_inc(s_gt, 1)

            for q in PASSES:
                c0, g0 = q.c_in, q.g
                qt0 = 3 * q.p + (1 if q.mini else 0)
                if q.mini:
                    split_done(transposes(q.src - 1, q.t - 4, YN))
                    pe.wait_ge(s_gfree, g0 - 1 + 2)
                    tokens_out(q.c - 1, q.c - 1, 2, KT, 256, AH, AL, True, True)
                    pe.wait_ge(s_qw2, q.qk)
                    turn_heads(qt0 - 1, ((8, 6),))
                pe.wait_ge(s_gfree, g0 + 2)
                split_done(transposes(q.src, q.t, YN, m=q.m_in, banks=(0, 2)))
                for k in range(3):
                    pe.wait_ge(s_ufree, q.u + k + 1)
                    features_out(c0 + k, c0 + k, 4 + (q.u + k) % 2, AH, AL)
                    if k == 0:
                        mod_columns(q.m_in, (0, 2))
                    if k == 1:
                        mod_done(q.m_in)
                pe.wait_ge(s_gfree, g0 + 1)
                tokens_out(c0 + 3, c0 + 3, 0, KT, 256, AH, AL, True, True)
                pe.wait_ge(s_gfree, g0 + 2)
                for h in range(2):
                    half_group(c0 + 4 + h, c0 + 4 + h, 1, h)
                pe.wait_ge(s_gfree, g0 + 3)
                tokens_out(c0 + 6, c0 + 6, 0, KT, 256, AH, AL, True, True)
                for f in range(2):
                    for b in range(2):
                        for t in range(NT):
                            tab = CT[:, K_CL + 2 * S * f + S * t:K_CL + 2 * S * f + S * t + S]
                            last = mm(PS[:, 6 + f, 256 * b:256 * b + 256], ZN[:, t, N_F + 128 * b:N_F + 128 * b + 128],
                                      tab, start=t == 0, stop=t == NT - 1)
                last.then_inc(s_fa, 1)
                for k in range(7, 19):
                    if k % 2:
                        pe.wait_ge(s_gfree, g0 + 3 + (k - 7) // 2 + 2)
                    half_group(c0 + k, c0 + k, 0, (k - 7) % 2)
                    if k == 7:
                        pe.wait_ge(s_fac, q.p + 1)
                        for b in range(2):
                            for f in range(2):
                                last = mm(PS[:, 6, 256 * b:256 * b + 256], CT[:, K_BD + 128 * f:K_BD + 128 * f + 128],
                                          A12[:, f, b, :], start=f == 0, stop=f == 1)
                        last.then_inc(s_fy, 1)
                    if k == 9:
                        pe.wait_ge(s_qw2, q.qk + 1)
                        pe.wait_ge(s_fyc, q.p + 1)
                        turn_heads(qt0, ((0, 6), (4, 7), (8, 6)))
                        pe.wait_ge(s_qc2, qt0 + 3 + 2)
                    n = 256 if q.stream else 512
                    for v in units(k):
                        if v < 16:
                            h, t = divmod(v, 2)
                            r = 64 * (h % 2)
                            pe.wait_ge(s_e2, q.att + v + 1)
                            mm(PS[:, 4 + v % 2, 0:n], QT2[r:r + 64, h // 2, 128 * t:128 * t + 128],
                               KTB[r:r + 64, 0 if h // 4 == h % 2 else 1, 2 * S - n if q.stream else 0:2 * S],
                               start=True, stop=True).then_inc(s_s2, 1)
                        if 2 <= v < 18:
                            pe.wait_ge(s_e2, q.att + v - 2 + 1 + 2)
                            pe.wait_ge(s_p2, q.att + v - 2 + 1)
                            for j in range(n // 128):
                                last = nc.tensor.transpose(PS[:, 6 + v % 2, 128 * j:128 * j + 128],
                                                           PM[:, v % 2, 128 * j:128 * j + 128], IDM)
                            last.then_inc(s_t2, 1)
                        if v >= 4:
                            h, t = divmod(v - 4, 2)
                            pe.wait_ge(s_p2, q.att + v - 4 + 1 + 2)
                            pe.wait_ge(s_oe2, q.att + v - 4 + 1)
                            for j in range(n // 128):
                                last = mm(PS[:, 2 + v % 2, 0:DH], PTS[:, v % 2, 128 * j:128 * j + 128],
                                          VB[:, j + 2 * q.stream, DH * (h // 4):DH * (h // 4) + DH],
                                          start=j == 0, stop=j == n // 128 - 1)
                            last.then_inc(s_o2, 1)
                split_done(transposes(q.src + 1, q.t + 4, YA, (2, 3)))
                pe.wait_ge(s_yl, q.p + 1)
                for b in range(2):
                    c = c0 + 19 + b
                    arrived(c)
                    hi, lo = slot(c, 2, D)
                    for half in range(2):
                        pe.wait_ge(s_gfree, g0 + 9 + 2 * b + half + (2 if b == 0 and half == 0 else 1))
                        for t in range(NT):
                            for j in range(2):
                                o, cols = PS[:, 2 * half + t, :], slice(512 * half, 512 * half + 512)
                                th, tl = (w[:, 2 * b + j, 128 * t:128 * t + 128] for w in (AH, AL))
                                mm(o, th, hi[:, j, cols], start=j == 0, stop=False)
                                mm(o, th, lo[:, j, cols], start=False, stop=False)
                                last = mm(o, tl, hi[:, j, cols], start=False, stop=j == 1)
                        last.then_inc(s_used if half else s_bg, 1)
                for half in range(2):
                    pe.wait_ge(s_gfree, g0 + 13 + half + 1)
                    c = c0 + 21 + half
                    tokens_out(c, c, 2 * half, 4, 512, AH[:, 4:8, :], AL[:, 4:8, :], True, True)
                split_done(transposes(q.src + 2, q.t + 6, M2, m=q.m_o))
                gate_rows(2 * q.p)
                for half in range(2):
                    pe.wait_ge(s_gfree, g0 + 15 + half + 1)
                    for h in range(2):
                        half_group(q.c_o + 2 * half + h, q.c_o + 2 * half + h, half, h)
                        if half == 0 and h == 0:
                            mod_columns(q.m_o, (4, 5))
                mod_done(q.m_o)
                pe.wait_ge(s_gfree, g0 + 17 + 2)
                split_done(transposes(q.src + 3, q.t + 10, YN, m=q.m_mlp, banks=(0, 2)))
                gate_rows(2 * q.p + 1)
                mlp(q.mlp, q.c_mlp, q.u + 3, q.m_mlp)


N_CONST = 22
INPUTS = ["x", "ln1", "w_in", "conv_w", "conv_b", "igate_b", "fgate_b", "mlstm_norm", "moba_q_norm", "moba_k_norm",
          "swa_q_norm", "swa_k_norm", "swa_sinks", "w_out", "ln2", "w_up", "w_down", "c_2", "ctx_2", "c_ctx_2",
          "w_mod_2", "b_mod_2", "g_norm1_2", "g_norm2_2", "w_in_2", "w_conv_2", "g_q_2", "g_k_2", "w_conv_out_2",
          "w_four_out_2", "w_attn_out_2", "w_o_2", "w_ff1_2", "w_ff2_2"]


def kernel(**inputs):
    import concourse.bacc as bacc
    from concourse.bass_utils import run_bass_kernel_spmd

    nc = bacc.Bacc("TRN2", target_bir_lowering=False, num_devices=1)
    arrays, args = {}, {}
    for name in INPUTS:
        v = np.ascontiguousarray(inputs[name])
        arrays[f"in_{name}"] = v
        args[name] = nc.dram_tensor(f"in_{name}", v.shape, mybir.dt.from_np(v.dtype), kind="ExternalInput").ap()
    table = shape_constants()
    arrays["constants"] = table
    args["constants"] = nc.dram_tensor("constants", table.shape, F32, kind="ExternalInput").ap()
    pairs = np.tile(np.eye(2, dtype=np.float32), (2, 1))
    arrays["selector"] = pairs
    args["selector"] = nc.dram_tensor("selector", pairs.shape, F32, kind="ExternalInput").ap()
    out = nc.dram_tensor("out", (1, S, D), F32, kind="ExternalOutput").ap()
    build(nc, args, out)
    return run_bass_kernel_spmd(nc, [arrays], core_ids=[0]).results[0]["out"]
```

```python
from contextlib import ExitStack

import numpy as np

import concourse.bass as bass
from concourse import mybir

F32 = mybir.dt.float32
F32R = mybir.dt.float32r
ALU = mybir.AluOpType
ACT = mybir.ActivationFunctionType
AX_X = mybir.AxisListType.X

P = 128
D = 1024
KT = D // P
S = 256
NT = S // P
DEPTH = 2
DH = 64
FF = 4 * D
EPS = 1e-6
ISC = DH ** -0.5

MOBA_H, ML_H, SWA_H, SWA_KV = 6, 4, 6, 2
C_MQ, C_MV, C_SQ, C_SV = 0, 2 * MOBA_H * DH, 3 * MOBA_H * DH, 3 * MOBA_H * DH + (SWA_H + SWA_KV) * DH
C_LQK = C_SV + SWA_KV * DH
C_LV = C_LQK + 2 * ML_H * DH
C_GATE = C_LV + 2 * ML_H * DH
N_IN1 = C_GATE + 2 * ML_H
Z_LV = C_LQK
Z_LO = Z_LV + ML_H * DH
Z_GATE = Z_LO + ML_H * DH
ZW = Z_GATE + 2 * ML_H
NQK = 2 * MOBA_H + SWA_H + SWA_KV
NSL = NQK + SWA_KV

B_X3, B_F, B_Q, B_K, B_G = 0, 768, 1024, 1536, 1792
N_IN2 = B_G + 3 * D
QH, KVH = 8, 2

RAW_N, HL_N = 3, 4
CW = 2048
SPLIT_LEAD = 3
MODC = 4
N1 = 12 + 4 + 32
GR1 = 10
UC1 = 18
CH2 = 59
GR2 = 19
UC2 = 19

N_F, N_Q, N_K, N_V = 0, 256, 768, 896
M_SH, M_SC, M_GT = (0, 24), (8, 32), (16, 40)


class Slot:
    made = 0

    def __init__(self, c, here):
        self.c, self.here, self.n = c, here, MODC if here else 0
        self.g = 2 * Slot.made
        Slot.made += here
        self.next = c + self.n


class Layer:

    def __init__(self, l):
        c = LAYERS[-1].end if l else 0
        self.m_in = Slot(c, l > 0)
        self.c_in = self.m_in.next
        self.m_o = Slot(self.c_in + 12, True)
        self.c_o = self.m_o.next
        self.m_mlp = Slot(self.c_o + 4, True)
        self.c_mlp = self.m_mlp.next
        self.end = self.c_mlp + 32


LAYERS = []
for _l in range(DEPTH):
    LAYERS.append(Layer(_l))


class Pass:

    def __init__(self, p):
        self.p, self.layer, self.stream = p, (0, 0, 1)[p], (1, 0, 0)[p]
        mini = p == 2
        self.mini = mini
        self.c = (PASSES[-1].end if p else LAYERS[-1].end) + mini
        self.m_in = Slot(self.c, p != 1)
        self.mod_banks = (2, 0) if mini else (0, 2)
        self.c_in = self.m_in.next
        self.m_o = Slot(self.c_in + 23, True)
        self.c_o = self.m_o.next
        self.m_mlp = Slot(self.c_o + 4, not mini)
        self.c_mlp = self.m_mlp.next
        self.end = self.c_mlp + 32
        self.g = GR1 * DEPTH + GR2 * p + mini
        self.u = UC1 * DEPTH + UC2 * p
        self.t = 12 * DEPTH + 14 * p + 4 * mini
        self.src = 3 * DEPTH + 4 * p + mini
        self.norm = 2 * DEPTH + 2 * p + mini
        self.pow = 5 * DEPTH + 3 * p + 2 * mini
        self.mlp = DEPTH + p
        self.qk = p + mini
        self.att = 16 * p


QT_BANK = (0, 1, 0, 0, 1, 0)
MT_BANK = (1, 0, 1)

PASSES = []
for _p in range(3):
    PASSES.append(Pass(_p))
assert Slot.made == DEPTH * 6
NO_SLOT = Slot(0, False)


class Early:

    def __init__(self, q, mini):
        self.q, self.stream = q, 1 if mini else q.stream
        self.src, self.t, self.norm, self.pow = ((q.src - 1, q.t - 4, q.norm - 1, q.pow - 2) if mini else
                                                 (q.src, q.t, q.norm, q.pow))


EARLY = {DEPTH - 1: Early(PASSES[0], False), PASSES[0].mlp: Early(PASSES[1], False), PASSES[1].mlp: Early(PASSES[2], True)}
NARROW = [k.c_in for k in LAYERS]

K_ID, K_ONE, K_TRI = 0, 128, 256
K_M = 384
K_R1 = K_M + 512
K_R2 = K_R1 + 128
K_CL = K_R2 + 128
K_BD = K_CL + 4 * S
K_W = K_BD + 256


def shape_constants():
    t = np.zeros((P, K_W), np.float32)
    i = np.arange(P)
    t[:, K_ID:K_ID + P] = np.eye(P)
    t[:, K_ONE:K_ONE + P] = 1.0
    t[:, K_TRI:K_TRI + P] = i[:, None] <= i[None, :]
    low = np.float32(-1e30)
    causal = np.where(i[None, :] > i[:, None], low, 0)
    window = np.where(i[None, :] <= i[:, None], low, 0)
    t[:, K_M + 128:K_M + 256] = causal
    t[:, K_M + 256:K_M + 384] = window
    t[:, K_M + 384:K_M + 512] = causal
    inv = (np.float32(10000.0) ** (-np.arange(0, DH, 2, dtype=np.float32) / np.float32(DH))).astype(np.float32)
    ang = np.arange(S, dtype=np.float32)[:, None] * inv[None, :]
    inv2 = (np.float32(10000.0) ** (-np.arange(16, dtype=np.float32) / np.float32(16))).astype(np.float32)
    rows = np.repeat(np.arange(S // 64, dtype=np.float32)[:, None] * inv2, 64, axis=0)
    cols = np.tile(np.arange(64, dtype=np.float32)[:, None] * inv2, (S // 64, 1))
    ang2 = np.concatenate([rows, cols], axis=1)
    for at, a in ((K_R1, ang), (K_R2, ang2)):
        for f, fn in enumerate((np.cos, np.sin)):
            v = fn(a.astype(np.float32)).astype(np.float32).reshape(NT, P, 32)
            for n in range(NT):
                t[:, at + f * 64 + n * 32:at + f * 64 + n * 32 + 32] = v[n]
    k = np.arange(S)
    w = 2 * np.pi * ((k[:, None] * k[None, :]) % S) / S
    for f, fn in enumerate((np.cos, np.sin)):
        v = (fn(w) / 16.0).astype(np.float32).reshape(NT, P, S)
        for n in range(NT):
            t[:, K_CL + f * 2 * S + n * S:K_CL + f * 2 * S + (n + 1) * S] = v[n]
    k = np.arange(64)
    w = 2 * np.pi * ((k[:, None] * k[None, :]) % 64) / 64
    for f, v in enumerate((np.cos(w) / 8.0, -np.sin(w) / 8.0)):
        for b in range(2):
            t[b * 64:b * 64 + 64, K_BD + f * 128 + b * 64:K_BD + f * 128 + b * 64 + 64] = v
    return t


def build(nc, a, out):
    with ExitStack() as ctx:
        at = [16512]

        def sb(name, shape, dt=F32, where=None):
            size = 4 * int(np.prod(shape[1:]))
            offset = at[0] if where is None else where
            if where is None:
                at[0] += (size + 31) // 32 * 32
            return nc.alloc_sbuf_tensor_at(name, shape, dt, offset=offset)

        def sem(name):
            return ctx.enter_context(nc.semaphore(name))

        RAW = sb("RAW", [P, RAW_N, CW])
        HI = sb("HI", [P, HL_N, CW], F32R)
        LO = sb("LO", [P, HL_N, CW], F32R)
        X = sb("X", [P, NT, D])
        at_ah = at[0]
        AH = sb("AH", [P, KT, S], F32R)
        AL = sb("AL", [P, KT, S], F32R)
        at_yn = at[0]
        YN = sb("YN", [P, NT, D])
        at_z = at[0]
        Z = sb("Z", [P, NT, ZW])
        QKT = sb("QKT", [P, NSL // 2, S])
        GN = sb("GN", [P, DEPTH, 4, DH])
        at[0] = at_z + 32768
        at_pm = at[0]
        PM = sb("PM", [P, 2, 512])
        at_pt = at[0]
        PTS = sb("PTS", [P, 2, 512])
        CT = sb("CT", [P, K_W])
        PAR = sb("PAR", [P, 256])
        MOD = sb("MOD", [P, DEPTH, 48, 2])
        MN = sb("MN", [P, DEPTH, ML_H * DH])
        IFB = sb("IFB", [P, DEPTH, 2 * ML_H])
        SK = sb("SK", [P, DEPTH, SWA_H])
        NSK = sb("NSK", [P, DEPTH, SWA_H])
        GQ2 = sb("GQ2", [P, DEPTH, 2, DH])
        CS = sb("CS", [P, 2, KT])
        C4 = sb("C4", [P, KT, 4], F32R)
        SEL = sb("SEL", [4, 2])
        SGC = sb("SGC", [P, 16])
        SSQ = sb("SSQ", [P, 2, NT])
        MS = sb("MS", [P, 64])
        RS = sb("RS", [P, 64])
        NHALF = sb("NHALF", [P, 64])
        MX = sb("MX", [P, 2, 2])
        NB = sb("NB", [P, MOBA_H + SWA_H, 2])
        SUM = sb("SUM", [P, MOBA_H + SWA_H, 2])
        SKE = sb("SKE", [P, SWA_H, 2])
        RIN = sb("RIN", [P, MOBA_H + SWA_H, 2])
        G8 = sb("G8", [P, NT, 8])
        GT1 = sb("GT1", [P, NT, 4])
        GT2 = sb("GT2", [P, NT, 4])
        ES = sb("ES", [P, NT, 4])
        BS = sb("BS", [P, NT, 4])
        RMX = sb("RMX", [P, 3, 4])
        RR = sb("RR", [P, NT, 4])
        DEN = sb("DEN", [P, NT, 4])
        SCL = sb("SCL", [P, DEPTH, 2, KT, 2])
        NM2 = sb("NM2", [P, QH, 2])
        SM2 = sb("SM2", [P, QH, 2])
        RN2 = sb("RN2", [P, QH, 2])
        at_scratch = at[0]
        QK = sb("QK", [P, NT, NSL, DH])
        HM = sb("HM", [P, NT, ML_H * DH], F32, at_scratch)
        XP = sb("XP", [P, 4, S + 3])
        CV = sb("CV", [P, 4, S])
        ME = sb("ME", [P, 3, ML_H, P])
        at_ptm = at[0]
        PTM = sb("PTM", [P, 3, ML_H, P])
        V65 = sb("V65", [P, NT, ML_H, DH + 1], F32, at_ah)
        PR0 = sb("PR0", [P, P], F32, at_z)
        PR1 = sb("PR1", [P, P], F32, at_z + 512)
        ROWS = sb("ROWS", [P, 2, 512], F32, at_yn)
        TMP = sb("TMP", [P, 2, 512], F32, at_pm)
        U2 = sb("U2", [P, 2, 512], F32, at_pm)
        RL = sb("RL", [P, 2, 512], F32, at_pt)
        DG = sb("DG", [P, NT, ML_H, P], F32, at_ptm)
        SG = sb("SG", [P, 4, S], F32, at_ptm)
        SO = sb("SO", [P, NT, ML_H * DH], F32, at_ptm)
        HIDH = sb("HIDH", [P, 2, 4, S], F32R, at_z)
        HIDL = sb("HIDL", [P, 2, 4, S], F32R, at_z + 8192)
        GA = sb("GA", [P, NT, 3 * D], F32, at_z)
        ZN = sb("ZN", [P, NT, 1024], F32, at_z + 24576)
        M2 = sb("M2", [P, NT, D], F32, at_z + 24576)
        A12 = sb("A12", [P, 2, 2, S], F32, at_yn)
        YA = sb("YA", [P, NT, 512], F32, at_yn + 4096)
        UB = sb("UB", [P, 3, 2, S], F32, at_pm)
        TM = sb("TM", [P, 2, 512], F32, at_pt)
        DGB = sb("DGB", [P, 8, P], F32, at_pt)
        at_end = at[0]
        at[0] = at_scratch
        CTX = sb("CTX", [P, NT, D])
        QK2 = sb("QK2", [P, NT, 12, DH])
        at_qt2 = at[0]
        QT2 = sb("QT2", [P, 4, S])
        KTB = sb("KTB", [P, 2, 2 * S])
        VB = sb("VB", [P, 2 * NT, P])
        GTB = sb("GTB", [P, D], F32, at_qt2)
        CXP = sb("CXP", [P, 2, S + 2])
        YC = sb("YC", [P, 2, S])
        YF = sb("YF", [P, 2, S])
        at[0] = max(at_end, at[0])
        assert at[0] <= nc.sbuf_usable_end, at[0]
        IDM = CT[:, K_ID:K_ID + P]
        ONES = CT[:, K_ONE:K_ONE + P]
        TRI = CT[:, K_TRI:K_TRI + P]

        PS = ctx.enter_context(nc.psum_tensor("PS", [P, 8, 512], F32))

        s_cst = sem("constants_loaded")
        s_row = sem("parameter_rows_loaded")
        s_xin = sem("x_loaded")
        s_raw = [sem(f"raw_loaded_{i}") for i in range(RAW_N)]
        s_hi = sem("chunk_high_done")
        s_lo = sem("chunk_split_done")
        s_used = sem("chunk_used")
        s_gfree = sem("group_evacuated")
        s_ufree = sem("ubank_evacuated")
        s_mrow = sem("mod_rows_copied")
        s_mcol = sem("mod_columns")
        s_modc = sem("mod_copied")
        s_c4 = sem("silu_c_split")
        s_sel = sem("selector_loaded")
        s_init = sem("pool_constants")
        s_par = sem("params_transposed")
        s_parc = sem("params_copied")
        s_cs = sem("silu_c")
        s_av = sem("act_chain")
        s_dv = sem("dve_chain")
        s_ss = sem("sum_squares")
        s_ms = sem("mean_squares")
        s_rs = sem("rstd_done")
        s_src = sem("transpose_source")
        s_tp = sem("transposed")
        s_thi = sem("activation_high")
        s_tlo = sem("activation_low")
        s_sq = sem("qk_squares")
        s_qk = sem("qk_rotated")
        s_qsw = sem("qk_swapped_copied")
        s_qt = sem("qk_transposed")
        s_qtc = sem("qk_transposed_copied")
        s_s = sem("scores")
        s_sm = sem("scores_masked")
        s_nb = sem("row_max")
        s_e = sem("exp_done")
        s_pt = sem("probs_transposed")
        s_pe = sem("probs_copied")
        s_o = sem("head_output")
        s_oe = sem("head_output_copied")
        s_ske = sem("sink_in")
        s_sko = sem("sink_exp")
        s_cv = sem("conv_done")
        s_sg = sem("conv_sigmoid")
        s_lqk = sem("mlstm_qk")
        s_ga = sem("gate_abs")
        s_gl = sem("gate_log")
        s_lf = sem("log_forget")
        s_b = sem("cum_forget")
        s_dg = sem("diag_e")
        s_eb = sem("e_rows")
        s_me = sem("mlstm_exponent")
        s_mex = sem("mlstm_weights")
        s_mem = sem("mlstm_stabilizer")
        s_exm = sem("mlstm_floor")
        s_ms3 = sem("mlstm_scores")
        s_mp = sem("mlstm_probs")
        s_mt = sem("mlstm_transposed")
        s_mtc = sem("mlstm_transposed_copied")
        s_mo = sem("mlstm_output")
        s_h = sem("mlstm_h")
        s_hsq = sem("mlstm_h_squares")
        s_v65 = sem("mlstm_values")
        s_so = sem("output_gate")
        s_rl = sem("hidden_relu")
        s_u2 = sem("hidden_square")
        s_hh = sem("hidden_high")
        s_hl = sem("hidden_low")
        s_out = sem("result_written")
        s_ctx = sem("ctx_loaded")
        s_scl = sem("norm_scales")
        s_pad = sem("conv_pads")
        s_sq2 = sem("qk2_squares")
        s_qk2 = sem("qk2_normed")
        s_qw2 = sem("qk2_swapped_copied")
        s_qt2 = sem("qk2_transposed")
        s_qc2 = sem("qk2_transposed_copied")
        s_fa = sem("dft_tokens")
        s_fac = sem("dft_tokens_copied")
        s_fy = sem("dft_channels")
        s_fyc = sem("fourier_branch")
        s_yc = sem("conv_branch")
        s_yh = sem("branches_high")
        s_yl = sem("branches_low")
        s_s2 = sem("scores2")
        s_n2 = sem("row_max2")
        s_e2 = sem("exp2_done")
        s_t2 = sem("probs2_transposed")
        s_p2 = sem("probs2_copied")
        s_o2 = sem("head2_output")
        s_oe2 = sem("head2_output_copied")
        s_bg = sem("branch_half_done")
        s_dgb = sem("gate_diagonals")
        s_gt = sem("gate_rows")
        s_gtc = sem("gate_rows_copied")

        def tiled(w, l, r, kt, c, n):
            return w[l, r:r + kt * P, c:c + n].rearrange("(a p) n -> p a n", p=P)

        def mlp_chunks(up, down, l):
            for i in range(4):
                for j in (2 * i, 2 * i + 1):
                    for h in range(2):
                        yield tiled(up, l, 0, KT, 512 * j + 256 * h, 256), KT, 256
                for j in (2 * i, 2 * i + 1):
                    for h in range(2):
                        yield tiled(down, l, 512 * j, 4, 512 * h, 512), 4, 512

        def halves(w, l, c):
            for h in range(2):
                yield tiled(w, l, 512 * h, 4, c, 512), 4, 512

        def mod_chunks(m):
            if m.here:
                for j in (m.g, m.g + 1):
                    yield from halves(a["w_mod_2"], j // 12, 512 * (j % 12))

        def chunks1(l):
            w = a["w_in"]
            yield from mod_chunks(LAYERS[l].m_in)
            yield tiled(w, l, 0, KT, C_GATE, 8), KT, 8
            for c in (C_LQK, C_LQK + 256):
                yield tiled(w, l, 0, KT, c, 256), KT, 256
            for c in (0, 512, 1024):
                yield from halves(w, l, c)
            yield tiled(w, l, 0, KT, 1536, 256), KT, 256
            yield from halves(w, l, C_LV)
            yield from mod_chunks(LAYERS[l].m_o)
            for c in (0, 512):
                yield from halves(a["w_out"], l, c)
            yield from mod_chunks(LAYERS[l].m_mlp)
            yield from mlp_chunks(a["w_up"], a["w_down"], l)

        def chunk_words(c):
            return KT * 8 if c in NARROW else CW

        def chunks2(q):
            w, l = a["w_in_2"], q.layer
            if q.mini:
                yield tiled(w, l, 0, KT, B_K, 256), KT, 256
            yield from mod_chunks(q.m_in)
            for c in (0, 256, 512, B_F):
                yield tiled(w, l, 0, KT, c, 256), KT, 256
            yield from halves(w, l, B_Q)
            yield tiled(w, l, 0, KT, B_K, 256), KT, 256
            for j in range(6):
                yield from halves(w, l, B_G + 512 * j)
            for name in ("w_conv_out_2", "w_four_out_2"):
                yield tiled(a[name], l, 0, 2, 0, D), 2, D
            for j in range(2):
                yield tiled(a["w_attn_out_2"], l, 0, 4, 512 * j, 512), 4, 512
            yield from mod_chunks(q.m_o)
            for j in range(2):
                yield from halves(a["w_o_2"], l, 512 * j)
            yield from mod_chunks(q.m_mlp)
            yield from mlp_chunks(a["w_ff1_2"], a["w_ff2_2"], l)

        LP = PASSES[-1]
        NCH = LP.end

        def vector_scales(s, shift):
            return shift is None or s % 2 == 1

        def scaled_by(e):
            return norm_scale(e.q, 0, e.stream)

        def norm_scale(q, n, stream):
            return (lambda k: SCL[:, q.layer, n, k, stream:stream + 1],
                    lambda k: MOD[:, q.layer, M_SH[n] + k, stream:stream + 1])

        UNITS = (0, 3, 6, 9, 11, 13, 15, 17, 20)

        def units(k):
            return range(*UNITS[k - 11:k - 9]) if k >= 11 else ()

        block = ctx.enter_context(nc.Block())

        @block.sync
        def _(sp):
            sp.dma_start(X[:, :, :], a["x"][0].rearrange("(t p) d -> p t d", p=P)).then_inc(s_xin, 16)

            def load(c, src, kt, n):
                sp.wait_ge(s_lo, c + 1)
                if c == 1:
                    sp.wait_ge(s_cst, 16 * N_CONST)
                dst = RAW[:, c % RAW_N, 0:kt * n].rearrange("p (a n) -> p a n", a=kt)
                sp.dma_start(dst, src).then_inc(s_raw[c % RAW_N], 16)

            n_row = [0]

            def rows(dst, src):
                sp.dma_start(dst, src.partition_broadcast(P)).then_inc(s_row, 16)
                n_row[0] += 1

            def parameter_rows():
                sp.dma_start(CT[:, K_M:K_W], a["constants"][:, K_M:K_W]).then_inc(s_row, 16)
                for i, name in enumerate(("moba_q_norm", "moba_k_norm", "swa_q_norm", "swa_k_norm")):
                    rows(GN[:, :, i, :], a[name])
                rows(MN[:, :, :], a["mlstm_norm"].rearrange("l h d -> l (h d)"))
                rows(IFB[:, :, 0:4], a["igate_b"])
                rows(IFB[:, :, 4:8], a["fgate_b"])
                rows(SK[:, :, :], a["swa_sinks"])
                for i, name in enumerate(("g_q_2", "g_k_2")):
                    rows(GQ2[:, :, i, :], a[name])

            for l in range(DEPTH):
                for k, (src, kt, n) in enumerate(chunks1(l)):
                    c = LAYERS[l].m_in.c + k
                    load(c, src, kt, n)
                    if c == RAW_N - 1:
                        parameter_rows()
                        assert n_row[0] + 1 == N_ROWS
                    if c == LAYERS[-1].c_mlp:
                        sp.wait_ge(s_src, 3 * l + 2)
                        sp.dma_start(CTX[:, :, :], a["ctx_2"][0].rearrange("(t p) d -> p t d", p=P)).then_inc(s_ctx, 16)
            for q in PASSES:
                for k, (src, kt, n) in enumerate(chunks2(q)):
                    c = q.c - q.mini + k
                    load(c, src, kt, n)
            sp.wait_ge(s_out, 32)

        @block.gpsimd
        def _(pool):
            nc.gpsimd.memset(NHALF[:, :], -0.5)
            nc.gpsimd.memset(XP[:, :, 0:3], 0.0).then_inc(s_init, 1)
            pool.wait_ge(s_init, 1)

            def rsqrt(n, width):
                pool.wait_ge(s_ms, n + 1)
                nc.gpsimd.tensor_tensor(RS[:, 0:width], MS[:, 0:width], NHALF[:, 0:width], ALU.pow).then_inc(s_rs, 1)

            for l in range(DEPTH):
                for j, width in enumerate((2, 24, 2 * (NQK - 12), 8, 2)):
                    rsqrt(5 * l + j, width)
            pool.wait_ge(s_src, 3 * DEPTH - 1)
            nc.gpsimd.memset(CXP[:, :, 0:1], 0.0)
            nc.gpsimd.memset(CXP[:, :, S + 1:S + 2], 0.0).then_inc(s_pad, 1)
            for q in PASSES:
                if q.mini:
                    rsqrt(q.pow - 2, 2)
                    rsqrt(q.pow - 1, 2)
                for j, width in enumerate((2 * KVH if q.mini else 2, 2 * (QH + KVH), 2)):
                    rsqrt(q.pow + j, width)

        @block.scalar
        def _(act):
            def cast(dst, src):
                return nc.scalar.copy(dst, src)

            chain = [0]

            def link(ins):
                chain[0] += 1
                ins.then_inc(s_av, 1)
                act.wait_ge(s_av, chain[0])

            n_cst = [0]

            def const(dst, src):
                act.dma_start(dst, src).then_inc(s_cst, 16)
                n_cst[0] += 1

            const(CT[:, 0:K_M], a["constants"][:, 0:K_M])
            for name, row, n in (("ln1", 0, 16), ("ln2", 16, 16), ("g_norm1_2", 32, 16), ("g_norm2_2", 48, 16)):
                const(PR0[row:row + n, :], a[name].rearrange("l (k p) -> (l k) p", p=P))
            const(PR0[64:72, :], a["c_2"].rearrange("l (k p) -> (l k) p", p=P))
            const(PR0[72:80, :], a["c_ctx_2"].rearrange("(k p) -> k p", p=P))
            const(PR0[80:112, :], a["conv_w"].rearrange("l j (k p) -> (l j k) p", p=P))
            const(PR0[112:120, :], a["conv_b"].rearrange("l (k p) -> (l k) p", p=P))
            const(PR1[0:96, :], a["b_mod_2"].rearrange("l (k p) -> (l k) p", p=P))
            const(PR1[96:108, :], a["w_conv_2"].rearrange("l j (k p) -> (l j k) p", p=P))

            const(SEL[:, :], a["selector"])
            assert n_cst[0] == N_CONST

            def parameters():
                act.wait_ge(s_par, 1)
                cast(PAR[:, 0:120], PS[:, 6, 0:120])
                cast(PAR[:, 128:236], PS[:, 7, 0:108]).then_inc(s_parc, 1)
                act.wait_ge(s_parc, 1)

            def silu_c():
                nc.scalar.activation(SGC[:, :], PAR[:, 64:80], ACT.Sigmoid).then_inc(s_cs, 1)
                act.wait_ge(s_cs, 2)
                cast(C4[:, :, 0:2], CS[:, :, :].rearrange("p s k -> p k s")).then_inc(s_c4, 1)

            def split(c):
                act.wait_ge(s_raw[c % RAW_N], 16 * (c // RAW_N + 1))
                act.wait_ge(s_used, c + 1)
                n = chunk_words(c)
                cast(HI[:, c % HL_N, 0:n], RAW[:, c % RAW_N, 0:n]).then_inc(s_hi, 1)

            def ahead(c):
                if c + SPLIT_LEAD < NCH:
                    split(c + SPLIT_LEAD)

            def sum_squares(src, free=None, m=NO_SLOT):
                for half in range(2):
                    if half:
                        spare(m, 0)
                    if free:
                        act.wait_ge(s_gfree, free - 1 + half)
                    cols = slice(512 * half, 512 * half + 512)
                    for t in range(NT):
                        last = nc.scalar.activation(YN[:, t, cols], src[:, t, cols], ACT.Square, scale=D ** -0.5,
                                                    accum_out=SSQ[:, half, t:t + 1])
                last.then_inc(s_ss, 1)

            def high(n, scale=None, shift=None, steps=range(4)):
                for s in steps:
                    act.wait_ge(s_tp, n + s - steps[0] + 1)
                    dst = AH[:, 2 * s:2 * s + 2, :].rearrange("p a n -> p (a n)")
                    if scale is None:
                        cast(dst, PS[:, 6 + s % 2, :]).then_inc(s_thi, 1)
                        continue
                    whole = vector_scales(s, shift)
                    out = dst if whole else TMP[:, s % 2, :]
                    for j in range(2):
                        last = nc.scalar.activation(out[:, 256 * j:256 * j + 256],
                                                    PS[:, 6 + s % 2, 256 * j:256 * j + 256], ACT.Identity,
                                                    scale=scale(2 * s + j),
                                                    bias=0.0 if shift is None else shift(2 * s + j))
                    if whole:
                        last.then_inc(s_thi, 1)
                    else:
                        link(last)
                        cast(dst, TMP[:, s % 2, :]).then_inc(s_thi, 1)

            def copy_group(pair, c, dst, n):
                act.wait_ge(s_used, c + 1 + HL_N)
                for t in range(NT):
                    last = cast(dst[:, t, :], PS[:, 2 * pair + t, 0:n])
                last.then_inc(s_gfree, 1)

            def spare(m, j):
                if m.here:
                    ahead(m.c + j)

            def rows_out(m, banks):
                if m.here:
                    for j in range(2):
                        act.wait_ge(s_used, m.c + 2 * j + 2 + HL_N)
                        cast(ROWS[0:4, j, :], PS[0:4, banks[j], :]).then_inc(s_mrow, 1)
                    ahead(m.c + 2)
                    ahead(m.c + 3)

            def mlp(q, c, u):
                e = EARLY.get(q)
                for i in range(4):
                    for j in range(8):
                        ahead(c + 8 * i + j)
                        if e and i == 2 and j == 4:
                            if e.q.p == 0:
                                act.wait_ge(s_ctx, 16)
                            sum_squares(CTX if e.stream else X)
                        if e and i == 3 and j == 5:
                            act.wait_ge(s_hl, 16 * q + 16)
                            act.wait_ge(s_scl, 2 * e.q.layer + 1)
                            high(e.t, *scaled_by(e), steps=(0, 1))
                        if e and i == 3 and j > 5:
                            high(e.t + j - 4, *scaled_by(e), steps=(j - 4,))
                        if j < 4:
                            act.wait_ge(s_used, c + 8 * i + j + 1 + HL_N)
                            nc.scalar.activation(RL[:, j % 2, :], PS[:, 4 + (u + j) % 2, :], ACT.Relu).then_inc(s_rl, 1)
                            act.wait_ge(s_rl, 16 * q + 4 * i + j + 1)
                            nc.scalar.activation(HIDH[:, j // 2, 2 * (j % 2):2 * (j % 2) + 2, :].rearrange("p a n -> p (a n)"),
                                                 RL[:, j % 2, :], ACT.Square).then_inc(s_hh, 1)


            for l in range(DEPTH):
                L = LAYERS[l]
                c0, g0, u0, t0, h0 = L.c_in, GR1 * l, UC1 * l, 3 * l, 12 * l
                if l == 0:
                    act.wait_ge(s_xin, 16)
                    sum_squares(X)
                else:
                    sum_squares(X, g0 + 2, L.m_in)
                if l == 0:
                    parameters()
                    split(0)
                spare(L.m_in, 1)
                high(4 * t0, lambda k: PAR[:, 8 * l + k:8 * l + k + 1])
                if l == 0:
                    for c in range(1, SPLIT_LEAD):
                        split(c)
                    silu_c()
                rows_out(L.m_in, (2, 3))
                for k in range(12):
                    ahead(c0 + k)
                    if k == 0:
                        copy_group(0, c0, Z[:, :, Z_GATE:ZW], 8)
                    if k in (1, 2):
                        act.wait_ge(s_used, c0 + k + 1 + HL_N)
                        j = k - 1
                        cast(XP[:, 2 * j:2 * j + 2, 3:3 + S],
                             PS[:, 4 + j, :].rearrange("p (a n) -> p a n", a=2)).then_inc(s_ufree, 1)
                    if k == 1:
                        act.wait_ge(s_ga, l + 1)
                        link(nc.scalar.activation(GT1[:, :, :], GT1[:, :, :], ACT.Exp))
                        nc.scalar.activation(GT1[:, :, :], GT1[:, :, :], ACT.Ln, bias=1.0).then_inc(s_gl, 1)
                    if k in (4, 6, 8):
                        j = (k - 4) // 2
                        copy_group(1 - j % 2, c0 + k, Z[:, :, 512 * j:512 * j + 512], 512)
                    if k == 6:
                        act.wait_ge(s_gfree, g0 + 5)
                        nc.scalar.activation(QK[:, :, 0:12, :].rearrange("p t h d -> p t (h d)"),
                                             Z[:, :, 0:768], ACT.Square).then_inc(s_sq, 1)
                        act.wait_ge(s_me, l + 1)
                        nc.scalar.activation(ME[:, :, :, :], ME[:, :, :, :], ACT.Exp).then_inc(s_mex, 1)
                        act.wait_ge(s_mem, l + 1)
                        nc.scalar.activation(GT2[:, :, :], GT2[:, :, :], ACT.Exp, scale=-1.0).then_inc(s_exm, 1)
                    if k == 8:
                        act.wait_ge(s_cv, l + 1)
                        nc.scalar.activation(SG[:, :, :], CV[:, :, :], ACT.Sigmoid).then_inc(s_sg, 1)
                    if k == 9:
                        copy_group(0, c0 + k, Z[:, :, 1536:1792], 256)
                        act.wait_ge(s_gfree, g0 + 7)
                        nc.scalar.activation(QK[:, :, 12:NQK, :].rearrange("p t h d -> p t (h d)"),
                                             Z[:, :, C_SQ:C_SV], ACT.Square).then_inc(s_sq, 1)
                    if k == 11:
                        copy_group(1, c0 + k, Z[:, :, Z_LV:Z_GATE], 512)
                        act.wait_ge(s_gfree, g0 + 8)
                        cast(V65[:, :, :, DH:DH + 1], ONES[:, 0:NT * ML_H].rearrange("p (t h d) -> p t h d", t=NT, d=1))
                        cast(V65[:, :, :, 0:DH],
                             Z[:, :, Z_LV:Z_LO].rearrange("p t (h d) -> p t h d", h=ML_H)).then_inc(s_v65, 1)
                        nc.scalar.activation(Z[:, :, Z_LO:Z_GATE], Z[:, :, Z_LO:Z_GATE], ACT.Sigmoid).then_inc(s_so, 1)

                def turned(j):
                    w = 512 if j < 5 else 256
                    act.wait_ge(s_qt, 6 * l + j + 1)
                    cast(QKT[:, 2 * j:2 * j + w // 256, :].rearrange("p a n -> p (a n)"),
                         PS[:, 6 + QT_BANK[j], 0:w]).then_inc(s_qtc, 1)

                def weights_turned(j):
                    act.wait_ge(s_mt, 3 * l + j + 1)
                    cast(PTM[:, j, :, :].rearrange("p a n -> p (a n)"), PS[:, 6 + MT_BANK[j], :]).then_inc(s_mtc, 1)

                for j in range(3):
                    turned(j)

                def exps(h):
                    act.wait_ge(s_nb, h0 + h + 1)
                    nc.scalar.activation(PM[:, h % 2, 0:128], PM[:, h % 2, 0:128], ACT.Exp, scale=ISC,
                                         bias=NB[:, h, 0:1], accum_out=SUM[:, h, 0:1])
                    nc.scalar.activation(PM[:, h % 2, 128:384], PM[:, h % 2, 128:384], ACT.Exp, scale=ISC,
                                         bias=NB[:, h, 1:2], accum_out=SUM[:, h, 1:2]).then_inc(s_e, 1)

                def head_out(h):
                    act.wait_ge(s_o, h0 + h + 1 + 2)
                    col = DH * h if h < MOBA_H else DH * (h + ML_H)
                    cast(YN[:, :, col:col + DH],
                         PS[:, 4 + h % 2, 0:128].rearrange("p (t d) -> p t d", t=2)).then_inc(s_oe, 1)

                for h in range(14):
                    if h < 12:
                        exps(h)
                    if h >= 2:
                        head_out(h - 2)
                    if h == 1:
                        weights_turned(0)
                        weights_turned(1)
                    if h == 2:
                        weights_turned(2)
                    if h == 3:
                        act.wait_ge(s_qk, 2 * l + 2)
                        cast(QK[:, :, NQK, :], QK[:, :, NQK - 1, :])
                        cast(QK[:, :, NQK + 1, :], QK[:, :, NQK - 2, :]).then_inc(s_qsw, 1)
                    if h == 4:
                        turned(3)
                    if h == 5:
                        turned(4)
                        turned(5)
                    if h == 8:
                        act.wait_ge(s_h, l + 1)
                        nc.scalar.activation(CV[:, 0:2, :], HM[:, :, :], ACT.Square).then_inc(s_hsq, 1)
                    if h == 12:
                        act.wait_ge(s_ske, l + 1)
                        nc.scalar.activation(SKE[:, :, :], SKE[:, :, :], ACT.Exp).then_inc(s_sko, 1)

                spare(L.m_o, 0)
                spare(L.m_o, 1)
                high(4 * t0 + 4)
                rows_out(L.m_o, (4, 5))
                for k in range(4):
                    ahead(L.c_o + k)
                sum_squares(X, g0 + 8 + 2, L.m_mlp)
                spare(L.m_mlp, 1)
                high(4 * t0 + 8, lambda k: PAR[:, 16 + 8 * l + k:17 + 8 * l + k])
                rows_out(L.m_mlp, (0, 2))
                mlp(l, L.c_mlp, u0 + 2)

            def keys_out(qk, j, ctx):
                act.wait_ge(s_qt2, j + 1)
                cast(KTB[:, :, S * ctx:S * ctx + S],
                     PS[:, 6, :].rearrange("p (a n) -> p a n", a=2)).then_inc(s_qc2, 1)

            def gate_rows(n, banks):
                act.wait_ge(s_gt, n + 1)
                cast(GTB[:, 0:512], PS[:, banks[0], :])
                cast(GTB[:, 512:1024], PS[:, banks[1], :]).then_inc(s_gtc, 1)

            for q in PASSES:
                c0, g0, R = q.c_in, q.g, CTX if q.stream else X
                if q.mini:
                    ahead(q.c - 1)
                    sum_squares(X, q.g - 1 + 2)
                    copy_group(0, q.c - 1, ZN[:, :, N_K:1024], 256)
                    act.wait_ge(s_gfree, q.g + 2)
                    cast(VB[:, 2:4, :], ZN[:, :, N_V:1024])
                    nc.scalar.activation(QK2[:, :, 8:10, :].rearrange("p t h d -> p t (h d)"), ZN[:, :, N_K:N_V],
                                         ACT.Square).then_inc(s_sq2, 1)
                    spare(q.m_in, 0)
                if q.p == 0:
                    spare(q.m_in, 0)
                spare(q.m_in, 1)
                if q.mini:
                    high(q.t, *norm_scale(q, 0, q.stream))
                if q.mini:
                    act.wait_ge(s_qk2, q.qk)
                    cast(QK2[:, :, 10, :], QK2[:, :, 9, :])
                    cast(QK2[:, :, 11, :], QK2[:, :, 8, :]).then_inc(s_qw2, 1)
                rows_out(q.m_in, q.mod_banks)
                qt0 = 3 * q.p + (1 if q.mini else 0)
                for k in range(19):
                    ahead(c0 + k)
                    if k == 18:
                        act.wait_ge(s_yc, q.p + 1)
                        act.wait_ge(s_fyc, q.p + 1)
                        act.wait_ge(s_used, c0 + 18 + HL_N)
                        cast(AH[:, 0:2, :], YC[:, :, :])
                        cast(AH[:, 2:4, :], YF[:, :, :]).then_inc(s_yh, 1)
                    if k == 0 and not q.mini:
                        act.wait_ge(s_gfree, q.g + 2)
                    if k < 3:
                        act.wait_ge(s_used, c0 + k + 1 + HL_N)
                        cast(UB[:, k, :, :].rearrange("p a n -> p (a n)"), PS[:, 4 + (q.u + k) % 2, :]).then_inc(s_ufree, 1)
                    if k == 0 and q.mini:
                        keys_out(q.qk - 1, 3 * (q.qk - 1), 1)
                    if k == 3:
                        copy_group(0, c0 + k, ZN[:, :, N_F:N_Q], 256)
                    if k == 5:
                        copy_group(1, c0 + k, ZN[:, :, N_Q:N_K], 512)
                    if k == 6:
                        copy_group(0, c0 + k, ZN[:, :, N_K:1024], 256)
                        act.wait_ge(s_gfree, g0 + 3 + 2)
                        nc.scalar.activation(QK2[:, :, 0:10, :].rearrange("p t h d -> p t (h d)"), ZN[:, :, N_Q:N_V],
                                             ACT.Square).then_inc(s_sq2, 1)
                        cast(VB[:, 2 * q.stream:2 * q.stream + 2, :], ZN[:, :, N_V:1024])
                        act.wait_ge(s_fa, q.p + 1)
                        for j in range(2):
                            last = cast(A12[:, j, :, :].rearrange("p a n -> p (a n)"), PS[:, 6 + j, :])
                        last.then_inc(s_fac, 1)
                    if k == 7:
                        act.wait_ge(s_fy, q.p + 1)
                        cast(YF[:, :, :].rearrange("p a n -> p (a n)"), PS[:, 6, :]).then_inc(s_fyc, 1)
                    if k >= 8 and k % 2 == 0:
                        j = k // 2 - 4
                        act.wait_ge(s_used, c0 + k + 1 + HL_N)
                        for t in range(NT):
                            last = nc.scalar.activation(GA[:, t, 512 * j:512 * j + 512], PS[:, t, :], ACT.Tanh, scale=0.5)
                        last.then_inc(s_gfree, 1)
                    if k == 10:
                        act.wait_ge(s_qk2, q.qk + 1)
                        cast(QK2[:, :, 10, :], QK2[:, :, 9, :])
                        cast(QK2[:, :, 11, :], QK2[:, :, 8, :]).then_inc(s_qw2, 1)
                        for j in range(2):
                            act.wait_ge(s_qt2, qt0 + j + 1)
                            cast(QT2[:, 2 * j:2 * j + 2, :].rearrange("p a n -> p (a n)"),
                                 PS[:, 6 + j, :]).then_inc(s_qc2, 1)
                        keys_out(q.qk, qt0 + 2, q.stream)
                    for v in units(k):
                        if v < 16:
                            h, t = divmod(v, 2)
                            n = 256 if q.stream else 512
                            act.wait_ge(s_n2, q.att + v + 1)
                            act.wait_ge(s_t2, q.att + v + 1)
                            nc.scalar.activation(PM[:, v % 2, 0:n], PS[:, 4 + v % 2, 0:n], ACT.Exp,
                                                 bias=NM2[:, h, t:t + 1], accum_out=SM2[:, h, t:t + 1]).then_inc(s_e2, 1)
                        if v >= 4:
                            h, t = divmod(v - 4, 2)
                            act.wait_ge(s_o2, q.att + v - 4 + 1 + 2)
                            cast(YA[:, t, DH * h:DH * h + DH], PS[:, 2 + v % 2, 0:DH]).then_inc(s_oe2, 1)
                for k in range(19, 23):
                    ahead(c0 + k)
                    if k == 19:
                        high(q.t + 4, steps=(2, 3))
                spare(q.m_o, 0)
                spare(q.m_o, 1)
                high(q.t + 6)
                gate_rows(2 * q.p, (2, 3))
                rows_out(q.m_o, (4, 5))
                for k in range(4):
                    ahead(q.c_o + k)
                sum_squares(R, g0 + 17 + 2, q.m_mlp)
                spare(q.m_mlp, 1)
                act.wait_ge(s_scl, 2 * q.layer + 2)
                high(q.t + 10, *norm_scale(q, 1, q.stream))
                gate_rows(2 * q.p + 1, (1, 3))
                rows_out(q.m_mlp, (0, 2))
                mlp(q.mlp, q.c_mlp, q.u + 3)

            for half in range(2):
                act.wait_ge(s_gfree, LP.g + GR2 - 1 + half + 2)
                cols = slice(512 * half, 512 * half + 512)
                act.dma_start(out[0].rearrange("(t p) d -> p t d", p=P)[:, :, cols], X[:, :, cols]).then_inc(s_out, 16)
            act.wait_ge(s_out, 32)

        @block.vector
        def _(dve):
            chain = [0]

            def link(ins):
                chain[0] += 1
                ins.then_inc(s_dv, 1)
                dve.wait_ge(s_dv, chain[0])

            tt, ts, stt = nc.vector.tensor_tensor, nc.vector.tensor_scalar, nc.vector.scalar_tensor_tensor
            for s, n in ((s_lo, RAW_N), (s_used, HL_N), (s_gfree, 2), (s_ufree, 2), (s_tlo, 2), (s_qtc, 2), (s_sm, 2), (s_pt, 2), (s_pe, 2), (s_o, 2), (s_oe, 2),
                         (s_qc2, 2), (s_e2, 2), (s_t2, 2), (s_p2, 2), (s_o2, 2), (s_oe2, 2)):
                dve.sem_inc(s, n)

            def split(c):
                dve.wait_ge(s_hi, c + 1)
                n = chunk_words(c)
                tt(LO[:, c % HL_N, 0:n], RAW[:, c % RAW_N, 0:n], HI[:, c % HL_N, 0:n].bitcast(F32),
                   ALU.subtract).then_inc(s_lo, 1)

            def ahead(c):
                if c + SPLIT_LEAD < NCH:
                    split(c + SPLIT_LEAD)

            def norm(n, m, src):
                dve.wait_ge(s_ss, n + 1)
                stt(MS[:, 0:2], SSQ[:, 0, :], EPS, SSQ[:, 1, :], ALU.add, ALU.add).then_inc(s_ms, 1)
                dve.wait_ge(s_rs, m + 1)
                for t in range(NT):
                    last = ts(YN[:, t, :], src[:, t, :], RS[:, t:t + 1], None, ALU.mult)
                last.then_inc(s_src, 1)

            def low(n, scale=None, shift=None, steps=range(4)):
                for s in steps:
                    d = 2 * s
                    hi = AH[:, d:d + 2, :].rearrange("p a n -> p (a n)").bitcast(F32)
                    lo = AL[:, d:d + 2, :].rearrange("p a n -> p (a n)")
                    dve.wait_ge(s_thi, n + s - steps[0] + 1)
                    full = PS[:, 6 + s % 2, :] if scale is None else TMP[:, s % 2, :]
                    if scale is not None and shift is not None and vector_scales(s, shift):
                        for j in range(2):
                            last = ts(TMP[:, s % 2, 256 * j:256 * j + 256], PS[:, 6 + s % 2, 256 * j:256 * j + 256],
                                      scale(d + j), shift(d + j), ALU.mult, ALU.add)
                        link(last)
                    if scale is not None and shift is None:
                        for j in range(2):
                            last = stt(lo[:, 256 * j:256 * j + 256], PS[:, 6 + s % 2, 256 * j:256 * j + 256],
                                       scale(d + j), hi[:, 256 * j:256 * j + 256], ALU.mult, ALU.subtract)
                        last.then_inc(s_tlo, 1)
                    else:
                        tt(lo, full, hi, ALU.subtract).then_inc(s_tlo, 1)

            def add_group(c, half, res=X, gate=None, g=None):
                dve.wait_ge(s_used, c + 1 + HL_N)
                cols = slice(512 * half, 512 * half + 512)
                src = [PS[:, 2 * half + t, :] for t in range(NT)]
                if gate is not None:
                    dve.wait_ge(s_gfree, g + 2)
                    for t in range(NT):
                        last = tt(TM[:, t, :], src[t], gate[:, cols], ALU.mult)
                    link(last)
                    src = [TM[:, t, :] for t in range(NT)]
                for t in range(NT):
                    last = tt(res[:, t, cols], src[t], res[:, t, cols], ALU.add)
                last.then_inc(s_gfree, 1)

            def spare(m, *js):
                if m.here:
                    for j in js:
                        ahead(m.c + j)

            def mod_out(m, banks):
                if m.here:
                    for j in range(2):
                        g = m.g + j
                        l, k = g // 12, 4 * (g % 12)
                        dve.wait_ge(s_mcol, g + 1)
                        tt(MOD[:, l, k:k + 4, :], PS[:, banks[j], 0:8].rearrange("p (c s) -> p c s", s=2),
                           PAR[:, 128 + 48 * l + k:132 + 48 * l + k].unsqueeze(2).to_broadcast((P, 4, 2)),
                           ALU.add).then_inc(s_modc, 1)

            def norm_scales(l, n):
                dve.wait_ge(s_modc, 12 * l + 4 + 6 * n)
                g = PAR[:, 32 + 16 * n + 8 * l:40 + 16 * n + 8 * l].unsqueeze(2).to_broadcast((P, KT, 2))
                last = stt(SCL[:, l, n, :, :], MOD[:, l, M_SC[n]:M_SC[n] + 8, :], 1.0, g, ALU.add, ALU.mult)
                if n == 0:
                    last = ts(GQ2[:, l, 0, :], GQ2[:, l, 0, :], ISC, None, ALU.mult)
                last.then_inc(s_scl, 1)
                dve.wait_ge(s_scl, 2 * l + n + 1)

            def mlp(q, c, u, m):
                e = EARLY.get(q)
                for i in range(4):
                    for j in range(8):
                        ahead(c + 8 * i + j)
                        if e and i == 2 and j == 4:
                            if e.stream:
                                norm_scales(e.q.layer, 0)
                            norm(e.norm, e.pow, CTX if e.stream else X)
                        if e and i == 3 and j == 5:
                            low(e.t, *scaled_by(e), steps=(0, 1))
                        if e and i == 3 and j > 5:
                            low(e.t + j - 4, *scaled_by(e), steps=(j - 4,))
                        if j < 4:
                            cols = 2 * (j % 2)
                            hid = HIDH[:, j // 2, cols:cols + 2, :].rearrange("p a n -> p (a n)")
                            dve.wait_ge(s_rl, 16 * q + 4 * i + j + 1)
                            stt(U2[:, j % 2, :], PS[:, 4 + (u + j) % 2, :], 0.0, RL[:, j % 2, :], ALU.max,
                                ALU.mult).then_inc(s_ufree, 1)
                            dve.wait_ge(s_ufree, u + 4 * i + j + 1 + 2)
                            dve.wait_ge(s_hh, 16 * q + 4 * i + j + 1)
                            tt(HIDL[:, j // 2, cols:cols + 2, :].rearrange("p a n -> p (a n)"),
                               U2[:, j % 2, :], hid.bitcast(F32), ALU.subtract).then_inc(s_hl, 1)
                        if i == 0 and j == 0:
                            mod_out(m, (0, 2))

            norm(0, 0, X)
            split(0)
            low(0, lambda k: PAR[:, k:k + 1])
            for c in range(1, SPLIT_LEAD):
                split(c)
            dve.wait_ge(s_row, 16 * N_ROWS)
            link(ts(NSK[:, :, :], SK[:, :, :], -1.0, None, ALU.mult))
            dve.wait_ge(s_cs, 1)
            tt(CS[:, :, :].rearrange("p s k -> p (s k)"), PAR[:, 64:80], SGC[:, :], ALU.mult).then_inc(s_cs, 1)
            dve.wait_ge(s_c4, 1)
            tt(C4[:, :, 2:4], CS[:, :, :].rearrange("p s k -> p k s"), C4[:, :, 0:2].bitcast(F32),
               ALU.subtract).then_inc(s_c4, 1)

            for l in range(DEPTH):
                L = LAYERS[l]
                c0, g0, u0, t0, h0 = L.c_in, GR1 * l, UC1 * l, 3 * l, 12 * l
                if l:
                    spare(L.m_in, 0)
                    norm(2 * l, 5 * l, X)
                    spare(L.m_in, 1)
                    low(4 * t0, lambda k: PAR[:, 8 * l + k:8 * l + k + 1])
                    spare(L.m_in, 2, 3)
                runs = ((0, 12, Z[:, :, 0:768], ((0, 6), (6, 12))),
                        (12, NQK, Z[:, :, C_SQ:C_SV], ((12, 18), (18, 20))))

                def parts(r):
                    h1, h2, z, gains = runs[r]
                    return QK[:, :, h1:h2, :], z.rearrange("p t (h d) -> p t h d", d=DH), h2 - h1, gains

                def qk_squares(r):
                    q, z, n, _ = parts(r)
                    dve.wait_ge(s_sq, 2 * l + r + 1)
                    link(nc.vector.tensor_reduce(MS[:, 0:2 * n].rearrange("p (t h) -> p t h", t=NT), q, AX_X, ALU.add))
                    ts(MS[:, 0:2 * n], MS[:, 0:2 * n], 1.0 / DH, EPS, ALU.mult, ALU.add).then_inc(s_ms, 1)

                def qk_norm(r):
                    q, z, n, gains = parts(r)
                    dve.wait_ge(s_rs, 5 * l + 2 + r)
                    rs = RS[:, 0:2 * n].rearrange("p (t h) -> p t h", t=NT).unsqueeze(3)
                    link(tt(q, z, rs.to_broadcast((P, NT, n, DH)), ALU.mult))
                    for i, (h1, h2) in enumerate(gains):
                        qh = QK[:, :, h1:h2, :]
                        g = GN[:, l:l + 1, 2 * r + i:2 * r + i + 1, :].to_broadcast((P, NT, h2 - h1, DH))
                        last = tt(qh, qh, g, ALU.mult)
                    link(last)

                def qk_sin(r):
                    q, z, n, _ = parts(r)
                    sin = CT[:, K_R1 + 64:K_R1 + 128].rearrange("p (t h d) -> p t h d", t=NT, h=1)
                    b = sin.to_broadcast((P, NT, n, 32))
                    tt(z[:, :, :, 0:32], q[:, :, :, 32:64], b, ALU.mult)
                    link(tt(z[:, :, :, 32:64], q[:, :, :, 0:32], b, ALU.mult))

                def qk_cos(r):
                    q, z, n, _ = parts(r)
                    cos = CT[:, K_R1:K_R1 + 64].rearrange("p (t h d) -> p t h d", t=NT, h=1)
                    q2 = q.rearrange("p t h (a d) -> p t (h a) d", a=2)
                    link(tt(q2, q2, cos.to_broadcast((P, NT, 2 * n, 32)), ALU.mult))
                    tt(q[:, :, :, 0:32], q[:, :, :, 0:32], z[:, :, :, 0:32], ALU.subtract)
                    tt(q[:, :, :, 32:64], q[:, :, :, 32:64], z[:, :, :, 32:64], ALU.add).then_inc(s_qk, 1)

                def convolve(*js):
                    wc = lambda j, q: PAR[:, 80 + 16 * l + 4 * j + q:81 + 16 * l + 4 * j + q]
                    for j in js:
                        for q in range(4):
                            if j == 0:
                                last = ts(CV[:, q, :], XP[:, q, 0:S], wc(0, q), PAR[:, 112 + 4 * l + q:113 + 4 * l + q],
                                          ALU.mult, ALU.add)
                            else:
                                last = stt(CV[:, q, :], XP[:, q, j:j + S], wc(j, q), CV[:, q, :], ALU.mult, ALU.add)
                        last.then_inc(s_cv, 1) if j == 3 else link(last)

                zero_m, caus = CT[:, K_M:K_M + 128], CT[:, K_M + 128:K_M + 256]
                f = G8[:, :, 4:8]
                late = (3, 5, 6)
                for k in range(12):
                    if k < 12 - len(late):
                        ahead(c0 + k)
                    if k == 1:
                        dve.wait_ge(s_gfree, g0 + 3)
                        link(tt(G8[:, :, :], Z[:, :, Z_GATE:ZW], IFB[:, l:l + 1, :].to_broadcast((P, NT, 8)), ALU.add))
                        stt(GT1[:, :, :], f, -1.0, f, ALU.mult, ALU.min).then_inc(s_ga, 1)
                        mod_out(L.m_in, (2, 3))
                    if k == 2:
                        dve.wait_ge(s_gl, l + 1)
                        stt(GT2[:, :, :], f, 0.0, GT1[:, :, :], ALU.min, ALU.subtract).then_inc(s_lf, 1)
                    if k == 3:
                        dve.wait_ge(s_b, l + 1)
                        link(nc.vector.tensor_copy(BS[:, :, :], PS[:, 6, 0:8].rearrange("p (t h) -> p t h", t=NT)))
                        link(tt(ES[:, :, :], G8[:, :, 0:4], BS[:, :, :], ALU.subtract))
                        for t in range(NT):
                            last = tt(DG[:, t, :, :], IDM.unsqueeze(1).to_broadcast((P, ML_H, P)),
                                      ES[:, t, :].unsqueeze(2).to_broadcast((P, ML_H, P)), ALU.mult)
                        last.then_inc(s_dg, 1)
                        dve.wait_ge(s_ufree, u0 + 2 + 2)
                        convolve(0)
                    if k == 4:
                        convolve(1)
                    if k == 5:
                        dve.wait_ge(s_eb, l + 1)
                        for j in range(3):
                            m = (zero_m if j == 1 else caus).unsqueeze(1).to_broadcast((P, ML_H, P))
                            last = tt(ME[:, j, :, :], PS[:, 6 + j // 2, :].rearrange("p (h n) -> p h n", h=ML_H), m,
                                      ALU.add)
                        link(last)
                        link(nc.vector.tensor_reduce(RMX[:, :, :], ME[:, :, :, :], AX_X, ALU.max))
                    if k == 6:
                        link(tt(RMX[:, 1, :], RMX[:, 1, :], RMX[:, 2, :], ALU.max))
                        link(ts(RR[:, :, :], RMX[:, 0:2, :], 0.0, None, ALU.max))
                        for j in range(3):
                            last = tt(ME[:, j, :, :], ME[:, j, :, :],
                                      RR[:, (j + 1) // 2, :].unsqueeze(2).to_broadcast((P, ML_H, P)), ALU.subtract)
                        last.then_inc(s_me, 1)
                        tt(GT2[:, :, :], BS[:, :, :], RR[:, :, :], ALU.add).then_inc(s_mem, 1)
                        convolve(2)
                    if k == 7:
                        convolve(3)
                        qk_squares(0)
                    if k == 8:
                        qk_norm(0)
                    if k == 9:
                        qk_sin(0)
                        dve.wait_ge(s_sg, l + 1)
                        tt(CV[:, :, :], CV[:, :, :], SG[:, :, :], ALU.mult).then_inc(s_lqk, 1)
                    if k == 10:
                        qk_cos(0)
                    if k == 11:
                        qk_squares(1)
                dve.wait_ge(s_mex, l + 1)
                dve.wait_ge(s_ms3, l + 1)
                for j in range(3):
                    for b in range(2):
                        m = ME[:, j, b:ML_H:2, :]
                        col = 256 * (j % 2)
                        last = stt(m, PS[:, 4 * (j // 2) + b, col:col + 256].rearrange("p (h n) -> p h n", h=2), ISC, m,
                                   ALU.mult, ALU.mult)
                last.then_inc(s_mp, 1)

                def divide(col, h1):
                    link(nc.vector.reciprocal(RIN[:, h1:h1 + 6, :], SUM[:, h1:h1 + 6, :]))
                    y = YN[:, :, col:col + 6 * DH].rearrange("p t (h d) -> p t h d", h=6)
                    return tt(y, y, RIN[:, h1:h1 + 6, :].rearrange("p h t -> p t h").unsqueeze(3)
                              .to_broadcast((P, NT, 6, DH)), ALU.mult)

                hm = HM[:, :, :].rearrange("p t (h d) -> p t h d", h=ML_H)
                for h in range(13):
                    if h < 12:
                        dve.wait_ge(s_s, h0 + h + 1)
                        dve.wait_ge(s_pt, h0 + h + 1)
                        old = CT[:, K_M:K_M + 256] if h < MOBA_H else CT[:, K_M + 256:K_M + 512]
                        nc.vector.tensor_tensor_reduce(PM[:, h % 2, 0:128], PS[:, h % 2, 0:128], caus, 1.0, -3e38,
                                                       ALU.add, ALU.max, MX[:, h % 2, 0:1])
                        nc.vector.tensor_tensor_reduce(PM[:, h % 2, 128:384], PS[:, h % 2, 128:384], old, 1.0, -3e38,
                                                       ALU.add, ALU.max, MX[:, h % 2, 1:2]).then_inc(s_sm, 1)
                        dve.wait_ge(s_sm, h0 + h + 1 + 2)
                        if h < MOBA_H:
                            ts(NB[:, h, :], MX[:, h % 2, :], -ISC, None, ALU.mult).then_inc(s_nb, 1)
                        else:
                            ts(NB[:, h, :], MX[:, h % 2, :], -ISC, NSK[:, l, h - 6:h - 5], ALU.mult,
                               ALU.min).then_inc(s_nb, 1)
                    if h >= 1:
                        dve.wait_ge(s_pt, h0 + h + 2)
                        dve.wait_ge(s_o, h0 + h)
                        nc.vector.tensor_copy(PTS[:, (h - 1) % 2, 0:384],
                                              PS[:, 2 + (h - 1) % 2, 0:384]).then_inc(s_pe, 1)
                    if h in late:
                        ahead(c0 + 12 - len(late) + late.index(h))
                    if h == 0:
                        qk_norm(1)
                    if h == 1:
                        qk_sin(1)
                    if h == 2:
                        qk_cos(1)
                    if h == 7:
                        dve.wait_ge(s_exm, l + 1)
                        dve.wait_ge(s_mo, l + 1)
                        o = PS[:, 6:8, 0:260].rearrange("p t (h d) -> p t h d", h=ML_H)
                        link(nc.vector.tensor_copy(DEN[:, :, :], o[:, :, :, DH]))
                        link(stt(GT1[:, :, :], DEN[:, :, :], -1.0, DEN[:, :, :], ALU.mult, ALU.max))
                        link(tt(DEN[:, :, :], GT1[:, :, :], GT2[:, :, :], ALU.max))
                        link(nc.vector.reciprocal(DEN[:, :, :], DEN[:, :, :]))
                        link(tt(hm, o[:, :, :, 0:DH], DEN[:, :, :].unsqueeze(3).to_broadcast((P, NT, ML_H, DH)),
                                ALU.mult))
                        dve.wait_ge(s_so, l + 1)
                        tt(HM[:, :, :], HM[:, :, :], Z[:, :, Z_LO:Z_GATE], ALU.mult).then_inc(s_h, 1)
                    if h == 9:
                        dve.wait_ge(s_hsq, l + 1)
                        link(nc.vector.tensor_reduce(MS[:, 0:8].rearrange("p (t h) -> p t h", t=NT),
                                                     CV[:, 0:2, :].rearrange("p t (h d) -> p t h d", h=ML_H), AX_X,
                                                     ALU.add))
                        ts(MS[:, 0:8], MS[:, 0:8], 1.0 / DH, EPS, ALU.mult, ALU.add).then_inc(s_ms, 1)
                    if h == 10:
                        dve.wait_ge(s_rs, 5 * l + 4)
                        link(tt(hm, hm, RS[:, 0:8].rearrange("p (t h) -> p t h", t=NT).unsqueeze(3)
                                .to_broadcast((P, NT, ML_H, DH)), ALU.mult))
                        tt(YN[:, :, MOBA_H * DH:(MOBA_H + ML_H) * DH], HM[:, :, :],
                           MN[:, l:l + 1, :].to_broadcast((P, NT, ML_H * DH)), ALU.mult)
                    if h == 11:
                        dve.wait_ge(s_oe, h0 + 6 + 2)
                        divide(0, 0)
                    if h == 12:
                        tt(SKE[:, :, :], NB[:, 6:12, :], SK[:, l, :].unsqueeze(2).to_broadcast((P, 6, 2)),
                           ALU.add).then_inc(s_ske, 1)
                dve.wait_ge(s_e, h0 + 12)
                dve.wait_ge(s_sko, l + 1)
                link(tt(SUM[:, 6:12, :], SUM[:, 6:12, :], SKE[:, :, :], ALU.add))
                dve.wait_ge(s_oe, h0 + 12 + 2)
                divide(DH * (MOBA_H + ML_H), 6).then_inc(s_src, 1)

                spare(L.m_o, 0, 1)
                low(4 * t0 + 4)
                spare(L.m_o, 2, 3)
                for k in range(4):
                    ahead(L.c_o + k)
                    if k == 0:
                        mod_out(L.m_o, (4, 5))
                    if k % 2:
                        add_group(L.c_o + k, k // 2)
                spare(L.m_mlp, 0)
                norm(2 * l + 1, 5 * l + 4, X)
                spare(L.m_mlp, 1)
                low(4 * t0 + 8, lambda k: PAR[:, 16 + 8 * l + k:17 + 8 * l + k])
                spare(L.m_mlp, 2, 3)
                mlp(l, L.c_mlp, u0 + 2, L.m_mlp)
                for half in range(2):
                    add_group(L.c_mlp + 30 + half, half)

            norm_scales(0, 1)
            dve.wait_ge(s_pad, 1)

            def head_squares(q, n, h1):
                dve.wait_ge(s_sq2, n + 1)
                w = NT * (10 - h1)
                link(nc.vector.tensor_reduce(MS[:, 0:w].rearrange("p (t h) -> p t h", t=NT), QK2[:, :, h1:10, :],
                                             AX_X, ALU.add))
                ts(MS[:, 0:w], MS[:, 0:w], 1.0 / DH, EPS, ALU.mult, ALU.add).then_inc(s_ms, 1)

            def head_norm(q, m, h1, signal):
                dve.wait_ge(s_rs, m + 1)
                w = NT * (10 - h1)
                z = ZN[:, :, N_Q + DH * h1:N_V].rearrange("p t (h d) -> p t h d", d=DH)
                rs = RS[:, 0:w].rearrange("p (t h) -> p t h", t=NT).unsqueeze(3)
                link(tt(QK2[:, :, h1:10, :], z, rs.to_broadcast((P, NT, 10 - h1, DH)), ALU.mult))
                for i, (a1, a2) in enumerate(((h1, 8), (8, 10))):
                    if a1 < a2:
                        h = QK2[:, :, a1:a2, :]
                        last = tt(h, h, GQ2[:, q.layer:q.layer + 1, i:i + 1, :].to_broadcast((P, NT, a2 - a1, DH)),
                                  ALU.mult)
                last.then_inc(s_qk2, 1) if signal else link(last)

            def gate_diagonals(q, n, factor):
                gt = MOD[:, q.layer, M_GT[n]:M_GT[n] + 8, q.stream]
                last = stt(DGB[:, :, :], gt.unsqueeze(2).to_broadcast((P, 8, P)), factor,
                           IDM.unsqueeze(1).to_broadcast((P, 8, P)), ALU.mult, ALU.mult)
                last.then_inc(s_dgb, 1)

            for q in PASSES:
                c0, g0, R = q.c_in, q.g, CTX if q.stream else X
                if q.mini:
                    ahead(q.c - 1)
                    norm(q.norm, q.pow - 1, R)
                    spare(q.m_in, 0)
                    head_squares(q, q.qk - 1, 8)
                    head_norm(q, q.pow, 8, True)
                    spare(q.m_in, 1)
                    low(q.t, *norm_scale(q, 0, q.stream))
                    spare(q.m_in, 2, 3)
                else:
                    spare(q.m_in, 0, 1, 2, 3)
                for k in range(19):
                    ahead(c0 + k)
                    if k == 0:
                        mod_out(q.m_in, q.mod_banks)
                        if q.mini:
                            norm_scales(1, 1)
                    if k == 18:
                        dve.wait_ge(s_yh, q.p + 1)
                        tt(AL[:, 0:2, :], YC[:, :, :], AH[:, 0:2, :].bitcast(F32), ALU.subtract)
                        tt(AL[:, 2:4, :], YF[:, :, :], AH[:, 2:4, :].bitcast(F32), ALU.subtract).then_inc(s_yl, 1)
                    if k == 3:
                        dve.wait_ge(s_ufree, q.u + 3 + 2)
                        link(tt(CXP[:, :, 1:1 + S], UB[:, 1, :, :], UB[:, 2, :, :], ALU.mult))
                        wc = lambda j, b: PAR[:, 224 + 6 * q.layer + 2 * j + b:225 + 6 * q.layer + 2 * j + b]
                        for b in range(2):
                            last = ts(YC[:, b, :], CXP[:, b, 0:S], wc(0, b), None, ALU.mult)
                        link(last)
                    if k in (4, 5):
                        for b in range(2):
                            last = stt(YC[:, b, :], CXP[:, b, k - 3:k - 3 + S], wc(k - 3, b), YC[:, b, :], ALU.mult,
                                       ALU.add)
                        link(last)
                        if k == 5:
                            tt(YC[:, :, :], YC[:, :, :], UB[:, 0, :, :], ALU.mult).then_inc(s_yc, 1)
                    if k == 7:
                        head_squares(q, q.qk, 0)
                        head_norm(q, q.pow + 1, 0, q.stream == 1)
                    if k == 8 and q.stream == 0:
                        qk = QK2[:, :, 0:10, :]
                        z = ZN[:, :, N_Q:N_V].rearrange("p t (h d) -> p t h d", d=DH)
                        sin = CT[:, K_R2 + 64:K_R2 + 128].rearrange("p (t h d) -> p t h d", t=NT, h=1)
                        cos = CT[:, K_R2:K_R2 + 64].rearrange("p (t h d) -> p t h d", t=NT, h=1)
                        b = sin.to_broadcast((P, NT, 10, 32))
                        tt(z[:, :, :, 0:32], qk[:, :, :, 32:64], b, ALU.mult)
                        link(tt(z[:, :, :, 32:64], qk[:, :, :, 0:32], b, ALU.mult))
                        q2 = qk.rearrange("p t h (a d) -> p t (h a) d", a=2)
                        link(tt(q2, q2, cos.to_broadcast((P, NT, 20, 32)), ALU.mult))
                        tt(qk[:, :, :, 0:32], qk[:, :, :, 0:32], z[:, :, :, 0:32], ALU.subtract)
                        tt(qk[:, :, :, 32:64], qk[:, :, :, 32:64], z[:, :, :, 32:64], ALU.add).then_inc(s_qk2, 1)
                    for v in units(k):
                        n = 256 if q.stream else 512
                        if v < 16:
                            h, t = divmod(v, 2)
                            dve.wait_ge(s_s2, q.att + v + 1)
                            nc.vector.tensor_reduce(NM2[:, h, t:t + 1], PS[:, 4 + v % 2, 0:n], AX_X, ALU.max,
                                                    negate=True).then_inc(s_n2, 1)
                        if 2 <= v < 18:
                            dve.wait_ge(s_t2, q.att + v - 2 + 1 + 2)
                            dve.wait_ge(s_o2, q.att + v - 2 + 1)
                            nc.vector.tensor_copy(PTS[:, v % 2, 0:n], PS[:, 6 + v % 2, 0:n]).then_inc(s_p2, 1)
                dve.wait_ge(s_oe2, q.att + 16 + 2)
                link(nc.vector.reciprocal(RN2[:, :, :], SM2[:, :, :]))
                for t in range(NT):
                    y = YA[:, t, :].rearrange("p (h d) -> p h d", h=QH)
                    last = tt(y, y, RN2[:, :, t].unsqueeze(2).to_broadcast((P, QH, DH)), ALU.mult)
                last.then_inc(s_src, 1)
                for k in range(19, 23):
                    b, halfs = ((0, (0, 1)), (1, (0, 1)), (2, (0,)), (2, (1,)))[k - 19]
                    ahead(c0 + k)
                    for half in halfs:
                        if b < 2 and half == 0:
                            dve.wait_ge(s_bg, 2 * q.p + b + 1)
                        else:
                            dve.wait_ge(s_used, c0 + k + 1 + HL_N)
                        cols = slice(512 * half, 512 * half + 512)
                        for t in range(NT):
                            ga = GA[:, t, D * b + 512 * half:D * b + 512 * half + 512]
                            dst = M2[:, t, cols] if b == 0 else TM[:, t, :]
                            last = stt(dst, ga, 1.0, PS[:, 2 * half + t, :], ALU.add, ALU.mult)
                        last.then_inc(s_gfree, 1)
                        if b > 0:
                            dve.wait_ge(s_gfree, g0 + 9 + 2 * b + half + 1 + 2)
                            for t in range(NT):
                                last = tt(M2[:, t, cols], M2[:, t, cols], TM[:, t, :], ALU.add)
                            if b == 2 and half == 1:
                                last.then_inc(s_src, 1)
                            else:
                                link(last)
                    if k == 19:
                        low(q.t + 4, steps=(2, 3))
                dve.wait_ge(s_src, q.src + 3)
                gate_diagonals(q, 0, 0.5)
                spare(q.m_o, 0, 1)
                low(q.t + 6)
                spare(q.m_o, 2, 3)
                dve.wait_ge(s_gtc, 2 * q.p + 1)
                for k in range(4):
                    ahead(q.c_o + k)
                    if k == 0:
                        mod_out(q.m_o, (4, 5))
                    if k % 2:
                        add_group(q.c_o + k, k // 2, R, GTB, g0 + 15 + k // 2)
                spare(q.m_mlp, 0)
                norm(q.norm + 1, q.pow + 2, R)
                dve.wait_ge(s_gfree, g0 + 17 + 2)
                gate_diagonals(q, 1, 1.0)
                spare(q.m_mlp, 1)
                low(q.t + 10, *norm_scale(q, 1, q.stream))
                spare(q.m_mlp, 2, 3)
                mlp(q.mlp, q.c_mlp, q.u + 3, q.m_mlp)
                dve.wait_ge(s_gtc, 2 * q.p + 2)
                for half in range(2):
                    add_group(q.c_mlp + 30 + half, half, R, GTB, g0 + 17 + half)

        @block.tensor
        def _(pe):
            mm = nc.tensor.matmul
            pe.wait_ge(s_cst, 16 * N_CONST)
            nc.tensor.transpose(PS[:, 6, 0:120], PR0[0:120, :], IDM[0:120, 0:120])
            nc.tensor.transpose(PS[:, 7, 0:108], PR1[0:108, :], IDM[0:108, 0:108]).then_inc(s_par, 1)
            pe.wait_ge(s_parc, 1)

            def transposes(source, n, src, steps=range(4), m=NO_SLOT, banks=(4, 5), first=0, free=0):
                if m.here:
                    for j in range(3):
                        if free and j != 1:
                            pe.wait_ge(s_gfree, free - (j == 0))
                        mod_chunk(m, j, banks)
                pe.wait_ge(s_src, source + 1)
                for s in range(len(steps)):
                    if m.here and s == 2:
                        mod_chunk(m, 3, banks)
                    pe.wait_ge(s_tlo, n + s + 1)
                    for k in range(2):
                        for t in range(NT):
                            col = 128 * (2 * (s + first) + k)
                            last = nc.tensor.transpose(PS[:, 6 + (s + first) % 2, 256 * k + 128 * t:256 * k + 128 * t + 128],
                                                       src[:, t, col:col + 128], IDM)
                    last.then_inc(s_tp, 1)
                return n

            def tile_split(n, j):
                if n is not None and j % 2 == 0:
                    pe.wait_ge(s_tlo, n + j // 2 + 1 + 2)

            def arrived(c):
                pe.wait_ge(s_lo, c + 1 + RAW_N)

            def slot(k, kt, n):
                hi = HI[:, k % HL_N, 0:kt * n].rearrange("p (a n) -> p a n", a=kt)
                lo = LO[:, k % HL_N, 0:kt * n].rearrange("p (a n) -> p a n", a=kt)
                return hi, lo

            def tokens_out(c, k, bank, kt, n, ah, al, first, last, ts=None, tile=0):
                arrived(c)
                hi, lo = slot(k, kt, n)
                for t in range(NT):
                    o = PS[:, bank + t, 0:n]
                    for j in range(kt):
                        if t == 0:
                            tile_split(ts, tile + j)
                        th, tl = ah[:, j, 128 * t:128 * t + 128], al[:, j, 128 * t:128 * t + 128]
                        mm(o, th, hi[:, j, :], start=first and j == 0, stop=False)
                        mm(o, th, lo[:, j, :], start=False, stop=False)
                        ins = mm(o, tl, hi[:, j, :], start=False, stop=last and j == kt - 1)
                ins.then_inc(s_used, 1)

            def features_out(c, k, bank, ah, al, ts=None):
                arrived(c)
                hi, lo = slot(k, KT, 256)
                for q in range(2):
                    o = PS[:, bank, 256 * q:256 * q + 256]
                    for j in range(KT):
                        if q == 0:
                            tile_split(ts, j)
                        wh, wl = hi[:, j, 128 * q:128 * q + 128], lo[:, j, 128 * q:128 * q + 128]
                        mm(o, wh, ah[:, j, :], start=j == 0, stop=False)
                        mm(o, wh, al[:, j, :], start=False, stop=False)
                        ins = mm(o, wl, ah[:, j, :], start=False, stop=j == KT - 1)
                ins.then_inc(s_used, 1)

            def group(g, c, k, n=512):
                pe.wait_ge(s_gfree, g + 1)
                for h in range(2):
                    half_group(c + h, k + h, g % 2, h, n)

            def half_group(c, k, pair, h, n=512, ts=None):
                tokens_out(c, k, 2 * pair, 4, n, AH[:, 4 * h:4 * h + 4, :], AL[:, 4 * h:4 * h + 4, :], h == 0, h == 1,
                           ts, 4 * h)

            def mod_chunk(m, j, banks):
                arrived(m.c + j)
                hi, lo = slot(m.c + j, 4, 512)
                for k in range(4):
                    w, o = C4[:, 4 * (j % 2) + k, :], PS[0:4, banks[j // 2], :]
                    mm(o, w, hi[:, k, :], start=j % 2 == 0 and k == 0, stop=False)
                    last = mm(o, w, lo[:, k, :], start=False, stop=j % 2 == 1 and k == 3)
                last.then_inc(s_used, 1)

            def mod_columns(m, banks):
                if m.here:
                    for j in range(2):
                        pe.wait_ge(s_mrow, m.g + j + 1)
                        for k in range(4):
                            last = mm(PS[:, banks[j], 2 * k:2 * k + 2], ROWS[0:4, j, 128 * k:128 * k + 128], SEL[:, :],
                                      start=True, stop=True)
                        last.then_inc(s_mcol, 1)

            def mod_done(m):
                if m.here:
                    pe.wait_ge(s_modc, m.g + 2)

            def mlp(q, c, u, m, ts):
                e = EARLY.get(q)
                for i in range(4):
                    for j in range(4):
                        pe.wait_ge(s_ufree, u + 4 * i + j + 1)
                        features_out(c + 8 * i + j, c + 8 * i + j, 4 + (u + j) % 2, AH, AL,
                                     ts if i == 0 and j == 0 else None)
                        if i == 0 and j == 0:
                            mod_columns(m, (0, 2))
                        if i == 0 and j == 1:
                            mod_done(m)
                    if i == 0 and q >= DEPTH:
                        pe.wait_ge(s_gtc, 2 * (q - DEPTH) + 2)
                    for j in range(4):
                        b = j // 2
                        pe.wait_ge(s_hl, 16 * q + 4 * i + 2 * b + 2)
                        tokens_out(c + 8 * i + 4 + j, c + 8 * i + 4 + j, 2 * (j % 2), 4, 512, HIDH[:, b, :, :],
                                   HIDL[:, b, :, :], i == 0 and b == 0, i == 3 and b == 1)
                        if e and i == 3 and j < 3:
                            transposes(e.src, e.t + j + (j > 0), YN, ((0, 1), (2,), (3,))[j], first=j + (j > 0))

            for l in range(DEPTH):
                L = LAYERS[l]
                c0, g0, u0, t0, h0 = L.c_in, GR1 * l, UC1 * l, 3 * l, 12 * l
                pe.wait_ge(s_ufree, u0 + 2)
                pe.wait_ge(s_gfree, g0 + 2)
                ts = transposes(t0, 4 * t0, YN, m=L.m_in, banks=(2, 3))
                tokens_out(c0, 0, 0, KT, 8, AH, AL, True, True, ts)
                for j in range(2):
                    pe.wait_ge(s_ufree, u0 + j + 1)
                    features_out(c0 + 1 + j, 1 + j, 4 + j, AH, AL)
                    if j == 0:
                        mod_columns(L.m_in, (2, 3))
                mod_done(L.m_in)
                for k in range(3, 12):
                    g = g0 + (k - 1) // 2 if k < 10 else g0 + 5
                    pe.wait_ge(s_gfree, g + 1)
                    if k == 9:
                        tokens_out(c0 + 9, 9, 0, KT, 256, AH, AL, True, True)
                    else:
                        half_group(c0 + k, k, (g - g0) % 2, (k - 3) % 2 if k < 10 else k % 2)
                    if k == 3:
                        pe.wait_ge(s_lf, l + 1)
                        mm(PS[:, 6, 0:4], TRI, GT2[:, 0, :], start=True, stop=True)
                        mm(PS[:, 6, 4:8], ONES, GT2[:, 0, :], start=True, stop=False)
                        mm(PS[:, 6, 4:8], TRI, GT2[:, 1, :], start=False, stop=True).then_inc(s_b, 1)
                    if k == 4:
                        pe.wait_ge(s_dg, l + 1)
                        for t in range(NT):
                            last = mm(PS[:, 6 + t, :], ONES, DG[:, t, :, :].rearrange("p h n -> p (h n)"), start=True,
                                      stop=True)
                        last.then_inc(s_eb, 1)

                pe.wait_ge(s_lqk, l + 1)
                pe.wait_ge(s_gfree, g0 + 5 + 2)
                pe.wait_ge(s_ufree, u0 + 2 + 2)
                for j, (t, s) in enumerate(((0, 0), (1, 0), (1, 1))):
                    for h in range(ML_H):
                        r = 64 * (h % 2)
                        col = 256 * (j % 2) + 128 * (h // 2)
                        last = mm(PS[:, 4 * (j // 2) + h % 2, col:col + 128], CV[r:r + 64, h // 2, 128 * t:128 * t + 128],
                                  CV[r:r + 64, 2 + h // 2, 128 * s:128 * s + 128], start=True, stop=True)
                last.then_inc(s_ms3, 1)

                def turn_qk(j):
                    for k in range(2 if j < 5 else 1):
                        for t in range(NT):
                            h = 2 * (2 * j + k)
                            last = nc.tensor.transpose(
                                PS[:, 6 + QT_BANK[j], 256 * k + 128 * t:256 * k + 128 * t + 128],
                                QK[:, t, h:h + 2, :].rearrange("p h d -> p (h d)"), IDM)
                    last.then_inc(s_qt, 1)

                def turn_weights(j):
                    for h in range(ML_H):
                        last = nc.tensor.transpose(PS[:, 6 + MT_BANK[j], 128 * h:128 * h + 128], ME[:, j, h, :], IDM)
                    last.then_inc(s_mt, 1)

                pe.wait_ge(s_qk, 2 * l + 1)
                turn_qk(0)
                turn_qk(1)
                pe.wait_ge(s_qtc, 6 * l + 1 + 2)
                turn_qk(2)
                pe.wait_ge(s_mp, l + 1)
                pe.wait_ge(s_gfree, g0 + 6 + 2)
                pe.wait_ge(s_qtc, 6 * l + 3 + 2)

                def scores(h):
                    r = 64 * (h % 2)
                    if h < MOBA_H:
                        q, k = QKT[r:r + 64, h // 2, :], QKT[r:r + 64, 3 + h // 2, :]
                    else:
                        kv = (h - 6) // 3
                        q = QKT[r:r + 64, 6 + (h - 6) // 2, :]
                        k = QKT[r:r + 64, 9 if kv == h % 2 else 10, :]
                    pe.wait_ge(s_sm, h0 + h + 1)
                    mm(PS[:, h % 2, 0:128], q[:, 0:128], k[:, 0:128], start=True, stop=True)
                    mm(PS[:, h % 2, 128:384], q[:, 128:256], k, start=True, stop=True).then_inc(s_s, 1)

                def turn(h):
                    pe.wait_ge(s_e, h0 + h + 1)
                    pe.wait_ge(s_pe, h0 + h + 1)
                    for j in range(3):
                        last = nc.tensor.transpose(PS[:, 2 + h % 2, 128 * j:128 * j + 128],
                                                   PM[:, h % 2, 128 * j:128 * j + 128], IDM)
                    last.then_inc(s_pt, 1)

                def values(h):
                    col = C_MV + DH * h if h < MOBA_H else C_SV + DH * ((h - 6) // 3)
                    v = Z[:, :, col:col + DH]
                    pe.wait_ge(s_pe, h0 + h + 1 + 2)
                    pe.wait_ge(s_oe, h0 + h + 1)
                    p, o = PTS[:, h % 2, :], PS[:, 4 + h % 2, :]
                    mm(o[:, 0:64], p[:, 0:128], v[:, 0, :], start=True, stop=True)
                    mm(o[:, 64:128], p[:, 128:256], v[:, 0, :], start=True, stop=False)
                    mm(o[:, 64:128], p[:, 256:384], v[:, 1, :], start=False, stop=True).then_inc(s_o, 1)

                for h in range(14):
                    if h < 12:
                        scores(h)
                    if 1 <= h <= 12:
                        turn(h - 1)
                    if h >= 2:
                        values(h - 2)
                    if h == 1:
                        turn_weights(0)
                        turn_weights(1)
                    if h == 2:
                        pe.wait_ge(s_mtc, 3 * l + 1)
                        turn_weights(2)
                    if h == 4:
                        pe.wait_ge(s_qsw, l + 1)
                        pe.wait_ge(s_mtc, 3 * l + 2)
                        turn_qk(3)
                        pe.wait_ge(s_mtc, 3 * l + 3)
                        turn_qk(4)
                    if h == 5:
                        pe.wait_ge(s_qtc, 6 * l + 4 + 2)
                        turn_qk(5)
                        pe.wait_ge(s_qtc, 6 * l + 6 + 2)
                    if h == 6:
                        pe.wait_ge(s_v65, l + 1)
                        for n in range(ML_H):
                            o0, o1 = PS[:, 6, 65 * n:65 * n + 65], PS[:, 7, 65 * n:65 * n + 65]
                            mm(o0, PTM[:, 0, n, :], V65[:, 0, n, :], start=True, stop=True)
                            mm(o1, PTM[:, 1, n, :], V65[:, 0, n, :], start=True, stop=False)
                            last = mm(o1, PTM[:, 2, n, :], V65[:, 1, n, :], start=False, stop=True)
                        last.then_inc(s_mo, 1)
                pe.wait_ge(s_oe, h0 + 12 + 2)
                pe.wait_ge(s_c4, 2)

                ts = transposes(t0 + 1, 4 * t0 + 4, YN, m=L.m_o)
                pe.wait_ge(s_gfree, g0 + 6 + 1)
                half_group(L.c_o, L.c_o, 0, 0, ts=ts)
                mod_columns(L.m_o, (4, 5))
                half_group(L.c_o + 1, L.c_o + 1, 0, 1, ts=ts)
                mod_done(L.m_o)
                group(g0 + 7, L.c_o + 2, L.c_o + 2)
                ts = transposes(t0 + 2, 4 * t0 + 8, YN, m=L.m_mlp, banks=(0, 2), free=g0 + 8 + 2)
                mlp(l, L.c_mlp, u0 + 2, L.m_mlp, ts)

            def turn_heads(n, steps):
                for j, (h, bank) in enumerate(steps):
                    pe.wait_ge(s_qc2, n + j + (2 if len(steps) == 1 or j == 2 else 1))
                    for k in range(2):
                        for t in range(NT):
                            last = nc.tensor.transpose(PS[:, bank, 256 * k + 128 * t:256 * k + 128 * t + 128],
                                                       QK2[:, t, h + 2 * k:h + 2 * k + 2, :].rearrange("p h d -> p (h d)"),
                                                       IDM)
                    last.then_inc(s_qt2, 1)

            def gate_rows(n, banks):
                pe.wait_ge(s_dgb, n + 1)
                for j in range(2):
                    last = mm(PS[:, banks[j], :], ONES, DGB[:, 4 * j:4 * j + 4, :].rearrange("p k n -> p (k n)"),
                              start=True, stop=True)
                last.then_inc(s_gt, 1)

            for q in PASSES:
                c0, g0 = q.c_in, q.g
                qt0 = 3 * q.p + (1 if q.mini else 0)
                if q.mini:
                    pe.wait_ge(s_gfree, g0 - 1 + 1)
                    tokens_out(q.c - 1, q.c - 1, 0, KT, 256, AH, AL, True, True, q.t - 4)
                ts = q.t
                if q.mini:
                    transposes(q.src, q.t, YN, m=q.m_in, banks=q.mod_banks, free=g0 + 2)
                elif q.m_in.here:
                    for j in range(MODC):
                        pe.wait_ge(s_gfree, g0 + 1 + j // 2)
                        mod_chunk(q.m_in, j, q.mod_banks)
                for k in range(3):
                    pe.wait_ge(s_ufree, q.u + k + 1)
                    features_out(c0 + k, c0 + k, 4 + (q.u + k) % 2, AH, AL, None if k else ts)
                    if k == 0 and q.mini:
                        pe.wait_ge(s_qw2, q.qk)
                        turn_heads(qt0 - 1, ((8, 6),))
                    if k == 0:
                        mod_columns(q.m_in, q.mod_banks)
                    if k == 1:
                        mod_done(q.m_in)
                pe.wait_ge(s_gfree, g0 + 1)
                tokens_out(c0 + 3, c0 + 3, 0, KT, 256, AH, AL, True, True)
                pe.wait_ge(s_gfree, g0 + 2)
                for h in range(2):
                    half_group(c0 + 4 + h, c0 + 4 + h, 1, h)
                pe.wait_ge(s_gfree, g0 + 3)
                tokens_out(c0 + 6, c0 + 6, 0, KT, 256, AH, AL, True, True)
                for f in range(2):
                    for b in range(2):
                        for t in range(NT):
                            tab = CT[:, K_CL + 2 * S * f + S * t:K_CL + 2 * S * f + S * t + S]
                            last = mm(PS[:, 6 + f, 256 * b:256 * b + 256], ZN[:, t, N_F + 128 * b:N_F + 128 * b + 128],
                                      tab, start=t == 0, stop=t == NT - 1)
                last.then_inc(s_fa, 1)
                for k in range(7, 19):
                    if k % 2:
                        pe.wait_ge(s_gfree, g0 + 3 + (k - 7) // 2 + 2)
                    half_group(c0 + k, c0 + k, 0, (k - 7) % 2)
                    if k == 7:
                        pe.wait_ge(s_fac, q.p + 1)
                        for b in range(2):
                            for f in range(2):
                                last = mm(PS[:, 6, 256 * b:256 * b + 256], CT[:, K_BD + 128 * f:K_BD + 128 * f + 128],
                                          A12[:, f, b, :], start=f == 0, stop=f == 1)
                        last.then_inc(s_fy, 1)
                    if k == 10:
                        pe.wait_ge(s_qw2, q.qk + 1)
                        pe.wait_ge(s_fyc, q.p + 1)
                        turn_heads(qt0, ((0, 6), (4, 7), (8, 6)))
                        pe.wait_ge(s_qc2, qt0 + 3 + 2)
                    n = 256 if q.stream else 512
                    for v in units(k):
                        if v < 16:
                            h, t = divmod(v, 2)
                            r = 64 * (h % 2)
                            pe.wait_ge(s_e2, q.att + v + 1)
                            mm(PS[:, 4 + v % 2, 0:n], QT2[r:r + 64, h // 2, 128 * t:128 * t + 128],
                               KTB[r:r + 64, 0 if h // 4 == h % 2 else 1, 2 * S - n if q.stream else 0:2 * S],
                               start=True, stop=True).then_inc(s_s2, 1)
                        if 2 <= v < 18:
                            pe.wait_ge(s_e2, q.att + v - 2 + 1 + 2)
                            pe.wait_ge(s_p2, q.att + v - 2 + 1)
                            for j in range(n // 128):
                                last = nc.tensor.transpose(PS[:, 6 + v % 2, 128 * j:128 * j + 128],
                                                           PM[:, v % 2, 128 * j:128 * j + 128], IDM)
                            last.then_inc(s_t2, 1)
                        if v >= 4:
                            h, t = divmod(v - 4, 2)
                            pe.wait_ge(s_p2, q.att + v - 4 + 1 + 2)
                            pe.wait_ge(s_oe2, q.att + v - 4 + 1)
                            for j in range(n // 128):
                                last = mm(PS[:, 2 + v % 2, 0:DH], PTS[:, v % 2, 128 * j:128 * j + 128],
                                          VB[:, j + 2 * q.stream, DH * (h // 4):DH * (h // 4) + DH],
                                          start=j == 0, stop=j == n // 128 - 1)
                            last.then_inc(s_o2, 1)
                pe.wait_ge(s_yl, q.p + 1)
                for b in range(2):
                    c = c0 + 19 + b
                    arrived(c)
                    hi, lo = slot(c, 2, D)
                    for half in range(2):
                        if b == 0 and half == 1:
                            pe.wait_ge(s_oe2, q.att + 16 + 2)
                        pe.wait_ge(s_gfree, g0 + 9 + 2 * b + half + (2 if b == 0 and half == 0 else 1))
                        for t in range(NT):
                            for j in range(2):
                                o, cols = PS[:, 2 * half + t, :], slice(512 * half, 512 * half + 512)
                                th, tl = (w[:, 2 * b + j, 128 * t:128 * t + 128] for w in (AH, AL))
                                mm(o, th, hi[:, j, cols], start=j == 0, stop=False)
                                mm(o, th, lo[:, j, cols], start=False, stop=False)
                                last = mm(o, tl, hi[:, j, cols], start=False, stop=j == 1)
                        last.then_inc(s_used if half else s_bg, 1)
                    if b == 0:
                        ts = transposes(q.src + 1, q.t + 4, YA, (2, 3))
                tile_split(ts, 2)
                for half in range(2):
                    pe.wait_ge(s_gfree, g0 + 13 + half + 1)
                    c = c0 + 21 + half
                    tokens_out(c, c, 2 * half, 4, 512, AH[:, 4:8, :], AL[:, 4:8, :], True, True)
                ts = transposes(q.src + 2, q.t + 6, M2, m=q.m_o)
                pe.wait_ge(s_gfree, g0 + 15 + 2)
                gate_rows(2 * q.p, (2, 3))
                for half in range(2):
                    if half == 1:
                        pe.wait_ge(s_gtc, 2 * q.p + 1)
                    pe.wait_ge(s_gfree, g0 + 15 + half + 1)
                    for h in range(2):
                        half_group(q.c_o + 2 * half + h, q.c_o + 2 * half + h, half, h, ts=None if half else ts)
                        if half == 0 and h == 0:
                            mod_columns(q.m_o, (4, 5))
                mod_done(q.m_o)
                ts = transposes(q.src + 3, q.t + 10, YN, m=q.m_mlp, banks=(0, 2), free=g0 + 17 + 2)
                pe.wait_ge(s_gfree, g0 + 17 + 2)
                gate_rows(2 * q.p + 1, (1, 3))
                mlp(q.mlp, q.c_mlp, q.u + 3, q.m_mlp, ts)


N_CONST, N_ROWS = 12, 11
INPUTS = ["x", "ln1", "w_in", "conv_w", "conv_b", "igate_b", "fgate_b", "mlstm_norm", "moba_q_norm", "moba_k_norm",
          "swa_q_norm", "swa_k_norm", "swa_sinks", "w_out", "ln2", "w_up", "w_down", "c_2", "ctx_2", "c_ctx_2",
          "w_mod_2", "b_mod_2", "g_norm1_2", "g_norm2_2", "w_in_2", "w_conv_2", "g_q_2", "g_k_2", "w_conv_out_2",
          "w_four_out_2", "w_attn_out_2", "w_o_2", "w_ff1_2", "w_ff2_2"]


def kernel(**inputs):
    import concourse.bacc as bacc
    from concourse.bass_utils import run_bass_kernel_spmd

    nc = bacc.Bacc("TRN2", target_bir_lowering=False, num_devices=1)
    arrays, args = {}, {}
    for name in INPUTS:
        v = np.ascontiguousarray(inputs[name])
        arrays[f"in_{name}"] = v
        args[name] = nc.dram_tensor(f"in_{name}", v.shape, mybir.dt.from_np(v.dtype), kind="ExternalInput").ap()
    table = shape_constants()
    arrays["constants"] = table
    args["constants"] = nc.dram_tensor("constants", table.shape, F32, kind="ExternalInput").ap()
    pairs = np.tile(np.eye(2, dtype=np.float32), (2, 1))
    arrays["selector"] = pairs
    args["selector"] = nc.dram_tensor("selector", pairs.shape, F32, kind="ExternalInput").ap()
    out = nc.dram_tensor("out", (1, S, D), F32, kind="ExternalOutput").ap()
    build(nc, args, out)
    return run_bass_kernel_spmd(nc, [arrays], core_ids=[0]).results[0]["out"]
```
